# Optimizing a Trainium2 kernel written in Bass

```python
import jax
import jax.numpy as jnp
from jax import lax
import numpy as np

D_MODEL = 1024
BATCH = 1
SEQ = 128
DEPTH = 2
DEC_BATCH = 1
DEC_SEQ = 512
PAST_LEN = 128

GRID_W = 64
EPS = 1e-6
CONV_W = 512
CONV_K = 3
GLA_HEADS = 4
GLA_DK = 128
GLA_DV = 128
GLA_QK_W = GLA_HEADS * GLA_DK
GLA_W = GLA_HEADS * GLA_DV
GLA_RANK = 16
GLA_TAU = 16.0
GLA_CHUNK = 64
ATT_HEADS = 8
ATT_KV_HEADS = 2
ATT_GROUP = ATT_HEADS // ATT_KV_HEADS
HEAD_DIM = 64
ATT_W = ATT_HEADS * HEAD_DIM
KV_W = ATT_KV_HEADS * HEAD_DIM
WINDOW = 128
BLOCK = 128
ROPE_THETA = 10000.0
N_BRANCH = 3
BRANCH_W = 512
N_EXPERT_GROUPS = 4
EXPERTS_PER_GROUP = 4
N_EXPERTS = N_EXPERT_GROUPS * EXPERTS_PER_GROUP
TOP_K = 2
D_EXPERT = 256
SPLITS = (CONV_W, CONV_W, CONV_W, GLA_QK_W, GLA_QK_W, GLA_W, GLA_W, GLA_RANK, GLA_RANK, ATT_W, KV_W, KV_W, D_MODEL, D_MODEL, D_MODEL)
N_IN = sum(SPLITS)
NEG_INF = -1e30

kernel_name = "hybrid_diffusion_prefix_step"

def rms_norm(x, g):
    xf = x.astype(jnp.float32)
    y = xf * lax.rsqrt(jnp.mean(xf * xf, axis=-1, keepdims=True) + EPS)
    return (y * g.astype(jnp.float32)).astype(x.dtype)

def split_cols(p):
    out, start = [], 0
    for n in SPLITS:
        out.append(p[..., start:start + n])
        start += n
    return out

def modulation(cond, w_ada, b_ada):
    m = jax.nn.silu(cond) @ w_ada + b_ada
    return [t[:, None, :] for t in jnp.split(m, 6, axis=-1)]

def axial_rope(x):
    L = x.shape[1]
    rows = L // GRID_W
    row = jnp.repeat(jnp.arange(rows, dtype=jnp.float32), GRID_W)
    col = jnp.tile(jnp.arange(GRID_W, dtype=jnp.float32), rows)
    axis_dim = HEAD_DIM // 2
    n_freq = axis_dim // 2
    inv = ROPE_THETA ** (-jnp.arange(n_freq, dtype=jnp.float32) / n_freq)
    xf = x.astype(jnp.float32)
    outs = []
    for i, pos in enumerate((row, col)):
        ang = pos[:, None] * inv[None, :]
        cos = jnp.cos(ang)[None, :, None, :]
        sin = jnp.sin(ang)[None, :, None, :]
        xa = xf[..., i * axis_dim:(i + 1) * axis_dim]
        x1, x2 = xa[..., :n_freq], xa[..., n_freq:]
        outs += [x1 * cos - x2 * sin, x1 * sin + x2 * cos]
    return jnp.concatenate(outs, axis=-1).astype(x.dtype)

def short_conv_mixer(b_gate, c_gate, h, conv_w):
    u = c_gate * h
    L = u.shape[1]
    pad = CONV_K // 2
    up = jnp.pad(u, ((0, 0), (pad, pad), (0, 0)))
    y = sum(up[:, j:j + L] * conv_w[j] for j in range(CONV_K))
    return b_gate * y

def gla_chunk_scan(q, k, v, log_a, s0):
    B, L, H, DK = q.shape
    DV = v.shape[-1]
    C = GLA_CHUNK
    N = L // C
    f32 = jnp.float32

    def chunks(t):
        return t.astype(f32).reshape(B, N, C, H, t.shape[-1]).transpose(1, 0, 3, 2, 4)

    qc, kc, vc, ac = chunks(q), chunks(k), chunks(v), chunks(log_a)
    b = jnp.cumsum(ac, axis=3)
    b_last = b[:, :, :, -1:, :]
    q_in = qc * jnp.exp(b)
    k_in = kc * jnp.exp(-b)
    k_end = kc * jnp.exp(b_last - b)
    causal = jnp.tril(jnp.ones((C, C), dtype=bool))
    att = jnp.where(causal, jnp.einsum("nbhcd,nbhsd->nbhcs", q_in, k_in), 0.0)
    o_intra = jnp.einsum("nbhcs,nbhsv->nbhcv", att, vc)
    ds = jnp.einsum("nbhsd,nbhsv->nbhdv", k_end, vc)
    decay = jnp.exp(b_last[:, :, :, 0, :])

    def step(s, inp):
        dec, d = inp
        return dec[..., None] * s + d, s

    s_fin, s_prev = lax.scan(step, s0.astype(f32), (decay, ds))
    o_inter = jnp.einsum("nbhcd,nbhdv->nbhcv", q_in, s_prev)
    o = (o_intra + o_inter).transpose(1, 0, 3, 2, 4).reshape(B, L, H, DV)
    return o, s_fin

def gla_mixer(q, k, v, r, lr_f, lr_b, w_gate, b_gate, norm_g, s0_f, s0_b):
    B, L, _ = q.shape
    f32 = jnp.float32
    qh = q.reshape(B, L, GLA_HEADS, GLA_DK) * (GLA_DK ** -0.5)
    kh = k.reshape(B, L, GLA_HEADS, GLA_DK)
    vh = v.reshape(B, L, GLA_HEADS, GLA_DV)

    def log_decay(lr, d):
        z = (lr @ w_gate[d]).astype(f32) + b_gate[d].astype(f32)
        return (jax.nn.log_sigmoid(z) / GLA_TAU).reshape(B, L, GLA_HEADS, GLA_DK)

    def rev(t):
        return t[:, ::-1]

    o_f, s_f = gla_chunk_scan(qh, kh, vh, log_decay(lr_f, 0), s0_f)
    o_b, s_b = gla_chunk_scan(rev(qh), rev(kh), rev(vh), rev(log_decay(lr_b, 1)), s0_b)
    o = o_f + rev(o_b)
    o = o * lax.rsqrt(jnp.mean(o * o, axis=-1, keepdims=True) + EPS)
    y = o.reshape(B, L, GLA_W) * norm_g.astype(f32) * jax.nn.silu(r.astype(f32))
    return y.astype(q.dtype), s_f.astype(q.dtype), s_b.astype(q.dtype)

def sink_softmax(s, sink):
    B, HKV, G, R, _ = s.shape
    sk = jnp.broadcast_to(sink.astype(jnp.float32).reshape(1, HKV, G, 1, 1), (B, HKV, G, R, 1))
    return jax.nn.softmax(jnp.concatenate([s, sk], axis=-1), axis=-1)[..., :-1]

def context_attention(q, k, v, sink):
    B, P = q.shape[:2]
    n_blk = P // BLOCK
    scale = HEAD_DIM ** -0.5
    qb = q.reshape(B, n_blk, BLOCK, ATT_KV_HEADS, ATT_GROUP, HEAD_DIM).transpose(1, 0, 2, 3, 4, 5)

    def one_block(qn):
        s = jnp.einsum("brkgd,bpkd->bkgrp", qn, k).astype(jnp.float32) * scale
        p = sink_softmax(s, sink).astype(v.dtype)
        return jnp.einsum("bkgrp,bpkd->brkgd", p, v)

    o = lax.map(one_block, qb)
    return o.transpose(1, 0, 2, 3, 4, 5).reshape(B, P, ATT_W)

def latent_window_attention(q, k, v, k_ctx, v_ctx, sink):
    B, L = q.shape[:2]
    n_blk = L // BLOCK
    span = BLOCK + 2 * WINDOW
    scale = HEAD_DIM ** -0.5
    P = k_ctx.shape[1]
    pad = ((0, 0), (WINDOW, WINDOW), (0, 0), (0, 0))
    kp, vp = jnp.pad(k, pad), jnp.pad(v, pad)
    qb = q.reshape(B, n_blk, BLOCK, ATT_KV_HEADS, ATT_GROUP, HEAD_DIM).transpose(1, 0, 2, 3, 4, 5)
    offs = jnp.arange(BLOCK)[:, None] + WINDOW - jnp.arange(span)[None, :]
    band = jnp.abs(offs) <= WINDOW

    def one_block(args):
        n, qn = args
        start = n * BLOCK
        kn = lax.dynamic_slice_in_dim(kp, start, span, axis=1)
        vn = lax.dynamic_slice_in_dim(vp, start, span, axis=1)
        kpos = start - WINDOW + jnp.arange(span)
        valid = band & ((kpos >= 0) & (kpos < L))[None, :]
        s_ctx = jnp.einsum("brkgd,bpkd->bkgrp", qn, k_ctx).astype(jnp.float32) * scale
        s_loc = jnp.einsum("brkgd,bckd->bkgrc", qn, kn).astype(jnp.float32) * scale
        s_loc = jnp.where(valid, s_loc, NEG_INF)
        p = sink_softmax(jnp.concatenate([s_ctx, s_loc], axis=-1), sink).astype(v.dtype)
        return (jnp.einsum("bkgrp,bpkd->brkgd", p[..., :P], v_ctx)
                + jnp.einsum("bkgrc,bckd->brkgd", p[..., P:], vn))

    o = lax.map(one_block, (jnp.arange(n_blk), qb))
    return o.transpose(1, 0, 2, 3, 4, 5).reshape(B, L, ATT_W)

def hier_moe(h, w_rg, b_rg, w_re, b_re, w_eg, w_eu, w_ed):
    B, L, D = h.shape
    t = h.reshape(B * L, D)
    f32 = jnp.float32
    lg = (t @ w_rg).astype(f32) + b_rg.astype(f32)
    grp = jnp.argmax(lg, axis=-1)
    p_grp = jnp.take_along_axis(jax.nn.softmax(lg, axis=-1), grp[:, None], axis=-1)
    le = ((t @ w_re).astype(f32) + b_re.astype(f32)).reshape(-1, N_EXPERT_GROUPS, EXPERTS_PER_GROUP)
    le_sel = jnp.take_along_axis(le, grp[:, None, None], axis=1)[:, 0]
    top_w, top_i = lax.top_k(jax.nn.softmax(le_sel, axis=-1), TOP_K)
    top_w = top_w / jnp.sum(top_w, axis=-1, keepdims=True)
    expert_id = grp[:, None] * EXPERTS_PER_GROUP + top_i
    gate = jnp.sum(jax.nn.one_hot(expert_id, N_EXPERTS, dtype=f32) * (p_grp * top_w)[..., None], axis=1)
    hid = jax.nn.silu(jnp.einsum("td,edf->tef", t, w_eg)) * jnp.einsum("td,edf->tef", t, w_eu)
    y = jnp.einsum("tef,efd->td", hid * gate[..., None].astype(hid.dtype), w_ed)
    return y.reshape(B, L, D)

def trunk_layer(x, cond, lw, ctx):
    (w_ada, b_ada, norm1_g, norm2_g, w_in, conv_w, gla_w_gate, gla_b_gate, gla_norm_g,
     attn_sink, w_branch, w_out, w_rg, b_rg, w_re, b_re, w_eg, w_eu, w_ed) = lw
    B, L, _ = x.shape
    sh1, sc1, gt1, sh2, sc2, gt2 = modulation(cond, w_ada, b_ada)
    h = rms_norm(x, norm1_g) * (1 + sc1) + sh1
    (a_b, a_c, a_h, g_q, g_k, g_v, g_r, g_lf, g_lb,
     t_q, t_k, t_v, m_a, m_b, m_c) = split_cols(h @ w_in)
    y_a = short_conv_mixer(a_b, a_c, a_h, conv_w)
    q = t_q.reshape(B, L, ATT_HEADS, HEAD_DIM)
    k = t_k.reshape(B, L, ATT_KV_HEADS, HEAD_DIM)
    v = t_v.reshape(B, L, ATT_KV_HEADS, HEAD_DIM)
    if ctx is None:
        s0 = jnp.zeros((B, GLA_HEADS, GLA_DK, GLA_DV), jnp.float32)
        y_b, s_f, s_b = gla_mixer(g_q, g_k, g_v, g_r, g_lf, g_lb, gla_w_gate, gla_b_gate, gla_norm_g, s0, s0)
        y_c = context_attention(q, k, v, attn_sink)
        side = (jnp.stack([s_f, s_b], axis=1), k, v)
    else:
        st, k_ctx, v_ctx = ctx
        y_b, _, _ = gla_mixer(g_q, g_k, g_v, g_r, g_lf, g_lb, gla_w_gate, gla_b_gate, gla_norm_g,
                              st[:, 0], st[:, 1])
        y_c = latent_window_attention(axial_rope(q), axial_rope(k), v, k_ctx, v_ctx, attn_sink)
        side = None
    z = (jax.nn.sigmoid(m_a) * (y_a @ w_branch[0])
         + jax.nn.sigmoid(m_b) * (y_b @ w_branch[1])
         + jax.nn.sigmoid(m_c) * (y_c @ w_branch[2]))
    x = x + gt1 * (z @ w_out)
    h2 = rms_norm(x, norm2_g) * (1 + sc2) + sh2
    x = x + gt2 * hier_moe(h2, w_rg, b_rg, w_re, b_re, w_eg, w_eu, w_ed)
    return x, side

def setup_inputs(seed: int = 0) -> dict:
    key = jax.random.key(seed)
    ks = jax.random.split(key, 27)
    D = D_MODEL

    def nrm(i, shape, scale):
        return jax.random.normal(ks[i], shape, jnp.float32) * scale

    return {
        "x_prompt": nrm(0, (BATCH, SEQ, D), 1.0),
        "x_sample": nrm(1, (DEC_BATCH, DEC_SEQ, D), 1.0),
        "state_gla": nrm(2, (DEC_BATCH, DEPTH, 2, GLA_HEADS, GLA_DK, GLA_DV), 0.5),
        "cache_k": nrm(3, (DEC_BATCH, DEPTH, PAST_LEN, ATT_KV_HEADS, HEAD_DIM), 1.0),
        "cache_v": nrm(4, (DEC_BATCH, DEPTH, PAST_LEN, ATT_KV_HEADS, HEAD_DIM), 1.0),
        "c": nrm(5, (DEC_BATCH, D), 1.0),
        "c_ctx": nrm(6, (D,), 1.0),
        "w_ada": nrm(7, (DEPTH, D, 6 * D), 0.5 * D ** -0.5),
        "b_ada": nrm(8, (DEPTH, 6 * D), 0.02),
        "norm1_g": 1.0 + nrm(9, (DEPTH, D), 0.02),
        "norm2_g": 1.0 + nrm(10, (DEPTH, D), 0.02),
        "w_in": nrm(11, (DEPTH, D, N_IN), D ** -0.5),
        "conv_w": nrm(12, (DEPTH, CONV_K, CONV_W), CONV_K ** -0.5),
        "gla_w_gate": nrm(13, (DEPTH, 2, GLA_RANK, GLA_QK_W), GLA_RANK ** -0.5),
        "gla_b_gate": 1.0 + nrm(14, (DEPTH, 2, GLA_QK_W), 0.5),
        "gla_norm_g": 1.0 + nrm(15, (DEPTH, GLA_W), 0.02),
        "attn_sink": nrm(16, (DEPTH, ATT_HEADS), 0.5),
        "w_branch": nrm(17, (DEPTH, N_BRANCH, BRANCH_W, D), BRANCH_W ** -0.5),
        "w_out": nrm(18, (DEPTH, D, D), D ** -0.5),
        "w_route_group": nrm(19, (DEPTH, D, N_EXPERT_GROUPS), D ** -0.5),
        "b_route_group": nrm(20, (DEPTH, N_EXPERT_GROUPS), 0.01),
        "w_route_expert": nrm(21, (DEPTH, D, N_EXPERTS), D ** -0.5),
        "b_route_expert": nrm(22, (DEPTH, N_EXPERTS), 0.01),
        "w_exp_gate": nrm(23, (DEPTH, N_EXPERTS, D, D_EXPERT), D ** -0.5),
        "w_exp_up": nrm(24, (DEPTH, N_EXPERTS, D, D_EXPERT), D ** -0.5),
        "w_exp_down": nrm(25, (DEPTH, N_EXPERTS, D_EXPERT, D), D_EXPERT ** -0.5),
        "final_norm_g": 1.0 + nrm(26, (D,), 0.02),
    }

def reference(x_prompt, x_sample, state_gla, cache_k, cache_v, c, c_ctx, w_ada, b_ada, norm1_g, norm2_g,
              w_in, conv_w, gla_w_gate, gla_b_gate, gla_norm_g, attn_sink, w_branch, w_out,
              w_route_group, b_route_group, w_route_expert, b_route_expert,
              w_exp_gate, w_exp_up, w_exp_down, final_norm_g):
    def layer_w(l):
        return (w_ada[l], b_ada[l], norm1_g[l], norm2_g[l], w_in[l], conv_w[l], gla_w_gate[l], gla_b_gate[l],
                gla_norm_g[l], attn_sink[l], w_branch[l], w_out[l], w_route_group[l], b_route_group[l],
                w_route_expert[l], b_route_expert[l], w_exp_gate[l], w_exp_up[l], w_exp_down[l])

    xp = x_prompt
    cond_ctx = c_ctx[None, :]
    gla_states, ctx_keys, ctx_vals = [], [], []
    for l in range(DEPTH):
        xp, (s_l, k_l, v_l) = trunk_layer(xp, cond_ctx, layer_w(l), None)
        gla_states.append(s_l)
        ctx_keys.append(k_l)
        ctx_vals.append(v_l)
    y_prompt = rms_norm(xp, final_norm_g)

    xs = x_sample
    for l in range(DEPTH):
        xs, _ = trunk_layer(xs, c, layer_w(l), (state_gla[:, l], cache_k[:, l], cache_v[:, l]))
    y_sample = rms_norm(xs, final_norm_g)

    new_state_gla = jnp.stack(gla_states, axis=1)
    new_cache_k = jnp.stack(ctx_keys, axis=1)
    new_cache_v = jnp.stack(ctx_vals, axis=1)
    return (y_prompt, y_sample, new_state_gla, new_cache_k, new_cache_v)


_drawn_inputs = setup_inputs


def setup_inputs(seed=0):
    import zlib

    import numpy as np

    out = dict(_drawn_inputs(seed))
    spreads = {}
    factors = {'state_gla': 8.0,
     'cache_k': 3.459,
     'cache_v': 3.142,
     'norm2_g': 3.519,
     'gla_norm_g': 5.393,
     'attn_sink': 8.0,
     'b_route_group': 8.0,
     'b_route_expert': 8.0,
     'final_norm_g': 2.796}
    for name, (base, spread) in spreads.items():
        noise = np.random.default_rng([zlib.crc32(name.encode()), seed]).standard_normal(out[name].shape)
        drawn = base * np.exp(spread * noise) if base else spread * noise
        out[name] = jnp.asarray(drawn.astype(out[name].dtype))
    for name, factor in factors.items():
        out[name] = (out[name] * factor).astype(out[name].dtype)
    return out
```

```python
from contextlib import ExitStack

import numpy as np

import concourse.bass as bass
import concourse.mybir as mybir

F32 = mybir.dt.float32
F32R = mybir.dt.float32r
I32 = mybir.dt.int32
U32 = mybir.dt.uint32
ALU = mybir.AluOpType
ACT = mybir.ActivationFunctionType
AX = mybir.AxisListType
P = 128

DEPTH, D = 2, 1024
KC = D // P
SAMPLE, PROMPT = 512, 128
TOK = SAMPLE + PROMPT
TILES = TOK // P
PT = TILES - 1
GRID_W = 64
EPS = 1e-6
CONV_W, CONV_K = 512, 3
HEADS, DK, DV, CHUNK = 4, 128, 128, 64
NCH = TOK // CHUNK
SCH = SAMPLE // CHUNK
RANK, TAU = 16, 16.0
AH, KVH, HD = 8, 2, 64
BR_W = 512
NG, EPG = 4, 4
NE = NG * EPG
FE = 256
SLOTS = P
BIG = 1e30
SET = 1

SPLITS = (CONV_W, CONV_W, CONV_W, HEADS * DK, HEADS * DK, HEADS * DV, HEADS * DV, RANK, RANK, AH * HD, KVH * HD, KVH * HD, D, D, D)
(C_AB, C_AC, C_AH, C_GQ, C_GK, C_GV, C_GR, C_LF, C_LB, C_TQ, C_TK, C_TV, C_MA, C_MB, C_MC) = [
    sum(SPLITS[:i]) for i in range(len(SPLITS))]

ADA_BLOCKS = 6
ADA = ADA_BLOCKS * KC
U_V, U_R, U_TV, U_LR, U_GLA = 0, 4, 8, 9, 10
U_K = U_GLA + 2 * HEADS
U_Q = U_K + KVH
U_CONV = U_Q + AH // 2
U_M = U_CONV + 3 * CONV_W // P
U_OUT = U_M + 6 * KC
UNITS = U_OUT + 8
RAW, SPL = 6, 3
EXU = 12
ROUND_UNITS = NE // 2 * EXU

CONST = {}
_at = 0
for _name, _n in (("ident", P), ("rot", P), ("tri", P), ("ones", P), ("iota", P), ("strip", 4 * P), ("fwd", CHUNK),
                  ("bwd", CHUNK), ("prio", NG), ("base", NE), ("tokid", TILES), ("cst", 2), ("thr", 4)):
    CONST[_name] = (_at, _n)
    _at += _n
CONST_RES = _at
for _name, _n in (("cos", SAMPLE), ("sin", SAMPLE), ("scan", TOK)):
    CONST[_name] = (_at, _n)
    _at += _n
CONST_COLS = _at


def shape_constants():
    t = np.zeros((P, CONST_COLS), np.float32)

    def put(name, v):
        a, n = CONST[name]
        t[:, a:a + n] = v

    r = np.arange(P)
    put("ident", np.eye(P))
    rot = np.zeros((P, P))
    half = HD // 4
    for m in range(P):
        rot[(m + half) if m % (2 * half) < half else (m - half), m] = -1.0 if m % (2 * half) < half else 1.0
    put("rot", rot)
    put("tri", (r[:, None] < r[None, :]).astype(np.float32))
    put("ones", 1.0)
    put("iota", r[None, :])
    strip = np.zeros((P, 4 * P))
    strip[:, 0:P] = np.where(r[None, :] >= r[:, None], 0.0, -BIG)
    strip[:, 3 * P:] = np.where(r[None, :] <= r[:, None], 0.0, -BIG)
    put("strip", strip)
    s, c = (r % CHUNK)[:, None], np.arange(CHUNK)[None, :]
    put("fwd", s <= c)
    put("bwd", s >= c)
    put("prio", np.arange(NG, 0, -1)[None, :])
    put("base", (np.arange(NE) * SLOTS)[None, :])
    put("tokid", r[:, None] + P * np.arange(TILES)[None, :])
    put("cst", np.array([[EPS, 1.0]]))
    put("thr", (P * np.arange(1, 5))[None, :])
    inv = (10000.0 ** (-np.arange(half, dtype=np.float32) / half)).astype(np.float32)
    pos = np.arange(SAMPLE)
    d = r % HD
    where = np.where((d // (2 * half))[:, None] == 0, (pos // GRID_W)[None, :], (pos % GRID_W)[None, :]).astype(np.float32)
    ang = (where * inv[d % half][:, None]).astype(np.float32)
    put("cos", np.cos(ang.astype(np.float64)))
    put("sin", np.sin(ang.astype(np.float64)))
    put("scan", (np.arange(TOK) % CHUNK != 0)[None, :])
    return t


def ds(a, n):
    return bass.ds(a, n)


def build(nc, a, out_yp, out_ys, out_st, out_ck, out_cv):
    with ExitStack() as ctx:
        ctx.enter_context(nc.allow_non_contiguous_dma(reason="small vectors, one element per partition"))

        sems = []

        def sem(name):
            sems.append(ctx.enter_context(nc.semaphore(name)))
            return sems[-1]

        def gather_sem(name):
            return ctx.enter_context(nc.semaphore(name))

        s_start = ctx.enter_context(nc.semaphore("semaphores_set"))

        base = [(nc.sbuf_base + 63) // 64 * 64]

        def at(name, shape, dt, offset):
            return nc.alloc_sbuf_tensor_at(name, shape, dt, offset=offset)

        def room(nbytes):
            o = base[0]
            base[0] += (nbytes + 31) // 32 * 32
            return o

        def own(name, shape, dt=F32):
            return at(name, shape, dt, room(4 * int(np.prod(shape[1:]))))

        ROW = 4 * TOK
        o_ht = room(2 * KC * ROW)
        o_yhi = room(12 * ROW)
        o_ylo = room(12 * ROW)
        o_w = room(2 * KC * ROW)
        o_m = room(5 * ROW)
        raw = own("raw", [P, RAW, 1024])
        w_hi = own("w_hi", [P, SPL, 1024], F32R)
        w_lo = own("w_lo", [P, SPL, 1024], F32R)
        con = own("con", [P, CONST_RES])
        condT = own("condT", [P, KC, 2])
        conv_w = own("conv_w", [P, CONV_W // P, CONV_K])
        b_gate = own("b_gate", [P, 2, HEADS])
        sink = own("sink", [P, AH])
        w_rt = own("w_rt", [P, KC, NG + NE])
        b_rt = own("b_rt", [P, NG + NE])
        small = own("small", [P, 64])
        info = own("info", [P, 2 * DEPTH + 2], I32)
        assert base[0] <= nc.sbuf_usable_end, (base[0], nc.sbuf_usable_end)

        def C(name):
            c, n = CONST[name]
            return con[:, c:c + n]

        ident, rot, tri, ones, iota, strip = (C(n) for n in ("ident", "rot", "tri", "ones", "iota", "strip"))
        eps = C("cst")[:, 0:1]
        one = C("cst")[:, 1:2]
        hT_hi = at("hT_hi", [P, KC, TOK], F32R, o_ht)
        hT_lo = at("hT_lo", [P, KC, TOK], F32R, o_ht + KC * ROW)
        yT_hi = at("yT_hi", [P, 12, TOK], F32R, o_yhi)
        yT_lo = at("yT_lo", [P, 12, TOK], F32R, o_ylo)
        zT_hi = at("zT_hi", [P, KC, TOK], F32R, o_w)
        zT_lo = at("zT_lo", [P, KC, TOK], F32R, o_w + KC * ROW)
        x = at("x", [P, TILES, D], F32, o_yhi)
        gt = at("gt", [P, 2, D], F32, o_yhi + 8 * ROW)
        modA = at("modA", [P, 2, D], F32, o_ylo)
        modB = at("modB", [P, 2, D], F32, o_ylo + 8192)
        hbuf = at("hbuf", [P, 2, D], F32, o_ylo + 16384)
        junk = at("junk", [P, D], F32, o_ylo + 24576)
        ada_b = at("ada_b", [2, ADA_BLOCKS, D], F32, o_w)
        ada_g = at("ada_g", [2, 2, D], F32, o_w + 24576)
        mrow = at("mrow", [2, 2, D], F32, o_w + 32768)
        v_sb = at("v_sb", [P, TILES, HEADS * DV], F32, o_w)
        rg = at("rg", [P, TILES, HEADS * DV], F32, o_w + 4 * ROW)
        tv = at("tv", [P, TILES, P], F32, o_w + 8 * ROW)
        lrT = at("lrT", [2 * RANK, TOK], F32, o_w + 9 * ROW)
        qs = at("qs", [P, TOK], F32, o_w + 10 * ROW)
        ks = at("ks", [P, TOK], F32, o_w + 11 * ROW)
        zb = at("zb", [P, 2, TOK], F32, o_w + 12 * ROW)
        sp_ = at("sp_", [P, 2, TOK], F32, o_w + 14 * ROW)
        cb = at("cb", [P, 2, TOK], F32, o_yhi)
        E_ = at("E_", [P, 2, TOK], F32, o_yhi + 2 * ROW)
        En = at("En", [P, 2, TOK], F32, o_yhi + 8 * ROW)
        attm = at("attm", [P, 2, TILES, P], F32, o_yhi + 10 * ROW)
        NST = 12
        st = [at("st0", [P, NST, DV], F32, o_ylo), at("st1", [P, NST, DV], F32, o_ylo + 8 * ROW)]
        scanm = at("scanm", [P, TOK], F32, o_ylo + NST * DV * 4)
        yb = at("yb", [P, TILES, DV], F32, o_ylo + 8 * ROW + NST * DV * 4)
        osq = at("osq", [P, TILES, DV], F32, o_w + 10 * ROW)
        w_gate = at("w_gate", [2 * RANK, 2, HEADS * DK], F32, o_m)
        g_norm = at("g_norm", [P, HEADS * DV], F32, o_m + 4096)
        cossin = at("cossin", [P, 2, SAMPLE], F32, o_m + 6144)
        cv = at("cv", [P, KVH * HD], F32, o_m + 10240)
        ckd = at("ckd", [P, KVH, 2, HD], F32, o_m + 10752)
        s_sb = at("s_sb", [P, 2, TILES, 4 * P], F32, o_w + 20480 + 2560 - 23040)
        tv_end = o_w + 9 * ROW
        KCOLS = P + TOK
        kT = at("kT", [P, KVH, KCOLS], F32, tv_end)
        pT = at("pT", [P, 2, 4 * P], F32, tv_end + KVH * KCOLS * 4)
        qT = at("qT", [P, 2, TOK], F32, tv_end + KVH * KCOLS * 4 + 4096)
        qraw = at("qraw", [P, TOK], F32, tv_end + KVH * KCOLS * 4 + 4096 + 2 * ROW)
        assert tv_end + KVH * KCOLS * 4 + 4096 + 3 * ROW <= o_w + 16 * ROW
        rt1 = at("rt1", [P, SAMPLE], F32, o_yhi)
        rt2 = at("rt2", [P, SAMPLE], F32, o_yhi + 2048)
        kout = at("kout", [P, KVH, HD], F32, o_yhi + 4096)
        csb = at("csb", [P, TOK], F32, o_w)
        upad = at("upad", [P, TOK + 4], F32, o_w + ROW)
        yf = at("yf", [P, TOK], F32, o_w + 3 * ROW)
        sg = at("sg", [P, 3, TOK], F32, o_m)
        zacc = at("zacc", [P, TOK], F32, o_m + 3 * ROW)
        zt = at("zt", [P, TOK], F32, o_m + 4 * ROW)
        h2T = at("h2T", [P, 2, KC, P], F32, o_ht)
        xg = at("xg", [P, 2, D], F32, o_ht + 8192)
        yg = at("yg", [P, 2, 2, D], F32, o_ht + 16384)
        onehot = at("onehot", [P, 2, TILES, SLOTS], F32, o_ht + 32768)
        xT_hi = at("xT_hi", [P, 2, KC, SLOTS], F32R, o_w)
        xT_lo = at("xT_lo", [P, 2, KC, SLOTS], F32R, o_w + 8192)
        hidT_hi = at("hidT_hi", [P, 2, 2, SLOTS], F32R, o_w + 16384)
        hidT_lo = at("hidT_lo", [P, 2, 2, SLOTS], F32R, o_w + 18432)
        hid = at("hid", [P, 2, FE], F32, o_w + 20480)
        hg = at("hg", [P, 2, FE], F32, o_w + 22528)
        yo = at("yo", [P, 2, D], F32, o_w + 24576)
        _rt = [o_m]

        def rt(name, shape, dt=F32):
            o = _rt[0]
            _rt[0] += (4 * int(np.prod(shape[1:])) + 31) // 32 * 32
            assert _rt[0] <= o_m + 5 * ROW
            return at(name, shape, dt, o)

        lgt = rt("lgt", [P, TILES, NG + NE])
        gmax = rt("gmax", [P, TILES, 1])
        geq = rt("geq", [P, TILES, NG])
        gpk = rt("gpk", [P, TILES, NG])
        goh = rt("goh", [P, TILES, NG])
        gex = rt("gex", [P, TILES, NG])
        gsum = rt("gsum", [P, TILES, 1])
        pgrp = rt("pgrp", [P, TILES, 1])
        lsel4 = rt("lsel4", [P, TILES, EPG, NG])
        lsel = rt("lsel", [P, TILES, EPG])
        lsel2 = rt("lsel2", [P, TILES, EPG])
        m1 = rt("m1", [P, TILES, 1])
        m2 = rt("m2", [P, TILES, 1])
        oh1 = rt("oh1", [P, TILES, EPG])
        oh2 = rt("oh2", [P, TILES, EPG])
        e21 = rt("e21", [P, TILES, 1])
        wt1 = rt("wt1", [P, TILES, 1])
        wt2 = rt("wt2", [P, TILES, 1])
        E1 = rt("E1", [P, TILES, NE])
        E2 = rt("E2", [P, TILES, NE])
        Em = rt("Em", [P, TILES, NE])
        rkm = rt("rkm", [P, TILES, NE])
        rpos = rt("rpos", [P, TILES, NE])
        rtmp = rt("rtmp", [P, TILES, NE])
        posf = rt("posf", [P, 2, TILES])
        rsel = rt("rsel", [P, 2, TILES])
        bsel = rt("bsel", [P, 2, TILES])
        wsel = rt("wsel", [P, 2, TILES])
        inr = rt("inr", [P, 2, TILES])
        in2 = rt("in2", [P, 2, TILES])
        pos = rt("pos", [P, 2, TILES], I32)
        cnt = rt("cnt", [P, NE])
        cmax = rt("cmax", [P, 1])
        cge = rt("cge", [P, 4])
        cr = rt("cr", [P, 1])
        crf = rt("crf", [P, 2])
        sidx = rt("sidx", [P, NE], I32)

        ss, sd, rstd = small[:, 0:5], small[:, 5:10], small[:, 10:15]
        g_ss, g_ln, g_rs = small[:, 15:20], small[:, 20:25], small[:, 25:30]
        a_mx, a_nm, a_rs, a_es, a_rd = (small[:, 30 + 5 * i:35 + 5 * i] for i in range(5))

        ps = ctx.enter_context(nc.psum_tensor("ps", [P, 8, 512], F32))
        psf = ps[:, :, :].rearrange("p b c -> p (b c)")

        def pair(i, n=TOK, m=P):
            return psf[0:m, 1024 * i:1024 * i + n]

        mod_d = nc.dram_tensor("mod_scratch", (ADA_BLOCKS, 2, D), F32, kind="Internal").ap()
        x_d = nc.dram_tensor("x_scratch", (TOK, D), F32, kind="Internal").ap()
        h2_d = nc.dram_tensor("h2_scratch", (TOK, D), F32, kind="Internal").ap()
        ye_d = nc.dram_tensor("expert_scratch", (NE * SLOTS, D), F32, kind="Internal").ap()

        s_held = {e.engine: sem(f"held_{i}") for i, e in enumerate((nc.sync, nc.gpsimd, nc.scalar, nc.vector, nc.tensor))}
        s_const, s_init, s_cond = sem("consts_loaded"), sem("init_done"), sem("cond_ready")
        s_raw = [sem(f"raw_loaded{i}") for i in range(RAW)]
        s_rawx = [sem(f"raw_expert_loaded{i}") for i in range(RAW)]
        s_lay, s_lay2, s_lay3 = sem("layer_rows_loaded"), sem("layer_consts_loaded"), sem("gla_consts_loaded")
        s_ada, s_mrow = sem("ada_unit_used"), sem("mod_row_ready")
        s_mst = [sem(f"mod_row_stored{i}") for i in range(2)]
        s_modl, s_xsav, s_xload, s_gtl = sem("mod_loaded"), sem("x_saved"), sem("x_loaded"), sem("gate_loaded")
        s_split, s_used = sem("unit_split"), sem("unit_used")
        s_sd, s_h, s_hps, s_hhi, s_hT = sem("norm_root"), sem("h_ready"), sem("h_transposed"), sem("hT_hi_ready"), sem("hT_ready")
        s_v, s_r, s_tv, s_lr = sem("v_ready"), sem("r_silu_ready"), sem("tv_ready"), sem("lr_ready")
        s_gqk, s_gz, s_gzb, s_gsp, s_gcb, s_gE, s_gin = (sem(n) for n in (
            "gla_q_k_copied", "gla_gate_logits", "gla_gate_biased", "gla_softplus", "gla_decay_sums", "gla_exps", "gla_qk_decayed"))
        s_gkT, s_gke, s_gatt, s_gam, s_gds, s_gst, s_go, s_gsq, s_gss, s_grs, s_gy, s_gyT = (sem(n) for n in (
            "gla_kend_transposed", "gla_kend_copied", "gla_scores", "gla_scores_masked", "gla_state_steps", "gla_states",
            "gla_out", "gla_squares", "gla_square_sums", "gla_rstd", "gla_y", "gla_y_transposed"))
        s_st0 = [sem(f"state_loaded{i}") for i in range(2)]
        s_y = sem("y_ready")
        s_kraw, s_rot, s_rope, s_kt, s_kc, s_qc = (sem(n) for n in (
            "attn_raw_copied", "attn_rotated", "attn_roped", "attn_keys_turned", "attn_keys_copied", "attn_prompt_copied"))
        s_sc, s_sce, s_nm, s_ex, s_p, s_pt, s_pte, s_ao = (sem(n) for n in (
            "attn_scores", "attn_scores_taken", "attn_max", "attn_exp", "attn_probs", "attn_probs_turned", "attn_pT_copied", "attn_out"))
        s_cc, s_cu, s_cy = sem("conv_c_copied"), sem("conv_u_ready"), sem("conv_y_taken")
        s_sig, s_zm, s_z = sem("merge_gate_ready"), sem("merge_branch_taken"), sem("z_ready")
        s_h2s = [sem(f"h2_stored{i}") for i in range(2)]
        s_x1, s_h2T, s_rl, s_rlog = sem("x_mixed"), sem("h2T_copied"), sem("router_logits"), sem("router_taken")
        s_gx, s_gxe, s_rM, s_rk, s_info = sem("router_shifted"), sem("router_exps"), sem("routes_ready"), sem("ranks_ready"), sem("rounds_known")
        r_oh, r_idx, r_slots = sem("onehot_ready"), sem("slot_step_done"), sem("slots_ready")
        r_xg = [gather_sem(f"slot_rows_loaded{i}") for i in range(2)]
        r_hi, r_lo, r_used = sem("expert_unit_hi"), sem("expert_unit_lo"), sem("expert_unit_used")
        r_T, r_Thi, r_Tlo = sem("rows_transposed"), sem("xT_hi_ready"), sem("xT_ready")
        r_hg, r_hid, r_HT, r_hT = sem("expert_silu"), sem("expert_hidden"), sem("hidden_transposed"), sem("hidT_ready")
        r_yo = sem("expert_rows_copied")
        r_ys = [sem(f"expert_rows_stored{i}") for i in range(2)]
        s_yg = [gather_sem(f"token_rows_loaded{i}") for i in range(2)]
        r_added, s_done = sem("round_added"), sem("layer_done")
        s_fsd, s_fy = sem("final_root"), sem("final_ready")
        s_fg, s_out, s_sto = sem("final_gain_loaded"), sem("outputs_stored"), sem("states_stored")

        block = ctx.enter_context(nc.Block())

        w_in_u = a["w_in"].rearrange("l (k p) n -> p (l k) n", p=P)
        w_br_u = a["w_branch"].rearrange("l b (k p) n -> p (l b k) n", p=P)
        w_out_u = a["w_out"].rearrange("l (k p) n -> p (l k) n", p=P)
        w_ada_u = a["w_ada"].rearrange("l d n -> (l d) n")
        w_eg_u = a["w_exp_gate"].rearrange("l e (k p) f -> p (l e k) f", p=P)
        w_eu_u = a["w_exp_up"].rearrange("l e (k p) f -> p (l e k) f", p=P)
        w_ed_u = a["w_exp_down"].rearrange("l e (k p) n -> (l e k p) n", p=P)

        def u_cols(u):
            if u == U_LR:
                return KC * 2 * RANK
            if U_M <= u < U_OUT and (u - U_M) % 2 == 1:
                return 4 * P
            return 1024

        def set_semaphores(eng, i):
            for s in sems[i::5]:
                eng.sem_inc(s, SET)
            eng.drain()
            eng.sem_inc(s_start, 1)
            eng.wait_ge(s_start, 5)
            hold(eng)

        def hold(eng):
            eng.sem_inc(s_held[eng.engine])

        def rounds_before(eng, l):
            hold(eng)
            return eng.value_load(info[0:1, ds(l * 2, 1)], min_val=0, max_val=5 * DEPTH)

        def rounds_now(eng, l):
            return eng.value_load(info[0:1, ds(l * 2 + 1, 1)], min_val=1, max_val=5)

        def span(b):
            if b == PT:
                return P, 2 * P
            return (P if b == 0 else 0), (3 * P if b == PT - 1 else 4 * P)

        def tiles_of(t):
            return (TILES + 1) // 2 if t % 2 == 0 else TILES // 2

        def ktiles(b):
            lo_, hi_ = span(b)
            return (hi_ - lo_) // P

        @block.sync
        def _(sp):
            set_semaphores(sp, 0)
            sp.dma_start(con[:, :], a["table"][:, 0:CONST_RES]).then_inc(s_const, 16)
            xs = a["x_sample"].rearrange("b (t p) d -> p (b t) d", p=P)
            sp.dma_start(x[:, 0:PT, :], xs).then_inc(s_const, 16)
            sp.dma_start(x[:, PT, :], a["x_prompt"][0]).then_inc(s_const, 16)
            for g, c in ((0, a["c"][0, :]), (1, a["c_ctx"])):
                for k in range(KC):
                    sp.dma_start(condT[:, k, g:g + 1], c[k * P:(k + 1) * P].rearrange("(p o) -> p o", o=1)).then_inc(s_const, 16)
            sp.wait_ge(s_init, SET + 1)

            def feature_unit(l, u, col, width=P):
                slot = u % RAW
                dst = raw[:, slot, 0:KC * width].rearrange("p (k n) -> p k n", k=KC)
                return sp.dma_start(dst, w_in_u[:, ds(l * KC, KC), col:col + width])

            def token_unit(l, u, j, src, col):
                dst = raw[:, u % RAW, :].rearrange("p (k n) -> p k n", k=2)
                return sp.dma_start(dst, src[:, ds(l * KC + 2 * j, 2), col:col + 512])

            def free_slot(l, u):
                if u < RAW:
                    sp.wait_ge(s_ada, SET + l * ADA + ADA - RAW + u + 1)
                else:
                    sp.wait_ge(s_split, SET + l * UNITS + u - RAW + 1)

            with sp.Fori(0, DEPTH) as l:
                done = rounds_before(sp, l)
                sp.wait_ge(s_done, SET + l)
                for g in range(2):
                    sp.dma_start(ada_b[g:g + 1, :, :], a["b_ada"][ds(l, 1), :].rearrange("l (b d) -> l b d", d=D)).then_inc(s_lay, 16)
                    for i, n in enumerate(("norm1_g", "norm2_g")):
                        sp.dma_start(ada_g[g:g + 1, i, :], a[n][ds(l, 1), :]).then_inc(s_lay, 16)
                for u in range(ADA):
                    b, k = u // KC, u % KC
                    if u < RAW:
                        sp.wait_ge(r_lo, SET + done * ROUND_UNITS)
                    else:
                        sp.wait_ge(s_ada, SET + l * ADA + u - RAW + 1)
                    sp.dma_start(raw[:, u % RAW, :], w_ada_u[ds(l * D + k * P, P), b * D:(b + 1) * D]).then_inc(s_raw[u % RAW], 16)
                    if u == 5:
                        sp.dma_start(g_norm[:, :], a["gla_norm_g"][ds(l, 1), :].broadcast_to([P, HEADS * DV])).then_inc(s_lay2, 16)
                        sp.dma_start(cossin[:, :, :], a["table"][:, CONST["cos"][0]:CONST["cos"][0] + 2 * SAMPLE]).then_inc(s_lay2, 16)
                        sp.dma_start(cv[:, :], a["cache_v"].rearrange("b l p k d -> p (b l) (k d)")[:, ds(l, 1), :]).then_inc(s_lay2, 16)
                        for kv in range(KVH):
                            for r in range(2):
                                sp.dma_start(ckd[:, kv, r, :], a["cache_k"].rearrange("b l p k d -> p (b l) (k d)")[
                                    :, ds(l, 1), kv * HD:(kv + 1) * HD]).then_inc(s_lay2, 16)
                        for d in range(2):
                            for o in range(2):
                                if o == d:
                                    sp.dma_start(w_gate[RANK * o:RANK * (o + 1), d, :], a["gla_w_gate"].rearrange(
                                        "l d r n -> (l d r) n")[ds(l * 2 * RANK + d * RANK, RANK), :]).then_inc(s_lay2, 16)
                                else:
                                    sp.dma_start(w_gate[RANK * o:RANK * (o + 1), d, :], a["zeros"][0:RANK, :]).then_inc(s_lay2, 16)
                            sp.dma_start(b_gate[:, d, :], a["gla_b_gate"].rearrange("l d (c p) -> p (l d) c", p=P)[
                                :, ds(l * 2 + d, 1), :]).then_inc(s_lay2, 16)
                        for j in range(CONV_K):
                            sp.dma_start(conv_w[:, :, j], a["conv_w"].rearrange("l j (c p) -> p (l j) c", p=P)[
                                :, ds(l * CONV_K + j, 1), :]).then_inc(s_lay2, 16)
                        sp.dma_start(sink[:, :], a["attn_sink"][ds(l, 1), :].broadcast_to([P, AH])).then_inc(s_lay2, 16)
                        sp.dma_start(w_rt[:, :, 0:NG], a["w_route_group"].rearrange("l (k p) n -> p (l k) n", p=P)[
                            :, ds(l * KC, KC), :]).then_inc(s_lay2, 16)
                        sp.dma_start(w_rt[:, :, NG:], a["w_route_expert"].rearrange("l (k p) n -> p (l k) n", p=P)[
                            :, ds(l * KC, KC), :]).then_inc(s_lay2, 16)
                        sp.dma_start(b_rt[:, 0:NG], a["b_route_group"][ds(l, 1), :].broadcast_to([P, NG])).then_inc(s_lay2, 16)
                        sp.dma_start(b_rt[:, NG:], a["b_route_expert"][ds(l, 1), :].broadcast_to([P, NE])).then_inc(s_lay2, 16)
                for u in range(U_M):
                    free_slot(l, u)
                    if u == U_CONV + 2:
                        hold(sp)
                    if u < U_TV:
                        ins = token_unit(l, u, u % 4, w_in_u, C_GV if u < U_R else C_GR)
                    elif u == U_TV:
                        ins = feature_unit(l, u, C_TV)
                    elif u == U_LR:
                        ins = feature_unit(l, u, C_LF, 2 * RANK)
                    elif u < U_K:
                        h, i = divmod(u - U_GLA, 2)
                        ins = feature_unit(l, u, (C_GQ, C_GK)[i] + h * P)
                    elif u < U_Q:
                        kv = u - U_K
                        dst = raw[:, u % RAW, :].rearrange("p (k r n) -> p k r n", k=KC, r=2)
                        for r in range(2):
                            ins = sp.dma_start(dst[:, :, r, :], w_in_u[:, ds(l * KC, KC), C_TK + kv * HD:C_TK + (kv + 1) * HD])
                            if r == 0:
                                ins.then_inc(s_raw[u % RAW], 16)
                    elif u < U_CONV:
                        ins = feature_unit(l, u, C_TQ + (u - U_Q) * P)
                    else:
                        f, i = divmod(u - U_CONV, 3)
                        ins = feature_unit(l, u, (C_AC, C_AH, C_AB)[i] + f * P)
                    ins.then_inc(s_raw[u % RAW], 16)
                hold(sp)
                with sp.Fori(0, KC) as n:
                    for i in range(3):
                        for j in range(2):
                            slot = 2 * i + j
                            sp.wait_ge(s_split, SET + l * UNITS + U_M - RAW + n * 6 + slot + 1)
                            if j == 0:
                                dst = raw[:, slot, :].rearrange("p (k n) -> p k n", k=KC)
                                sp.dma_start(dst, w_in_u[:, ds(l * KC, KC), ds(n * P + (C_MA, C_MB, C_MC)[i], P)]).then_inc(s_raw[slot], 16)
                            else:
                                dst = raw[:, slot, 0:512].rearrange("p (k n) -> p k n", k=4)
                                sp.dma_start(dst, w_br_u[:, ds(l * 12 + 4 * i, 4), ds(n * P, P)]).then_inc(s_raw[slot], 16)
                for u in range(U_OUT, UNITS):
                    free_slot(l, u)
                    token_unit(l, u, (u - U_OUT) % 4, w_out_u, 512 * ((u - U_OUT) // 4)).then_inc(s_raw[u % RAW], 16)
                sp.wait_ge(s_info, SET + l + 1)
                done = rounds_before(sp, l)
                now = rounds_now(sp, l)
                sp.wait_ge(s_split, SET + (l + 1) * UNITS)
                hold(sp)
                with sp.Fori(0, now) as r:
                    hold(sp)
                    with sp.Fori(0, NE // 2) as ep:
                        for j in range(EXU):
                            slot = j % RAW
                            g = (done + r) * ROUND_UNITS + ep * EXU
                            if j < RAW:
                                sp.wait_ge(r_lo, SET + g)
                            else:
                                sp.wait_ge(r_lo, SET + g + j - RAW + 1)
                            if j < 8:
                                e = (l * NE + ep * 2 + j // 4) * KC + 2 * (j % 4)
                                dst = raw[:, slot, :].rearrange("p (k i f) -> p k i f", k=2, i=2)
                                sp.dma_start(dst[:, :, 0, :], w_eg_u[:, ds(e, 2), :]).then_inc(s_rawx[slot], 16)
                                sp.dma_start(dst[:, :, 1, :], w_eu_u[:, ds(e, 2), :]).then_inc(s_rawx[slot], 16)
                            else:
                                e = (l * NE + ep * 2 + (j - 8) // 2) * 2 + (j - 8) % 2
                                sp.dma_start(raw[:, slot, 0:512], w_ed_u[ds(e * P, P), 0:512]).then_inc(s_rawx[slot], 16)
                                sp.dma_start(raw[:, slot, 512:], w_ed_u[ds(e * P, P), 512:D]).then_inc(s_rawx[slot], 16)
            sp.wait_ge(s_done, SET + DEPTH)
            sp.dma_start(gt[:, 0, :], a["final_norm_g"].rearrange("(o d) -> o d", o=1).broadcast_to([P, D])).then_inc(s_fg, 16)
            for t in range(TILES):
                sp.wait_ge(s_fy, SET + t + 1)
                dst = out_ys[0, t * P:(t + 1) * P, :] if t < PT else out_yp[0]
                sp.dma_start(dst, x[:, t, :]).then_inc(s_out, 16)
            sp.wait_ge(s_out, SET + 16 * (TILES + 2 * DEPTH))
            sp.wait_ge(s_sto, SET + 16 * 2 * HEADS * DEPTH)

        def raw_value(l, u):
            slot = u % RAW
            fills = ADA // RAW
            per_layer = fills + sum(1 + (U_K <= v < U_Q) for v in range(UNITS) if v % RAW == slot)
            here = fills + sum(1 + (U_K <= v < U_Q) for v in range(u + 1) if v % RAW == slot)
            return l * (16 * per_layer) + 16 * here

        @block.gpsimd
        def _(pool):
            set_semaphores(pool, 1)
            nc.gpsimd.memset(info[:, :], 0).then_inc(s_init, 1)

            def split(l, u, value=None, cols=None):
                slot, ring = u % RAW, u % SPL
                n = u_cols(u) if cols is None else cols
                pool.wait_ge(s_raw[slot], SET + (raw_value(l, u) if value is None else value[0]))
                if value is None:
                    if u >= SPL:
                        pool.wait_ge(s_used, SET + l * UNITS + u - SPL + 1)
                else:
                    pool.wait_ge(s_used, SET + value[1])
                hold(pool)
                nc.gpsimd.tensor_copy(w_hi[:, ring, 0:n], raw[:, slot, 0:n])
                pool.drain()
                nc.gpsimd.tensor_tensor(w_lo[:, ring, 0:n], raw[:, slot, 0:n], w_hi[:, ring, 0:n].bitcast(F32),
                                        ALU.subtract).then_inc(s_split, 1)

            with pool.Fori(0, DEPTH) as l:
                done = None
                pool.wait_ge(s_done, SET + l)
                for u in range(U_M):
                    split(l, u)
                hold(pool)
                with pool.Fori(0, KC) as n:
                    for j in range(6):
                        split(l, U_M + j, (raw_value(l, U_M + j) + n * 16, l * UNITS + U_M + n * 6 + j - SPL + 1),
                              u_cols(U_M + j))
                for u in range(U_OUT, UNITS):
                    split(l, u)
                pool.wait_ge(s_info, SET + l + 1)
                done = rounds_before(pool, l)
                now = rounds_now(pool, l)
                for i in range(2):
                    pool.wait_ge(s_h2s[i], SET + 16 * tiles_of(i) * (l + 1))
                hold(pool)
                with pool.Fori(0, now) as r:
                    g = done + r
                    pool.wait_ge(r_slots, SET + 2 * g + 2)
                    for e in range(NE):
                        if e >= 2:
                            pool.wait_ge(r_T, SET + g * NE + e - 1)
                        else:
                            pool.wait_ge(r_T, SET + g * NE)
                        hold(pool)
                        nc.gpsimd.indirect_dma_start(
                            out=xg[:, e % 2, :], out_offset=None, in_=h2_d,
                            in_offset=bass.IndirectOffsetOnAxis(ap=sidx[:, e:e + 1].bitcast(U32), axis=0)).then_inc(r_xg[e % 2], 16)
                    for i in range(2):
                        pool.wait_ge(r_ys[i], SET + (g + 1) * (16 * NE // 2))
                    for t in range(TILES):
                        if t >= 2:
                            pool.wait_ge(r_added, SET + g * TILES + t - 1)
                        for k in range(2):
                            hold(pool)
                            nc.gpsimd.indirect_dma_start(
                                out=yg[:, t % 2, k, :], out_offset=None, in_=ye_d,
                                in_offset=bass.IndirectOffsetOnAxis(ap=pos[:, k, t:t + 1].bitcast(U32), axis=0)).then_inc(s_yg[t % 2], 16)

        @block.scalar
        def _(act):
            set_semaphores(act, 2)
            A = nc.scalar.activation
            act.wait_ge(s_const, SET + 16 * (3 + 2 * KC))
            A(condT[:, :, :], condT[:, :, :], ACT.Silu).then_inc(s_cond, 1)

            def roots(l, which):
                for t in range(TILES):
                    act.drain()
                    if which == 1:
                        act.wait_ge(s_x1, SET + l * 2 * TILES + TILES + t + 1)
                    A(junk[:, :], x[:, t, :], ACT.Square, accum_out=ss[:, t:t + 1])
                act.drain()
                A(sd, ss, ACT.Sqrt, bias=eps, scale=1.0 / D).then_inc(s_sd, 1)

            with act.Fori(0, DEPTH) as l:
                act.wait_ge(s_done, SET + l)
                act.dma_start(x_d.rearrange("(t p) d -> p t d", p=P), x[:, :, :]).then_inc(s_xsav, 16)
                roots(l, 0)
                for b in range(ADA_BLOCKS):
                    act.wait_ge(s_mrow, SET + l * ADA_BLOCKS + b + 1)
                    act.dma_start(mod_d[b], mrow[:, b % 2, :]).then_inc(s_mst[b % 2], 16)
                    if b == 1:
                        act.wait_ge(s_mst[0], SET + 16 * (l * 3 + 1))
                        act.wait_ge(s_mst[1], SET + 16 * (l * 3 + 1))
                        for g in range(2):
                            act.dma_start(modB[:, g, :], mod_d[0, g:g + 1, :].broadcast_to([P, D])).then_inc(s_modl, 16)
                            act.dma_start(modA[:, g, :], mod_d[1, g:g + 1, :].broadcast_to([P, D])).then_inc(s_modl, 16)
                for i in range(2):
                    act.wait_ge(s_mst[i], SET + 16 * 3 * (l + 1))
                for t in range(TILES):
                    act.wait_ge(s_hps, SET + l * 2 * TILES + t + 1)
                    nc.scalar.copy(hT_hi[:, :, t * P:(t + 1) * P], pair(2 + t % 2, 1024).rearrange("p (k n) -> p k n", k=KC)).then_inc(s_hhi, 1)
                act.wait_ge(s_used, SET + l * UNITS + U_V + 4)
                for t in range(TILES):
                    nc.scalar.copy(v_sb[:, t, :], ps[:, t, :]).then_inc(s_v, 1)
                act.wait_ge(s_used, SET + l * UNITS + U_R + 4)
                for t in range(TILES):
                    A(rg[:, t, :], ps[:, (5 + t) % 8, :], ACT.Silu).then_inc(s_r, 1)
                act.wait_ge(s_used, SET + l * UNITS + U_TV + 1)
                nc.scalar.copy(tv[:, :, :], pair(1).rearrange("p (t n) -> p t n", n=P)).then_inc(s_tv, 1)
                act.wait_ge(s_used, SET + l * UNITS + U_LR + 1)
                nc.scalar.copy(lrT[:, :], pair(2, TOK, 2 * RANK)).then_inc(s_lr, 1)
                act.wait_ge(s_tv, SET + l + 1)
                act.dma_start(out_cv[0, ds(l, 1)].rearrange("l p k d -> p (l k d)"), tv[:, PT, :]).then_inc(s_out, 16)
                act.wait_ge(s_hT, SET + (l + 1) * TILES)
                act.wait_ge(s_xsav, SET + 16 * (l + 1))
                act.dma_start(scanm[:, :], a["table"][:, CONST["scan"][0]:CONST["scan"][0] + TOK]).then_inc(s_lay3, 16)
                for h in range(HEADS):
                    for d in range(2):
                        act.wait_ge(s_go, SET + l * HEADS + h)
                        act.wait_ge(s_sto, SET + 16 * (l * 2 * HEADS + 2 * h))
                        act.dma_start(st[d][:, 0, :], a["state_gla"].rearrange("b l d h k v -> k (b l d h) v")[
                            :, ds(l * 2 * HEADS + d * HEADS + h, 1), :]).then_inc(s_st0[d], 16)
                    act.wait_ge(s_used, SET + l * UNITS + U_GLA + 2 * h + 1)
                    act.wait_ge(s_y, SET + l * 12 + h)
                    A(qs[:, :], pair(0), ACT.Copy, scale=float(DK) ** -0.5).then_inc(s_gqk, 1)
                    act.wait_ge(s_used, SET + l * UNITS + U_GLA + 2 * h + 2)
                    nc.scalar.copy(ks[:, :], pair(1)).then_inc(s_gqk, 1)
                    hh = l * HEADS + h
                    for d in range(2):
                        act.wait_ge(s_gzb, SET + hh * 2 + d + 1)
                        A(sp_[:, d, :], zb[:, d, :], ACT.Abs)
                        act.drain()
                        A(sp_[:, d, :], sp_[:, d, :], ACT.Exp, scale=-1.0)
                        act.drain()
                        A(sp_[:, d, :], sp_[:, d, :], ACT.Ln, bias=one).then_inc(s_gsp, 1)
                    for d in range(2):
                        act.wait_ge(s_gcb, SET + hh * 2 + d + 1)
                        A(E_[:, d, :], cb[:, d, :], ACT.Exp, scale=1.0 / TAU)
                        A(En[:, d, :], cb[:, d, :], ACT.Exp, scale=-1.0 / TAU).then_inc(s_gE, 1)
                    for d in range(2):
                        act.wait_ge(s_gkT, SET + hh * 2 + d + 1)
                        nc.scalar.copy(zb[:, d, :], pair(2 + d)).then_inc(s_gke, 1)
                    for d in range(2):
                        act.wait_ge(s_gst, SET + hh * 2 + d + 1)
                        act.dma_start(out_st[0, ds(l, 1), d, h].rearrange("l k v -> k (l v)"), st[d][:, SCH + 3, :]).then_inc(s_sto, 16)
                    act.wait_ge(s_go, SET + hh + 1)
                    A(osq[:, :, :], pair(3).rearrange("p (t n) -> p t n", n=DV), ACT.Square).then_inc(s_gsq, 1)
                    act.wait_ge(s_gss, SET + hh + 1)
                    A(g_ln, g_ss, ACT.Ln, bias=eps, scale=1.0 / DV)
                    act.drain()
                    A(g_rs, g_ln, ACT.Exp, scale=-0.5).then_inc(s_grs, 1)
                for kv in range(KVH):
                    j = l * (KVH + 4) + kv
                    act.drain()
                    act.wait_ge(s_y, SET + l * 12 + HEADS)
                    act.wait_ge(s_used, SET + l * UNITS + U_K + kv + 1)
                    act.wait_ge(s_rope, SET + j)
                    act.wait_ge(s_kt, SET + l * KVH + kv)
                    nc.scalar.copy(qraw[:, :], pair(0)).then_inc(s_kraw, 1)
                    act.drain()
                    nc.scalar.copy(kT[:, kv, P + SAMPLE:], qraw[:, SAMPLE:])
                    act.wait_ge(s_kt, SET + l * KVH + kv + 1)
                    nc.scalar.copy(kT[:, kv, 0:P], ps[:, 5, 0:P])
                    nc.scalar.copy(kout[:, kv, :], ps[:, 5, P:P + HD]).then_inc(s_kc, 1)
                act.wait_ge(s_kc, SET + (l + 1) * KVH)
                act.dma_start(out_ck[0, ds(l, 1)].rearrange("l p k d -> p (l k d)"), kout[:, :, :]).then_inc(s_out, 16)

                def q_chunk(c):
                    j = l * (KVH + 4) + KVH + c
                    act.drain()
                    act.wait_ge(s_used, SET + l * UNITS + U_Q + c + 1)
                    act.wait_ge(s_rope, SET + j)
                    nc.scalar.copy(qraw[:, :], pair(0)).then_inc(s_kraw, 1)
                    act.drain()
                    if c >= 2:
                        act.wait_ge(s_sc, SET + (l * AH + 2 * (c - 1)) * TILES)
                    nc.scalar.copy(qT[:, c % 2, SAMPLE:], qraw[:, SAMPLE:]).then_inc(s_qc, 1)

                def exps(hd):
                    i, b_ = hd % 2, l * AH + hd
                    act.wait_ge(s_nm, SET + b_ + 1)
                    for b in range(TILES):
                        lo_, hi_ = span(b)
                        A(s_sb[:, i, b, lo_:hi_], s_sb[:, i, b, lo_:hi_], ACT.Exp, bias=a_nm[:, b:b + 1], accum_out=a_rs[:, b:b + 1])
                    A(a_es, a_nm, ACT.Exp, bias=sink[:, hd:hd + 1]).then_inc(s_ex, 1)

                def probs_copy(hd):
                    b_ = l * AH + hd
                    for b in range(TILES):
                        n = ktiles(b) * P
                        act.drain()
                        act.wait_ge(s_pt, SET + b_ * TILES + b + 1)
                        nc.scalar.copy(pT[:, b % 2, 0:n], ps[:, 2 + b % 2, 0:n]).then_inc(s_pte, 1)

                q_chunk(0)
                for hd in range(AH + 1):
                    if hd < AH:
                        exps(hd)
                        if hd % 2 == 0 and hd < AH - 2:
                            q_chunk(hd // 2 + 1)
                    if hd >= 1:
                        probs_copy(hd - 1)
                for f in range(4):
                    act.drain()
                    act.wait_ge(s_y, SET + l * 12 + HEADS + 4)
                    act.wait_ge(s_used, SET + l * UNITS + U_CONV + 3 * f + 1)
                    act.wait_ge(s_cu, SET + l * 4 + f)
                    nc.scalar.copy(csb[:, :], pair((3 * f) % 4)).then_inc(s_cc, 1)
                hold(act)
                with act.Fori(0, KC) as n:
                    for i in range(3):
                        act.drain()
                        act.wait_ge(s_used, SET + l * UNITS + U_M + n * 6 + 2 * i + 1)
                        if i == 0:
                            act.wait_ge(s_y, SET + (l + 1) * 12)
                        act.wait_ge(s_zm, SET + (l * KC + n) * 3)
                        A(sg[:, i, :], pair((2 * i) % 4), ACT.Sigmoid).then_inc(s_sig, 1)
                act.wait_ge(s_used, SET + l * UNITS + U_OUT)
                act.dma_start(x[:, :, :], x_d.rearrange("(t p) d -> p t d", p=P)).then_inc(s_xload, 16)
                for g in range(2):
                    act.dma_start(gt[:, g, :], mod_d[2, g:g + 1, :].broadcast_to([P, D])).then_inc(s_gtl, 16)
                    act.dma_start(modB[:, g, :], mod_d[3, g:g + 1, :].broadcast_to([P, D])).then_inc(s_modl, 16)
                    act.dma_start(modA[:, g, :], mod_d[4, g:g + 1, :].broadcast_to([P, D])).then_inc(s_modl, 16)
                roots(l, 1)
                for g in range(2):
                    act.dma_start(gt[:, g, :], mod_d[5, g:g + 1, :].broadcast_to([P, D])).then_inc(s_gtl, 16)
                for t in range(TILES):
                    act.wait_ge(s_h, SET + (l * 2 + 1) * TILES + t + 1)
                    act.dma_start(h2_d[t * P:(t + 1) * P, :], hbuf[:, t % 2, :]).then_inc(s_h2s[t % 2], 16)
                    act.drain()
                    act.wait_ge(s_hps, SET + (l * 2 + 1) * TILES + t + 1)
                    if t >= 2:
                        act.wait_ge(s_rl, SET + l * TILES + t - 1)
                    nc.scalar.copy(h2T[:, t % 2, :, :], pair(t % 2, 1024).rearrange("p (k n) -> p k n", k=KC)).then_inc(s_h2T, 1)
                act.wait_ge(s_gx, SET + l + 1)
                A(gex[:, :, :], gex[:, :, :], ACT.Exp)
                A(e21[:, :, :], e21[:, :, :], ACT.Exp).then_inc(s_gxe, 1)
                act.wait_ge(s_info, SET + l + 1)
                done = rounds_before(act, l)
                now = rounds_now(act, l)
                hold(act)
                with act.Fori(0, now) as r:
                    act.wait_ge(r_added, SET + (done + r) * TILES)
                    hold(act)
                    with act.Fori(0, NE // 2) as ep:
                        g = (done + r) * (NE // 2) + ep

                        def half(j):
                            slot, ring = j % RAW, j % SPL
                            act.drain()
                            act.wait_ge(s_rawx[slot], SET + g * 64 + 32 * (j // RAW) + 32)
                            if j >= SPL:
                                act.wait_ge(r_used, SET + g * EXU + j - SPL + 1)
                            else:
                                act.wait_ge(r_used, SET + g * EXU)
                            nc.scalar.copy(w_hi[:, ring, :], raw[:, slot, :]).then_inc(r_hi, 1)

                        def rows(i):
                            act.wait_ge(r_T, SET + g * 2 + i + 1)
                            act.wait_ge(r_used, SET + g * EXU)
                            nc.scalar.copy(xT_hi[:, i, :, :], pair(i, 1024).rearrange("p (k n) -> p k n", k=KC)).then_inc(r_Thi, 1)

                        def silu(i):
                            act.wait_ge(r_used, SET + g * EXU + 4 * (i + 1))
                            act.wait_ge(r_hid, SET + g * 2)
                            A(hg[:, i, :], ps[:, 4 + i, 0:FE], ACT.Silu).then_inc(r_hg, 1)

                        def result(i):
                            act.wait_ge(r_used, SET + g * EXU + 8 + 2 * (i + 1))
                            act.wait_ge(r_ys[i], SET + g * 16)
                            nc.scalar.copy(yo[:, i, :], pair(i, 1024)).then_inc(r_yo, 1)
                            act.wait_ge(r_yo, SET + g * 2 + i + 1)
                            act.dma_start(ye_d[ds((ep * 2 + i) * SLOTS, SLOTS), :], yo[:, i, :]).then_inc(r_ys[i], 16)

                        for j in range(3):
                            half(j)
                        rows(0)
                        rows(1)
                        for j in range(3, 7):
                            half(j)
                        silu(0)
                        for j in range(7, 11):
                            half(j)
                        silu(1)
                        half(11)
                        result(0)
                        result(1)
            for t in range(TILES):
                act.drain()
                act.wait_ge(s_done, SET + DEPTH)
                A(junk[:, :], x[:, t, :], ACT.Square, accum_out=ss[:, t:t + 1])
            act.drain()
            A(sd, ss, ACT.Sqrt, bias=eps, scale=1.0 / D).then_inc(s_fsd, 1)

        @block.vector
        def _(dve):
            set_semaphores(dve, 3)
            V = nc.vector
            gl = lambda t: 0 if t < PT else 1

            def norm_tile(l, which, t, k):
                if t >= 2:
                    dve.wait_ge(s_hps, SET + (l * 2 + which) * TILES + t - 1)
                    if which:
                        dve.wait_ge(s_h2s[t % 2], SET + 16 * (l * tiles_of(t) + t // 2))
                V.scalar_tensor_tensor(hbuf[:, t % 2, :], x[:, t, :], rstd[:, t:t + 1], modA[:, gl(t), :], ALU.mult, ALU.mult)
                dve.drain()
                V.tensor_tensor(hbuf[:, t % 2, :], hbuf[:, t % 2, :], modB[:, gl(t), :], ALU.add).then_inc(s_h, 1)

            dve.wait_ge(s_const, SET + 16 * (3 + 2 * KC))
            with dve.Fori(0, DEPTH) as l:
                for b in range(ADA_BLOCKS):
                    dve.drain()
                    dve.wait_ge(s_lay, SET + (l + 1) * 16 * 6)
                    dve.wait_ge(s_ada, SET + l * ADA + KC * (b + 1))
                    dve.wait_ge(s_mst[b % 2], SET + 16 * (l * 3 + b // 2))
                    ins = V.tensor_tensor(mrow[:, b % 2, :], pair(b % 2, 1024, 2), ada_b[:, b, :], ALU.add)
                    if b % 3 == 1:
                        dve.drain()
                        ins = V.scalar_tensor_tensor(mrow[:, b % 2, :], mrow[:, b % 2, :], 1.0, ada_g[:, b // 3, :], ALU.add, ALU.mult)
                    ins.then_inc(s_mrow, 1)
                dve.wait_ge(s_sd, SET + l * 2 + 1)
                V.reciprocal(rstd, sd)
                dve.drain()
                dve.wait_ge(s_modl, SET + 16 * 8 * l + 64)

                def hT_low(t):
                    dve.wait_ge(s_hhi, SET + l * TILES + t + 1)
                    V.tensor_tensor(hT_lo[:, :, t * P:(t + 1) * P], pair(2 + t % 2, 1024).rearrange("p (k n) -> p k n", k=KC),
                                    hT_hi[:, :, t * P:(t + 1) * P].bitcast(F32), ALU.subtract).then_inc(s_hT, 1)

                norm_tile(l, 0, 0, 0)
                norm_tile(l, 0, 1, 0)
                for t in range(TILES):
                    hT_low(t)
                    if t + 2 < TILES:
                        norm_tile(l, 0, t + 2, 0)
                dve.wait_ge(s_lay2, SET + (l + 1) * 16 * 21)
                for t in range(TILES):
                    dve.wait_ge(s_r, SET + l * TILES + t + 1)
                    V.tensor_tensor(rg[:, t, :], rg[:, t, :], g_norm[:, :], ALU.mult)
                dve.drain()
                dve.wait_ge(s_lay3, SET + (l + 1) * 16)
                dve.wait_ge(s_xsav, SET + 16 * (l + 1))
                for d in range(2):
                    V.memset(st[d][:, SCH + 1, :], 0.0)
                    V.memset(attm[:, d, :, :], 0.0)
                for h in range(HEADS):
                    hh = l * HEADS + h
                    for d in range(2):
                        dve.drain()
                        dve.wait_ge(s_gz, SET + hh * 2 + d + 1)
                        V.tensor_scalar(zb[:, d, :], pair(2 + d), b_gate[:, d, h:h + 1], None, ALU.add).then_inc(s_gzb, 1)
                    for d in range(2):
                        dve.wait_ge(s_gsp, SET + hh * 2 + d + 1)
                        V.scalar_tensor_tensor(zb[:, d, :], zb[:, d, :], 0.0, sp_[:, d, :], ALU.min, ALU.subtract)
                        dve.drain()
                        if d == 0:
                            V.tensor_tensor_scan(cb[:, d, :], scanm[:, :], zb[:, d, :], 0.0, ALU.mult, ALU.add).then_inc(s_gcb, 1)
                        else:
                            V.tensor_tensor_scan(cb[:, d, ::-1], scanm[:, :], zb[:, d, ::-1], 0.0, ALU.mult, ALU.add).then_inc(s_gcb, 1)
                    for d in range(2):
                        dve.wait_ge(s_gqk, SET + hh * 2 + 2)
                        dve.wait_ge(s_gE, SET + hh * 2 + d + 1)
                        V.tensor_tensor(cb[:, d, :], qs[:, :], E_[:, d, :], ALU.mult)
                        V.tensor_tensor(En[:, d, :], ks[:, :], En[:, d, :], ALU.mult)
                        dve.drain()
                        last = CHUNK - 1 if d == 0 else 0
                        ev = E_[:, d, :].rearrange("p (n c) -> p n c", c=CHUNK)[:, :, last:last + 1].broadcast_to([P, NCH, CHUNK])
                        V.tensor_tensor(sp_[:, d, :].rearrange("p (n c) -> p n c", c=CHUNK), En[:, d, :].rearrange("p (n c) -> p n c", c=CHUNK),
                                        ev, ALU.mult).then_inc(s_gin, 1)
                    for d in range(2):
                        dve.wait_ge(s_gatt, SET + hh * 2 + d + 1)
                        hold(dve)
                        for o in (0, CHUNK):
                            c = slice(o, o + CHUNK)
                            m = C(("fwd", "bwd")[d])[c, :].bitcast(I32).rearrange("p (o c) -> p o c", o=1).broadcast_to([CHUNK, TILES, CHUNK])
                            ins = V.copy_predicated(attm[c, d, :, c], m, pair(d)[c, :].rearrange("p (t c) -> p t c", c=P)[:, :, c])
                        ins.then_inc(s_gam, 1)
                    for d in range(2):
                        dve.drain()
                        dve.wait_ge(s_gds, SET + hh * 4 + 2 * d + 2)
                        dve.wait_ge(s_st0[d], SET + 16 * (hh + 1))
                        dst_ = psf[:, 1536 * d:1536 * d + NCH * DV].rearrange("p (n v) -> p n v", v=DV)
                        steps = [(i, i if d == 0 else SCH - 1 - i) for i in range(SCH - 1)]
                        steps += [(SCH + 1 + i, SCH + i if d == 0 else NCH - 1 - i) for i in range(2)]
                        for q, (i, n) in enumerate(sorted(steps, key=lambda s: s[0] % (SCH + 1))):
                            if q:
                                dve.drain()
                            e_col = n * CHUNK + (CHUNK - 1 if d == 0 else 0)
                            ins = V.scalar_tensor_tensor(st[d][:, i + 1, :], st[d][:, i, :], E_[:, d, e_col:e_col + 1], dst_[:, n, :], ALU.mult, ALU.add)
                        ins.then_inc(s_gst, 1)
                    dve.wait_ge(s_gsq, SET + hh + 1)
                    V.tensor_reduce(g_ss, osq[:, :, :], AX.X, ALU.add).then_inc(s_gss, 1)
                    dve.wait_ge(s_grs, SET + hh + 1)
                    for t in range(TILES):
                        ins = V.scalar_tensor_tensor(yb[:, t, :], pair(3)[:, t * DV:(t + 1) * DV], g_rs[:, t:t + 1], rg[:, t, h * DV:(h + 1) * DV],
                                                     ALU.mult, ALU.mult)
                    ins.then_inc(s_gy, 1)
                    dve.wait_ge(s_gyT, SET + hh + 1)
                    V.tensor_copy(yT_hi[:, 4 + h, :], pair(2))
                    dve.drain()
                    V.tensor_tensor(yT_lo[:, 4 + h, :], pair(2), yT_hi[:, 4 + h, :].bitcast(F32), ALU.subtract).then_inc(s_y, 1)

                dve.drain()
                for i in range(2):
                    V.memset(s_sb[:, i, 0, 0:P], -BIG)
                    V.memset(s_sb[:, i, PT - 1, 3 * P:], -BIG)
                    V.memset(s_sb[:, i, PT, 0:P], -BIG)
                    V.memset(s_sb[:, i, PT, 2 * P:], -BIG)

                def rope(j, dst):
                    dve.drain()
                    dve.wait_ge(s_kraw, SET + l * (KVH + 4) + j + 1)
                    V.tensor_tensor(rt1[:, :], qraw[:, 0:SAMPLE], cossin[:, 0, :], ALU.mult)
                    dve.wait_ge(s_rot, SET + l * (KVH + 4) + j + 1)
                    V.tensor_tensor(rt2[:, :], ps[:, 4, :], cossin[:, 1, :], ALU.mult)
                    dve.drain()
                    V.tensor_tensor(dst, rt1[:, :], rt2[:, :], ALU.add).then_inc(s_rope, 1)

                rope(0, kT[:, 0, P:P + SAMPLE])
                rope(1, kT[:, 1, P:P + SAMPLE])
                rope(2, qT[:, 0, 0:SAMPLE])

                def scores(hd):
                    i, b_ = hd % 2, l * AH + hd
                    if hd >= 2:
                        dve.wait_ge(s_pt, SET + (b_ - 1) * TILES)
                    for b in range(TILES):
                        lo_, hi_ = span(b)
                        dve.wait_ge(s_sc, SET + b_ * TILES + b + 1)
                        V.scalar_tensor_tensor(s_sb[:, i, b, lo_:hi_], ps[:, 5 + b % 2, lo_:hi_], float(HD) ** -0.5, strip[:, lo_:hi_],
                                               ALU.mult, ALU.add).then_inc(s_sce, 1)
                    dve.drain()
                    V.tensor_reduce(a_mx, s_sb[:, i, :, :], AX.X, ALU.max)
                    dve.drain()
                    V.tensor_scalar(a_nm, a_mx, sink[:, hd:hd + 1], -1.0, ALU.max, ALU.mult).then_inc(s_nm, 1)

                def normalise(hd):
                    i = hd % 2
                    dve.wait_ge(s_ex, SET + l * AH + hd + 1)
                    V.tensor_tensor(a_rd, a_rs, a_es, ALU.add)
                    dve.drain()
                    V.reciprocal(a_rd, a_rd)
                    dve.drain()
                    for b in range(TILES):
                        lo_, hi_ = span(b)
                        ins = V.tensor_scalar(s_sb[:, i, b, lo_:hi_], s_sb[:, i, b, lo_:hi_], a_rd[:, b:b + 1], None, ALU.mult)
                    ins.then_inc(s_p, 1)

                def take_y(c):
                    dve.wait_ge(s_ao, SET + l * 4 + c + 1)
                    dve.wait_ge(s_sto, SET + 16 * 2 * HEADS * (l + 1))
                    V.tensor_copy(yT_hi[:, 8 + c, 0:SAMPLE], ps[:, 7, :])
                    V.tensor_copy(yT_hi[:, 8 + c, SAMPLE:], ps[:, 1, 256:384])
                    dve.drain()
                    V.tensor_tensor(yT_lo[:, 8 + c, 0:SAMPLE], ps[:, 7, :], yT_hi[:, 8 + c, 0:SAMPLE].bitcast(F32), ALU.subtract)
                    V.tensor_tensor(yT_lo[:, 8 + c, SAMPLE:], ps[:, 1, 256:384], yT_hi[:, 8 + c, SAMPLE:].bitcast(F32), ALU.subtract).then_inc(s_y, 1)

                for hd in range(AH + 1):
                    if hd < AH:
                        scores(hd)
                        normalise(hd)
                    if hd % 2 == 0 and hd >= 2:
                        take_y(hd // 2 - 1)
                    if hd % 2 == 0 and hd < AH - 2:
                        rope(3 + hd // 2, qT[:, (hd // 2 + 1) % 2, 0:SAMPLE])
                dve.drain()
                for z in (0, SAMPLE + 1, SAMPLE + 2, TOK + 3):
                    V.memset(upad[:, z:z + 1], 0.0)
                for f in range(4):
                    dve.drain()
                    dve.wait_ge(s_cc, SET + l * 4 + f + 1)
                    dve.wait_ge(s_used, SET + l * UNITS + U_CONV + 3 * f + 2)
                    hp = pair((3 * f + 1) % 4)
                    V.tensor_tensor(upad[:, 1:SAMPLE + 1], hp[:, 0:SAMPLE], csb[:, 0:SAMPLE], ALU.mult)
                    V.tensor_tensor(upad[:, SAMPLE + 3:TOK + 3], hp[:, SAMPLE:], csb[:, SAMPLE:], ALU.mult).then_inc(s_cu, 1)
                    dve.drain()
                    for j in range(CONV_K):
                        for a0, u0, n in ((0, 0, SAMPLE), (SAMPLE, SAMPLE + 2, PROMPT)):
                            if j == 0:
                                V.tensor_scalar(yf[:, a0:a0 + n], upad[:, u0:u0 + n], conv_w[:, f, 0:1], None, ALU.mult)
                            else:
                                V.scalar_tensor_tensor(yf[:, a0:a0 + n], upad[:, u0 + j:u0 + j + n], conv_w[:, f, j:j + 1], yf[:, a0:a0 + n],
                                                       ALU.mult, ALU.add)
                        dve.drain()
                    dve.wait_ge(s_used, SET + l * UNITS + U_CONV + 3 * f + 3)
                    dve.wait_ge(s_out, SET + 32 * (l + 1))
                    V.tensor_tensor(yf[:, :], yf[:, :], pair((3 * f + 2) % 4), ALU.mult).then_inc(s_cy, 1)
                    dve.drain()
                    V.tensor_copy(yT_hi[:, f, :], yf[:, :])
                    dve.drain()
                    V.tensor_tensor(yT_lo[:, f, :], yf[:, :], yT_hi[:, f, :].bitcast(F32), ALU.subtract).then_inc(s_y, 1)
                hold(dve)
                with dve.Fori(0, KC) as n:
                    for i in range(3):
                        g = (l * KC + n) * 3
                        dve.drain()
                        dve.wait_ge(s_sig, SET + g + i + 1)
                        dve.wait_ge(s_used, SET + l * UNITS + U_M + n * 6 + 2 * i + 2)
                        V.tensor_tensor((zacc if i == 0 else zt)[:, :], sg[:, i, :], pair((2 * i + 1) % 4), ALU.mult).then_inc(s_zm, 1)
                        dve.drain()
                        if i:
                            V.tensor_tensor(zacc[:, :], zacc[:, :], zt[:, :], ALU.add)
                            dve.drain()
                    V.tensor_copy(zT_hi[:, ds(n, 1), :], zacc[:, :].rearrange("p (o c) -> p o c", o=1))
                    dve.drain()
                    V.tensor_tensor(zT_lo[:, ds(n, 1), :], zacc[:, :].rearrange("p (o c) -> p o c", o=1),
                                    zT_hi[:, ds(n, 1), :].bitcast(F32), ALU.subtract).then_inc(s_z, 1)
                for hf in range(2):
                    for t in range(TILES):
                        c0 = 512 * hf
                        dve.drain()
                        dve.wait_ge(s_xload, SET + 16 * (l + 1))
                        dve.wait_ge(s_gtl, SET + 64 * l + 32)
                        dve.wait_ge(s_used, SET + l * UNITS + U_OUT + 4 * (hf + 1))
                        V.tensor_tensor(hbuf[:, t % 2, 0:512], ps[:, (5 * hf + t) % 8, :], gt[:, gl(t), c0:c0 + 512], ALU.mult)
                        dve.drain()
                        V.tensor_tensor(x[:, t, c0:c0 + 512], x[:, t, c0:c0 + 512], hbuf[:, t % 2, 0:512], ALU.add).then_inc(s_x1, 1)
                dve.wait_ge(s_sd, SET + l * 2 + 2)
                V.reciprocal(rstd, sd)
                dve.drain()
                dve.wait_ge(s_modl, SET + 16 * 8 * (l + 1))
                for t in range(TILES):
                    norm_tile(l, 1, t, 0)
                dve.wait_ge(s_rl, SET + (l + 1) * TILES)
                V.tensor_tensor(lgt[:, :, :], ps[:, 7, 0:TILES * 32].rearrange("p (t n) -> p t n", n=32)[:, :, 0:NG + NE],
                                b_rt[:, :].rearrange("p (o n) -> p o n", o=1).broadcast_to([P, TILES, NG + NE]), ALU.add).then_inc(s_rlog, 1)
                dve.drain()
                lg = lgt[:, :, 0:NG]

                def bc(ap, n):
                    return ap.broadcast_to([P, TILES, n])

                def tt(o, i0, i1, op):
                    V.tensor_tensor(o, i0, i1, op)
                    dve.drain()

                def first_best(oh, scores_, mx, eq, pk, top):
                    V.tensor_reduce(mx[:, :, 0], scores_, AX.X, ALU.max)
                    dve.drain()
                    tt(eq[:, :, :], scores_, bc(mx[:, :, :], NG), ALU.is_equal)
                    tt(pk[:, :, :], eq[:, :, :], C("prio").rearrange("p (o n) -> p o n", o=1).broadcast_to([P, TILES, NG]), ALU.mult)
                    V.tensor_reduce(top[:, :, 0], pk[:, :, :], AX.X, ALU.max)
                    dve.drain()
                    tt(oh[:, :, :], pk[:, :, :], bc(top[:, :, :], NG), ALU.is_equal)

                first_best(goh, lg, gmax, geq, gpk, gsum)
                tt(gex[:, :, :], lg, bc(gmax[:, :, :], NG), ALU.subtract)
                le = lgt[:, :, NG:].rearrange("p t (g j) -> p t j g", g=NG)
                for t in range(TILES):
                    V.tensor_tensor(lsel4[:, t, :, :], le[:, t, :, :], goh[:, t, :].rearrange("p (o g) -> p o g", o=1).broadcast_to([P, EPG, NG]), ALU.mult)
                dve.drain()
                V.tensor_reduce(lsel[:, :, :], lsel4[:, :, :, :], AX.X, ALU.add)
                dve.drain()
                first_best(oh1, lsel[:, :, :], m1, geq, gpk, gsum)
                V.scalar_tensor_tensor(lsel2[:, :, :], oh1[:, :, :], -BIG, lsel[:, :, :], ALU.mult, ALU.add)
                dve.drain()
                first_best(oh2, lsel2[:, :, :], m2, geq, gpk, gsum)
                V.tensor_tensor(e21[:, :, :], m2[:, :, :], m1[:, :, :], ALU.subtract).then_inc(s_gx, 1)
                dve.wait_ge(s_gxe, SET + l + 1)
                V.tensor_reduce(gsum[:, :, 0], gex[:, :, :], AX.X, ALU.add)
                V.tensor_scalar(wt1[:, :, :], e21[:, :, :], 1.0, None, ALU.add)
                dve.drain()
                V.reciprocal(pgrp[:, :, :], gsum[:, :, :])
                V.reciprocal(wt2[:, :, :], wt1[:, :, :])
                dve.drain()
                tt(wt1[:, :, :], pgrp[:, :, :], wt2[:, :, :], ALU.mult)
                tt(wt2[:, :, :], wt1[:, :, :], e21[:, :, :], ALU.mult)
                for t in range(TILES):
                    for oh, Ek in ((oh1, E1), (oh2, E2)):
                        V.tensor_tensor(Ek[:, t, :].rearrange("p (g j) -> p g j", g=NG), goh[:, t, :].rearrange("p (g o) -> p g o", o=1).broadcast_to([P, NG, EPG]),
                                        oh[:, t, :].rearrange("p (o j) -> p o j", o=1).broadcast_to([P, NG, EPG]), ALU.mult)
                dve.drain()
                V.tensor_tensor(Em[:, :, :], E1[:, :, :], E2[:, :, :], ALU.add).then_inc(s_rM, 1)
                dve.wait_ge(s_rk, SET + l + 1)
                rk = ps[:, 6, 0:TILES * NE].rearrange("p (t e) -> p t e", e=NE)
                V.scalar_tensor_tensor(rkm[:, :, :], rk, 1.0, Em[:, :, :], ALU.add, ALU.mult)
                V.tensor_reduce(cmax[:, :], ps[:, 6, TILES * NE:TILES * NE + NE], AX.X, ALU.max)
                dve.drain()
                V.tensor_scalar(rkm[:, :, :], rkm[:, :, :], -1.0, None, ALU.add)
                V.tensor_tensor(cge[:, :], cmax[:, :].broadcast_to([P, 4]), C("thr"), ALU.is_gt)
                for k, Ek in enumerate((E1, E2)):
                    tt(rtmp[:, :, :], rk, Ek[:, :, :], ALU.mult)
                    V.tensor_reduce(rsel[:, k, :], rtmp[:, :, :], AX.X, ALU.add)
                    tt(rpos[:, :, :], C("base").rearrange("p (o e) -> p o e", o=1).broadcast_to([P, TILES, NE]), Ek[:, :, :], ALU.mult)
                    V.tensor_reduce(bsel[:, k, :], rpos[:, :, :], AX.X, ALU.add)
                    dve.drain()
                V.tensor_reduce(cr[:, :], cge[:, :], AX.X, ALU.add)
                V.tensor_copy(crf[:, 0:1], info[:, ds(l * 2, 1)])
                dve.drain()
                V.tensor_scalar(cr[:, :], cr[:, :], 1.0, None, ALU.add)
                dve.drain()
                V.tensor_copy(info[:, ds(l * 2 + 1, 1)], cr[:, :])
                V.tensor_tensor(crf[:, 1:2], crf[:, 0:1], cr[:, :], ALU.add)
                dve.drain()
                V.tensor_copy(info[:, ds(l * 2 + 2, 1)], crf[:, 1:2]).then_inc(s_info, 1)
                dve.wait_ge(s_info, SET + l + 1)
                done = rounds_before(dve, l)
                now = rounds_now(dve, l)
                hold(dve)
                with dve.Fori(0, now) as r:
                    hold(dve)
                    with dve.Fori(0, NE // 2) as ep:
                        for i in range(2):
                            g = (done + r) * NE + ep * 2
                            dve.wait_ge(r_idx, SET + g)
                            V.tensor_tensor(onehot[:, i, :, :], iota.rearrange("p (o s) -> p o s", o=1).broadcast_to([P, TILES, SLOTS]),
                                            rkm[:, :, ds(ep * 2 + i, 1)].broadcast_to([P, TILES, SLOTS]), ALU.is_equal).then_inc(r_oh, 1)
                            dve.drain()
                    dve.wait_ge(r_idx, SET + (done + r + 1) * NE)
                    V.tensor_copy(sidx[:, :], ps[:, 5, 0:NE]).then_inc(r_slots, 1)
                    V.tensor_scalar(rkm[:, :, :], rkm[:, :, :], -float(SLOTS), None, ALU.add)
                    V.tensor_scalar(posf[:, :, :], rsel[:, :, :], 0.0, float(SLOTS - 1), ALU.max, ALU.min)
                    V.tensor_scalar(inr[:, :, :], rsel[:, :, :], 0.0, None, ALU.is_ge)
                    V.tensor_scalar(in2[:, :, :], rsel[:, :, :], float(SLOTS), None, ALU.is_lt)
                    dve.drain()
                    V.tensor_tensor(posf[:, :, :], posf[:, :, :], bsel[:, :, :], ALU.add)
                    V.tensor_tensor(inr[:, :, :], inr[:, :, :], in2[:, :, :], ALU.mult)
                    V.tensor_scalar(rsel[:, :, :], rsel[:, :, :], -float(SLOTS), None, ALU.add)
                    dve.drain()
                    V.tensor_copy(pos[:, :, :], posf[:, :, :])
                    V.tensor_tensor(wsel[:, 0, :], inr[:, 0, :], wt1[:, :, 0], ALU.mult)
                    V.tensor_tensor(wsel[:, 1, :], inr[:, 1, :], wt2[:, :, 0], ALU.mult).then_inc(r_slots, 1)
                    dve.drain()
                    hold(dve)
                    with dve.Fori(0, NE // 2) as ep:
                        g = (done + r) * (NE // 2) + ep

                        def low(j):
                            slot, ring = j % RAW, j % SPL
                            dve.drain()
                            dve.wait_ge(r_hi, SET + g * EXU + j + 1)
                            V.tensor_tensor(w_lo[:, ring, :], raw[:, slot, :], w_hi[:, ring, :].bitcast(F32), ALU.subtract).then_inc(r_lo, 1)

                        def rows(i):
                            dve.drain()
                            dve.wait_ge(r_Thi, SET + g * 2 + i + 1)
                            V.tensor_tensor(xT_lo[:, i, :, :], pair(i, 1024).rearrange("p (k n) -> p k n", k=KC), xT_hi[:, i, :, :].bitcast(F32),
                                            ALU.subtract).then_inc(r_Tlo, 1)

                        def hidden(i):
                            dve.drain()
                            dve.wait_ge(r_hg, SET + g * 2 + i + 1)
                            dve.wait_ge(r_HT, SET + g * 2)
                            V.tensor_tensor(hid[:, i, :], hg[:, i, :], ps[:, 4 + i, FE:2 * FE], ALU.mult).then_inc(r_hid, 1)

                        def turned(i):
                            src = ps[:, 6, 256 * i:256 * i + 256].rearrange("p (k n) -> p k n", k=2)
                            dve.wait_ge(r_HT, SET + g * 2 + i + 1)
                            V.tensor_copy(hidT_hi[:, i, :, :], src)
                            dve.drain()
                            V.tensor_tensor(hidT_lo[:, i, :, :], src, hidT_hi[:, i, :, :].bitcast(F32), ALU.subtract).then_inc(r_hT, 1)

                        for j in range(3):
                            low(j)
                        rows(0)
                        rows(1)
                        for j in range(3, 7):
                            low(j)
                        hidden(0)
                        for j in range(7, 10):
                            low(j)
                        turned(0)
                        low(10)
                        hidden(1)
                        turned(1)
                        low(11)
                    dve.wait_ge(s_gtl, SET + 64 * (l + 1))
                    for t in range(TILES):
                        dve.wait_ge(s_yg[t % 2], 32 * ((done + r) * tiles_of(t) + t // 2 + 1))
                        V.tensor_scalar(yg[:, t % 2, 0, :], yg[:, t % 2, 0, :], wsel[:, 0, t:t + 1], None, ALU.mult)
                        dve.drain()
                        V.scalar_tensor_tensor(yg[:, t % 2, 0, :], yg[:, t % 2, 1, :], wsel[:, 1, t:t + 1], yg[:, t % 2, 0, :], ALU.mult, ALU.add)
                        dve.drain()
                        V.tensor_tensor(yg[:, t % 2, 0, :], yg[:, t % 2, 0, :], gt[:, gl(t), :], ALU.mult)
                        dve.drain()
                        V.tensor_tensor(x[:, t, :], x[:, t, :], yg[:, t % 2, 0, :], ALU.add).then_inc(r_added, 1)
                dve.drain()
                dve.sem_inc(s_done, 1)
            dve.wait_ge(s_fsd, SET + 1)
            V.reciprocal(rstd, sd)
            dve.drain()
            dve.wait_ge(s_fg, SET + 16)
            for t in range(TILES):
                V.scalar_tensor_tensor(x[:, t, :], x[:, t, :], rstd[:, t:t + 1], gt[:, 0, :], ALU.mult, ALU.mult).then_inc(s_fy, 1)

        @block.tensor
        def _(pe):
            set_semaphores(pe, 4)
            mm = nc.tensor.matmul
            tr = nc.tensor.transpose

            def passes(ring):
                return ((w_hi[:, ring, :], 0), (w_hi[:, ring, :], 1), (w_lo[:, ring, :], 0))

            def feature(l, u, b, act_pair, value=None, k0=0, nk=KC, m=P, chunk0=0):
                ring = u % SPL
                pe.wait_ge(s_split, SET + (l * UNITS + u + 1 if value is None else value))
                for k in range(nk):
                    for i, (w, h) in enumerate(passes(ring)):
                        for c0, c1 in ((0, SAMPLE), (SAMPLE, TOK)):
                            ins = mm(psf[0:m, 1024 * b + c0:1024 * b + c1], w[:, k * m:(k + 1) * m], act_pair[h][:, chunk0 + k, c0:c1],
                                     start=(k == 0 and i == 0), stop=(k == nk - 1 and i == 2))
                ins.then_inc(s_used, 1)

            def tokens(l, u, j, act_pair, bank):
                ring = u % SPL
                pe.wait_ge(s_split, SET + l * UNITS + u + 1)
                for kk in range(2):
                    k = 2 * j + kk
                    cols = slice(512 * kk, 512 * kk + 512)
                    for t in range(TILES):
                        for i, (w, h) in enumerate(passes(ring)):
                            ins = mm(ps[:, bank(t), :], act_pair[h][:, k, t * P:(t + 1) * P], w[:, cols],
                                     start=(k == 0 and i == 0), stop=(k == KC - 1 and i == 2))
                ins.then_inc(s_used, 1)

            hT, yT, zT = (hT_hi, hT_lo), (yT_hi, yT_lo), (zT_hi, zT_lo)
            pe.wait_ge(s_const, SET + 16 * (3 + 2 * KC))
            pe.wait_ge(s_cond, SET + 1)
            with pe.Fori(0, DEPTH) as l:
                pe.wait_ge(s_done, SET + l)
                for b in range(ADA_BLOCKS):
                    if b >= 2:
                        pe.wait_ge(s_mrow, SET + l * ADA_BLOCKS + b - 1)
                    for k in range(KC):
                        u = b * KC + k
                        slot = u % RAW
                        per_layer = raw_value(1, 0) - raw_value(0, 0) if slot == 0 else raw_value(1, slot) - raw_value(0, slot)
                        pe.wait_ge(s_raw[slot], SET + l * per_layer + 16 * (u // RAW + 1))
                        for c in range(2):
                            ins = mm(ps[0:2, 2 * (b % 2) + c, :], condT[:, k, :], raw[:, slot, 512 * c:512 * c + 512], start=(k == 0), stop=(k == KC - 1))
                        ins.then_inc(s_ada, 1)
                for t in range(TILES):
                    pe.wait_ge(s_h, SET + l * 2 * TILES + t + 1)
                    if t >= 2:
                        pe.wait_ge(s_hT, SET + l * TILES + t - 1)
                    for k in range(KC):
                        ins = tr(psf[:, 1024 * (2 + t % 2) + k * P:1024 * (2 + t % 2) + (k + 1) * P], hbuf[:, t % 2, k * P:(k + 1) * P], ident)
                    ins.then_inc(s_hps, 1)
                pe.wait_ge(s_hT, SET + (l + 1) * TILES)
                pe.wait_ge(s_mrow, SET + (l + 1) * ADA_BLOCKS)
                for j in range(4):
                    tokens(l, U_V + j, j, hT, lambda t: t)
                pe.wait_ge(s_v, SET + (l + 1) * TILES)
                for j in range(4):
                    tokens(l, U_R + j, j, hT, lambda t: (5 + t) % 8)
                pe.wait_ge(s_split, SET + l * UNITS + U_TV + 1)
                for t in range(TILES):
                    for k in range(KC):
                        for i, (w, h) in enumerate(passes(U_TV % SPL)):
                            ins = mm(psf[:, 1024 + t * P:1024 + (t + 1) * P], hT[h][:, k, t * P:(t + 1) * P], w[:, k * P:(k + 1) * P],
                                     start=(k == 0 and i == 0), stop=(k == KC - 1 and i == 2))
                ins.then_inc(s_used, 1)
                pe.wait_ge(s_r, SET + (l + 1) * TILES)
                feature(l, U_LR, 2, hT, m=2 * RANK)
                pe.wait_ge(s_tv, SET + l + 1)
                pe.wait_ge(s_lr, SET + l + 1)
                pe.wait_ge(s_lay2, SET + (l + 1) * 16 * 21)
                for h in range(HEADS):
                    hh = l * HEADS + h
                    pe.wait_ge(s_gst, SET + hh * 2)
                    feature(l, U_GLA + 2 * h, 0, hT)
                    feature(l, U_GLA + 2 * h + 1, 1, hT)
                    pe.wait_ge(s_y, SET + l * 12 + h)
                    for d in range(2):
                        for c0, c1 in ((0, SAMPLE), (SAMPLE, TOK)):
                            ins = mm(psf[:, 1024 * (2 + d) + c0:1024 * (2 + d) + c1], w_gate[:, d, h * DK:(h + 1) * DK], lrT[:, c0:c1], start=True, stop=True)
                        ins.then_inc(s_gz, 1)
                    for d in range(2):
                        pe.wait_ge(s_gin, SET + hh * 2 + d + 1)
                        for t in range(TILES):
                            ins = tr(psf[:, 1024 * (2 + d) + t * P:1024 * (2 + d) + (t + 1) * P], sp_[:, d, t * P:(t + 1) * P], ident)
                        ins.then_inc(s_gkT, 1)
                        for t in range(TILES):
                            cs = slice(t * P, (t + 1) * P)
                            ins = mm(psf[:, 1024 * d + t * P:1024 * d + (t + 1) * P], En[:, d, cs], cb[:, d, cs], start=True, stop=True)
                        ins.then_inc(s_gatt, 1)
                    for d in range(2):
                        pe.wait_ge(s_gke, SET + hh * 2 + d + 1)
                        pe.wait_ge(s_gam, SET + hh * 2 + 2)
                        for q in range(2):
                            if q:
                                pe.wait_ge(s_gds, SET + hh * 4 + 2 * d + 1)
                                hold(pe)
                            o = CHUNK * q
                            for t in range(TILES):
                                n = 2 * t + q
                                ins = mm(psf[:, 1536 * d + n * DV:1536 * d + (n + 1) * DV], zb[o:o + CHUNK, d, t * P:(t + 1) * P],
                                         v_sb[o:o + CHUNK, t, h * DV:(h + 1) * DV], start=True, stop=True)
                            ins.then_inc(s_gds, 1)
                    pe.wait_ge(s_gst, SET + hh * 2 + 2)
                    hold(pe)
                    for t in range(TILES):
                        dst = ps[:, 6 + t // 4, (t % 4) * DV:(t % 4 + 1) * DV]
                        for d in range(2):
                            mm(dst, attm[:, d, t, :], v_sb[:, t, h * DV:(h + 1) * DV], start=(d == 0), stop=False, skip_group_check=True)
                        for d in range(2):
                            for n in (2 * t, 2 * t + 1):
                                o = CHUNK * (n % 2)
                                if n < SCH:
                                    i = n if d == 0 else SCH - 1 - n
                                else:
                                    i = SCH + 1 + (n - SCH if d == 0 else NCH - 1 - n)
                                ins = mm(dst[o:o + CHUNK, :], cb[:, d, n * CHUNK:(n + 1) * CHUNK], st[d][:, i, :], start=False, stop=(d == 1),
                                         skip_group_check=True)
                    ins.then_inc(s_go, 1)
                    pe.wait_ge(s_gy, SET + hh + 1)
                    for t in range(TILES):
                        ins = tr(psf[:, 2048 + t * P:2048 + (t + 1) * P], yb[:, t, :], ident)
                    ins.then_inc(s_gyT, 1)
                for kv in range(KVH):
                    j = l * (KVH + 4) + kv
                    pe.wait_ge(s_kraw, SET + j)
                    feature(l, U_K + kv, 0, hT)
                    if kv == 0:
                        pe.wait_ge(s_y, SET + l * 12 + HEADS)
                    pe.wait_ge(s_kraw, SET + j + 1)
                    pe.wait_ge(s_rope, SET + j)
                    mm(ps[:, 4, :], rot, qraw[:, 0:SAMPLE], start=True, stop=True).then_inc(s_rot, 1)
                    pe.wait_ge(s_kc, SET + l * KVH + kv)
                    tr(ps[:, 5, 0:P], ckd[:, kv, :, :], ident)
                    tr(ps[:, 5, P:2 * P], qraw[:, SAMPLE:], ident).then_inc(s_kt, 1)

                def q_chunk(c):
                    j = l * (KVH + 4) + KVH + c
                    pe.wait_ge(s_kraw, SET + j)
                    feature(l, U_Q + c, 0, hT)
                    pe.wait_ge(s_kraw, SET + j + 1)
                    pe.wait_ge(s_rope, SET + j)
                    mm(ps[:, 4, :], rot, qraw[:, 0:SAMPLE], start=True, stop=True).then_inc(s_rot, 1)

                def scores(hd):
                    c, o, kv, b_ = hd // 2, HD * (hd % 2), hd // 4, l * AH + hd
                    if hd == 0:
                        pe.wait_ge(s_kc, SET + (l + 1) * KVH)
                    if hd % 2 == 0:
                        pe.wait_ge(s_rope, SET + l * (KVH + 4) + KVH + c + 1)
                        pe.wait_ge(s_qc, SET + l * 4 + c + 1)
                    rows = slice(o, o + HD)
                    for b in range(TILES):
                        n = b_ * TILES + b
                        if b >= 2:
                            pe.wait_ge(s_sce, SET + n - 1)
                        else:
                            pe.wait_ge(s_sce, SET + b_ * TILES)
                        q = qT[rows, c % 2, b * P:(b + 1) * P]
                        dst = ps[:, 5 + b % 2, :]
                        own_ = P + b * P
                        if b == PT:
                            ins = mm(dst[:, P:2 * P], q, kT[rows, kv, own_:own_ + P], start=True, stop=True)
                        else:
                            if b == 0:
                                mm(dst[:, P:2 * P], q, kT[rows, kv, own_:own_ + P], start=True, stop=True)
                            else:
                                mm(dst[:, 0:2 * P], q, kT[rows, kv, own_ - P:own_ + P], start=True, stop=True)
                            ins = mm(dst[:, 2 * P:3 * P], q, kT[rows, kv, 0:P], start=True, stop=True)
                            if b < PT - 1:
                                ins = mm(dst[:, 3 * P:4 * P], q, kT[rows, kv, own_ + P:own_ + 2 * P], start=True, stop=True)
                        ins.then_inc(s_sc, 1)

                def values(hd):
                    c, o, kv, b_ = hd // 2, HD * (hd % 2), hd // 4, l * AH + hd
                    pe.wait_ge(s_p, SET + b_ + 1)
                    if hd % 2 == 0:
                        pe.wait_ge(s_y, SET + l * 12 + HEADS + c)

                    def turn(b):
                        n = b_ * TILES + b
                        lo_, hi_ = span(b)
                        pe.wait_ge(s_pte, SET + (n - 1 if b >= 2 else b_ * TILES))
                        for i in range(ktiles(b)):
                            ins = tr(ps[:, 2 + b % 2, i * P:(i + 1) * P], s_sb[:, hd % 2, b, lo_ + i * P:lo_ + (i + 1) * P], ident)
                        ins.then_inc(s_pt, 1)

                    def weigh(b):
                        pe.wait_ge(s_pte, SET + b_ * TILES + b + 1)
                        vals = [tv[:, PT, :]] if b == PT else (
                            ([tv[:, b - 1, :]] if b > 0 else []) + [tv[:, b, :], cv[:, :]] + ([tv[:, b + 1, :]] if b < PT - 1 else []))
                        dst = ps[o:o + HD, 1, 256:384] if b == PT else ps[o:o + HD, 7, b * P:(b + 1) * P]
                        for i, v in enumerate(vals):
                            ins = mm(dst, v[:, kv * HD:(kv + 1) * HD], pT[:, b % 2, i * P:(i + 1) * P], start=(i == 0), stop=(i == len(vals) - 1))
                        return ins

                    for b in range(TILES + 1):
                        if b < TILES:
                            turn(b)
                        if b >= 1:
                            ins = weigh(b - 1)
                    if hd % 2:
                        ins.then_inc(s_ao, 1)

                q_chunk(0)
                for hd in range(AH + 1):
                    if hd < AH:
                        scores(hd)
                        if hd % 2 == 0 and hd < AH - 2:
                            q_chunk(hd // 2 + 1)
                    if hd >= 1:
                        values(hd - 1)
                pe.wait_ge(s_y, SET + l * 12 + HEADS + 4)
                for f in range(4):
                    for i in range(3):
                        n = 3 * f + i
                        if n >= 4:
                            fo, io = divmod(n - 4, 3)
                            pe.wait_ge((s_cc, s_cu, s_cy)[io], SET + l * 4 + fo + 1)
                        feature(l, U_CONV + n, n % 4, hT)
                pe.wait_ge(s_cy, SET + (l + 1) * 4)
                pe.wait_ge(s_y, SET + (l + 1) * 12)
                hold(pe)
                with pe.Fori(0, KC) as n:
                    for i in range(3):
                        v = l * UNITS + U_M + n * 6 + 2 * i + 1
                        g = (l * KC + n) * 3
                        if i == 2:
                            pe.wait_ge(s_sig, SET + g + 1)
                        else:
                            pe.wait_ge(s_sig, SET + g)
                        feature(l, U_M + 2 * i, (2 * i) % 4, hT, v)
                        if i == 2:
                            pe.wait_ge(s_zm, SET + g + 1)
                        else:
                            pe.wait_ge(s_zm, SET + g)
                        feature(l, U_M + 2 * i + 1, (2 * i + 1) % 4, yT, v + 1, nk=4, chunk0=4 * i)
                pe.wait_ge(s_z, SET + (l + 1) * KC)
                for hf in range(2):
                    if hf == 1:
                        pe.wait_ge(s_x1, SET + l * 2 * TILES + 2)
                    for j in range(4):
                        tokens(l, U_OUT + 4 * hf + j, j, zT, lambda t: (5 * hf + t) % 8)
                pe.wait_ge(s_x1, SET + (l + 1) * 2 * TILES)
                for t in range(TILES + 1):
                    if t < TILES:
                        pe.wait_ge(s_h, SET + (l * 2 + 1) * TILES + t + 1)
                        if t >= 2:
                            pe.wait_ge(s_h2T, SET + l * TILES + t - 1)
                        for k in range(KC):
                            ins = tr(psf[:, 1024 * (t % 2) + k * P:1024 * (t % 2) + (k + 1) * P], hbuf[:, t % 2, k * P:(k + 1) * P], ident)
                        ins.then_inc(s_hps, 1)
                    if t >= 1:
                        pe.wait_ge(s_h2T, SET + l * TILES + t)
                        for k in range(KC):
                            ins = mm(ps[:, 7, (t - 1) * 32:(t - 1) * 32 + NG + NE], h2T[:, (t - 1) % 2, k, :], w_rt[:, k, :], start=(k == 0), stop=(k == KC - 1))
                        ins.then_inc(s_rl, 1)
                pe.wait_ge(s_rM, SET + l + 1)
                for t in range(TILES + 1):
                    for i in range(min(t + 1, TILES)):
                        ins = mm(ps[:, 6, t * NE:(t + 1) * NE], tri if i == t else ones, Em[:, i, :], start=(i == 0), stop=(i == min(t, TILES - 1)))
                ins.then_inc(s_rk, 1)
                pe.wait_ge(s_info, SET + l + 1)
                done = rounds_before(pe, l)
                now = rounds_now(pe, l)
                hold(pe)
                with pe.Fori(0, now) as r:
                    pe.wait_ge(r_hid, SET + (done + r) * NE)
                    hold(pe)
                    with pe.Fori(0, NE // 2) as ep:
                        for i in range(2):
                            pe.wait_ge(r_oh, SET + (done + r) * NE + ep * 2 + i + 1)
                            for t in range(TILES):
                                ins = mm(ps[:, 5, ds(ep * 2 + i, 1)], onehot[:, i, t, :], C("tokid")[:, t:t + 1], start=(t == 0), stop=(t == TILES - 1))
                            ins.then_inc(r_idx, 1)
                    pe.wait_ge(r_slots, SET + (done + r) * 2 + 1)
                    hold(pe)
                    with pe.Fori(0, NE // 2) as ep:
                        g = (done + r) * (NE // 2) + ep

                        def unit(j):
                            pe.wait_ge(r_lo, SET + g * EXU + j + 1)
                            return passes(j % SPL)

                        for i in range(2):
                            pe.wait_ge(r_xg[i], (g + 1) * 16)
                            pe.wait_ge(r_yo, SET + g * 2)
                            for k in range(KC):
                                ins = tr(psf[:, 1024 * i + k * P:1024 * i + (k + 1) * P], xg[:, i, k * P:(k + 1) * P], ident)
                            ins.then_inc(r_T, 1)
                        for i in range(2):
                            pe.wait_ge(r_Tlo, SET + g * 2 + i + 1)
                            pe.wait_ge(r_hid, SET + g * 2)
                            for j in range(4):
                                for kk in range(2):
                                    k = 2 * j + kk
                                    for q, (w, h) in enumerate(unit(4 * i + j) if kk == 0 else passes((4 * i + j) % SPL)):
                                        ins = mm(ps[:, 4 + i, :], (xT_hi, xT_lo)[h][:, i, k, :], w[:, 512 * kk:512 * kk + 512],
                                                 start=(k == 0 and q == 0), stop=(k == KC - 1 and q == 2))
                                ins.then_inc(r_used, 1)
                        for i in range(2):
                            pe.wait_ge(r_hid, SET + g * 2 + i + 1)
                            pe.wait_ge(r_hT, SET + g * 2)
                            for k in range(2):
                                ins = tr(ps[:, 6, 256 * i + k * P:256 * i + (k + 1) * P], hid[:, i, k * P:(k + 1) * P], ident)
                            ins.then_inc(r_HT, 1)
                            pe.wait_ge(r_hT, SET + g * 2 + i + 1)
                            for k in range(2):
                                for q, (w, h) in enumerate(unit(8 + 2 * i + k)):
                                    for c in range(2):
                                        ins = mm(ps[:, 2 * i + c, :], (hidT_hi, hidT_lo)[h][:, i, k, :], w[:, 512 * c:512 * c + 512],
                                                 start=(k == 0 and q == 0), stop=(k == 1 and q == 2))
                                ins.then_inc(r_used, 1)


_INS = ["x_prompt", "x_sample", "state_gla", "cache_k", "cache_v", "c", "c_ctx", "w_ada", "b_ada", "norm1_g", "norm2_g",
        "w_in", "conv_w", "gla_w_gate", "gla_b_gate", "gla_norm_g", "attn_sink", "w_branch", "w_out", "w_route_group",
        "b_route_group", "w_route_expert", "b_route_expert", "w_exp_gate", "w_exp_up", "w_exp_down", "final_norm_g"]
_OUTS = [("y_prompt", (1, PROMPT, D)), ("y_sample", (1, SAMPLE, D)), ("new_state_gla", (1, DEPTH, 2, HEADS, DK, DV)),
         ("new_cache_k", (1, DEPTH, PROMPT, KVH, HD)), ("new_cache_v", (1, DEPTH, PROMPT, KVH, HD))]


def kernel(**inputs):
    import concourse.bacc as bacc
    from concourse.bass_utils import run_bass_kernel_spmd

    nc = bacc.Bacc("TRN2", target_bir_lowering=False, num_devices=1)
    arrays = {n: np.ascontiguousarray(inputs[n]) for n in _INS}
    arrays["table"] = shape_constants()
    arrays["zeros"] = np.zeros((RANK, HEADS * DK), np.float32)
    ins = {n: nc.dram_tensor(f"in_{n}", v.shape, F32, kind="ExternalInput").ap() for n, v in arrays.items()}
    outs = [nc.dram_tensor(f"out_{n}", s, F32, kind="ExternalOutput").ap() for n, s in _OUTS]
    build(nc, ins, *outs)
    r = run_bass_kernel_spmd(nc, [{f"in_{n}": v for n, v in arrays.items()}], core_ids=[0])
    return tuple(r.results[0][f"out_{n}"] for n, _ in _OUTS)
```

```python
from contextlib import ExitStack

import numpy as np

import concourse.bass as bass
import concourse.mybir as mybir

F32 = mybir.dt.float32
F32R = mybir.dt.float32r
I32 = mybir.dt.int32
BF16 = mybir.dt.bfloat16
U32 = mybir.dt.uint32
ALU = mybir.AluOpType
ACT = mybir.ActivationFunctionType
AX = mybir.AxisListType
P = 128

DEPTH, D = 2, 1024
KC = D // P
SAMPLE, PROMPT = 512, 128
TOK = SAMPLE + PROMPT
TILES = TOK // P
PT = TILES - 1
GRID_W = 64
EPS = 1e-6
CONV_W, CONV_K = 512, 3
HEADS, DK, DV, CHUNK = 4, 128, 128, 64
NCH = TOK // CHUNK
HT = TOK // 2
SCH = SAMPLE // CHUNK
RANK, TAU = 16, 16.0
AH, KVH, HD = 8, 2, 64
BR_W = 512
NG, EPG = 4, 4
NE = NG * EPG
FE = 256
SLOTS = P
BIG = 1e30
SET = 1

SPLITS = (CONV_W, CONV_W, CONV_W, HEADS * DK, HEADS * DK, HEADS * DV, HEADS * DV, RANK, RANK, AH * HD, KVH * HD, KVH * HD, D, D, D)
(C_AB, C_AC, C_AH, C_GQ, C_GK, C_GV, C_GR, C_LF, C_LB, C_TQ, C_TK, C_TV, C_MA, C_MB, C_MC) = [
    sum(SPLITS[:i]) for i in range(len(SPLITS))]

ADA_BLOCKS = 6
ADA = ADA_BLOCKS * KC
U_V, U_R, U_TV, U_LR, U_GLA = 0, 4, 8, 9, 10
U_K = U_GLA + 2 * HEADS
U_Q = U_K + KVH
U_CONV = U_Q + AH // 2
U_M = U_CONV + 3 * CONV_W // P
U_OUT = U_M + 6 * KC
UNITS = U_OUT + 8
RAW, SPL = 6, 3
EXU = 12
ONEHOTS = 8
ROUND_UNITS = NE // 2 * EXU

CONST = {}
_at = 0
for _name, _n in (("ident", P), ("rot", P), ("iota", P), ("strip", 4 * P), ("fwd", CHUNK),
                  ("bwd", CHUNK), ("prio", NG), ("base", NE), ("tokid", 2 * TILES), ("cst", 2), ("thr", 4)):
    CONST[_name] = (_at, _n)
    _at += _n
CONST_RES = _at
for _name, _n in (("cos", SAMPLE), ("sin", SAMPLE), ("scan", TOK), ("tri", P), ("ones", P)):
    CONST[_name] = (_at, _n)
    _at += _n
CONST_COLS = _at


def shape_constants():
    t = np.zeros((P, CONST_COLS), np.float32)

    def put(name, v):
        a, n = CONST[name]
        t[:, a:a + n] = v

    r = np.arange(P)
    put("ident", np.eye(P))
    rot = np.zeros((P, P))
    half = HD // 4
    for m in range(P):
        rot[(m + half) if m % (2 * half) < half else (m - half), m] = -1.0 if m % (2 * half) < half else 1.0
    put("rot", rot)
    put("tri", (r[:, None] < r[None, :]).astype(np.float32))
    put("ones", 1.0)
    put("iota", r[None, :])
    strip = np.zeros((P, 4 * P))
    strip[:, 0:P] = np.where(r[None, :] >= r[:, None], 0.0, -BIG)
    strip[:, 3 * P:] = np.where(r[None, :] <= r[:, None], 0.0, -BIG)
    put("strip", strip)
    s, c = (r % CHUNK)[:, None], np.arange(CHUNK)[None, :]
    put("fwd", s <= c)
    put("bwd", s >= c)
    put("prio", np.arange(NG, 0, -1)[None, :])
    put("base", (np.arange(NE) * SLOTS)[None, :])
    put("tokid", np.stack([np.broadcast_to(r[:, None], (P, TILES)), np.broadcast_to(P * np.arange(TILES), (P, TILES))], -1).reshape(P, 2 * TILES))
    put("cst", np.array([[EPS, 1.0]]))
    put("thr", (P * np.arange(1, 5))[None, :])
    inv = (10000.0 ** (-np.arange(half, dtype=np.float32) / half)).astype(np.float32)
    pos = np.arange(SAMPLE)
    d = r % HD
    where = np.where((d // (2 * half))[:, None] == 0, (pos // GRID_W)[None, :], (pos % GRID_W)[None, :]).astype(np.float32)
    ang = (where * inv[d % half][:, None]).astype(np.float32)
    put("cos", np.cos(ang.astype(np.float64)))
    put("sin", np.sin(ang.astype(np.float64)))
    put("scan", (np.arange(TOK) % CHUNK != 0)[None, :])
    return t


def ds(a, n):
    return bass.ds(a, n)


def build(nc, a, out_yp, out_ys, out_st, out_ck, out_cv):
    with ExitStack() as ctx:
        ctx.enter_context(nc.allow_non_contiguous_dma(reason="small vectors, one element per partition"))

        sems = []

        def sem(name):
            sems.append(ctx.enter_context(nc.semaphore(name)))
            return sems[-1]

        def gather_sem(name):
            return ctx.enter_context(nc.semaphore(name))

        s_start = ctx.enter_context(nc.semaphore("semaphores_set"))

        base = [(nc.sbuf_base + 63) // 64 * 64]

        def at(name, shape, dt, offset):
            return nc.alloc_sbuf_tensor_at(name, shape, dt, offset=offset)

        def room(nbytes):
            o = base[0]
            base[0] += (nbytes + 31) // 32 * 32
            return o

        def own(name, shape, dt=F32):
            return at(name, shape, dt, room((2 if dt == BF16 else 4) * int(np.prod(shape[1:]))))

        ROW = 4 * TOK
        o_ht = room(2 * KC * ROW)
        o_yhi = room(12 * ROW)
        o_ylo = room(12 * ROW)
        o_w = room(2 * KC * ROW)
        o_m = room(5 * ROW)
        raw = own("raw", [P, RAW, 1024])
        w_hi = own("w_hi", [P, SPL, 1024], F32R)
        w_lo = own("w_lo", [P, SPL, 1024], F32R)
        con = own("con", [P, CONST_RES])
        condT = own("condT", [P, KC, 2])
        conv_w = own("conv_w", [P, CONV_W // P, CONV_K])
        b_gate = own("b_gate", [P, 2, HEADS])
        sink = own("sink", [P, AH])
        w_rt = own("w_rt", [P, KC, NG + NE])
        b_rt = own("b_rt", [P, NG + NE])
        small = own("small", [P, 80])
        tri_b = own("tri_b", [P, 2 * P], BF16)
        tok_b = own("tok_b", [P, TILES, 2], BF16)
        info = own("info", [P, 2 * DEPTH + 2], I32)
        assert base[0] <= nc.sbuf_usable_end, (base[0], nc.sbuf_usable_end)

        def C(name):
            c, n = CONST[name]
            return con[:, c:c + n]

        ident, rot, iota, strip = (C(n) for n in ("ident", "rot", "iota", "strip"))
        tri_in = at("tri_in", [P, 2 * P], F32, o_ht)
        eps = C("cst")[:, 0:1]
        one = C("cst")[:, 1:2]
        hT_hi = at("hT_hi", [P, KC, TOK], F32R, o_ht)
        hT_lo = at("hT_lo", [P, KC, TOK], F32R, o_ht + KC * ROW)
        yT_hi = at("yT_hi", [P, 12, TOK], F32R, o_yhi)
        yT_lo = at("yT_lo", [P, 12, TOK], F32R, o_ylo)
        zT_hi = at("zT_hi", [P, KC, TOK], F32R, o_w)
        zT_lo = at("zT_lo", [P, KC, TOK], F32R, o_w + KC * ROW)
        x = at("x", [P, TILES, D], F32, o_yhi)
        gt = at("gt", [P, 2, D], F32, o_yhi + 8 * ROW)
        raw_more = at("raw_more", [P, EXU - RAW, 1024], F32, o_ylo)
        modA = at("modA", [P, 2, D], F32, o_ylo)
        modB = at("modB", [P, 2, D], F32, o_ylo + 8192)
        hbuf = at("hbuf", [P, 2, D], F32, o_ylo + 16384)
        junk = at("junk", [P, D], F32, o_ylo + 24576)
        ada_b = at("ada_b", [2, ADA_BLOCKS, D], F32, o_w)
        ada_g = at("ada_g", [2, 2, D], F32, o_w + 24576)
        mrow = at("mrow", [2, 2, D], F32, o_w + 32768)
        v_sb = at("v_sb", [P, TILES, HEADS * DV], F32, o_w)
        rg = at("rg", [P, TILES, HEADS * DV], F32, o_w + 4 * ROW)
        tv = at("tv", [P, TILES, P], F32, o_w + 8 * ROW)
        lrT = at("lrT", [2 * RANK, TOK], F32, o_w + 9 * ROW)
        qs = [at("qs0", [P, TOK], F32, o_w + 10 * ROW), at("qs1", [P, TOK], F32, o_yhi + 7 * ROW)]
        ks = [at("ks0", [P, TOK], F32, o_w + 11 * ROW), at("ks1", [P, TOK], F32, o_ylo + 7 * ROW)]
        zb = at("zb", [P, 2, TOK], F32, o_w + 12 * ROW)
        sp_ = at("sp_", [P, 2, TOK], F32, o_w + 14 * ROW)
        cb = at("cb", [P, 2, TOK], F32, o_yhi)
        E_ = at("E_", [P, 2, TOK], F32, o_yhi + 2 * ROW)
        En = at("En", [P, 2, TOK], F32, o_yhi + 8 * ROW)
        attm = at("attm", [P, 2, TILES, P], F32, o_yhi + 10 * ROW)
        NST = 12
        st = [at("st0", [P, NST, DV], F32, o_ylo), at("st1", [P, NST, DV], F32, o_ylo + 8 * ROW)]
        scanm = at("scanm", [P, TOK], F32, o_ylo + NST * DV * 4)
        yb = at("yb", [P, TILES, DV], F32, o_ylo + 8 * ROW + NST * DV * 4)
        osq = at("osq", [P, TILES, DV], F32, o_w + 15 * ROW)
        w_gate = at("w_gate", [2 * RANK, 2, HEADS * DK], F32, o_m)
        g_norm = at("g_norm", [P, HEADS * DV], F32, o_m + 4096)
        cossin = at("cossin", [P, 2, SAMPLE], F32, o_m + 6144)
        cv = at("cv", [P, KVH * HD], F32, o_m + 10240)
        ckd = at("ckd", [P, KVH, 2, HD], F32, o_m + 10752)
        s_sb = at("s_sb", [P, 2, TILES, 4 * P], F32, o_w + 20480 + 2560 - 23040)
        tv_end = o_w + 9 * ROW
        KCOLS = P + TOK
        kT = at("kT", [P, KVH, KCOLS], F32, tv_end)
        pT = at("pT", [P, 2, 4 * P], F32, tv_end + KVH * KCOLS * 4)
        qT = at("qT", [P, 2, TOK], F32, tv_end + KVH * KCOLS * 4 + 4096)
        qraw = at("qraw", [P, TOK], F32, tv_end + KVH * KCOLS * 4 + 4096 + 2 * ROW)
        assert tv_end + KVH * KCOLS * 4 + 4096 + 3 * ROW <= o_w + 16 * ROW
        rt1 = at("rt1", [P, SAMPLE], F32, o_yhi)
        rt2 = at("rt2", [P, SAMPLE], F32, o_yhi + 2048)
        kout = at("kout", [P, KVH, HD], F32, o_yhi + 4096)
        csb = at("csb", [P, TOK], F32, o_w)
        upad = at("upad", [P, TOK + 4], F32, o_w + ROW)
        yf = at("yf", [P, TOK], F32, o_w + 3 * ROW)
        sg = at("sg", [P, 3, TOK], F32, o_m)
        zacc = at("zacc", [P, TOK], F32, o_m + 3 * ROW)
        zt = at("zt", [P, TOK], F32, o_m + 4 * ROW)
        h2T = at("h2T", [P, 2, KC, P], F32, o_ht)
        xg = at("xg", [P, 2, D], F32, o_ht + 8192)
        yg = at("yg", [P, 2, 2, D], F32, o_ht + 16384)
        onehot = at("onehot", [P, ONEHOTS, TILES, SLOTS], BF16, o_ht + 16384)
        xT_hi = at("xT_hi", [P, 2, KC, SLOTS], F32R, o_w)
        xT_lo = at("xT_lo", [P, 2, KC, SLOTS], F32R, o_w + 8192)
        hidT_hi = at("hidT_hi", [P, 2, 2, SLOTS], F32R, o_w + 16384)
        hidT_lo = at("hidT_lo", [P, 2, 2, SLOTS], F32R, o_w + 18432)
        hid = at("hid", [P, 2, FE], F32, o_w + 20480)
        hg = at("hg", [P, 2, FE], F32, o_w + 22528)
        yo = at("yo", [P, 2, D], F32, o_w + 24576)
        _rt = [o_m]

        def rt(name, shape, dt=F32):
            o = _rt[0]
            _rt[0] += (4 * int(np.prod(shape[1:])) + 31) // 32 * 32
            assert _rt[0] <= o_m + 5 * ROW
            return at(name, shape, dt, o)

        lgt = rt("lgt", [P, TILES, NG + NE])
        gmax = rt("gmax", [P, TILES, 1])
        geq = rt("geq", [P, TILES, NG])
        gpk = rt("gpk", [P, TILES, NG])
        goh = rt("goh", [P, TILES, NG])
        gex = rt("gex", [P, TILES, NG])
        gsum = rt("gsum", [P, TILES, 1])
        pgrp = rt("pgrp", [P, TILES, 1])
        lsel4 = rt("lsel4", [P, TILES, EPG, NG])
        lsel = rt("lsel", [P, TILES, EPG])
        lsel2 = rt("lsel2", [P, TILES, EPG])
        m1 = rt("m1", [P, TILES, 1])
        m2 = rt("m2", [P, TILES, 1])
        oh1 = rt("oh1", [P, TILES, EPG])
        oh2 = rt("oh2", [P, TILES, EPG])
        e21 = rt("e21", [P, TILES, 1])
        wt1 = rt("wt1", [P, TILES, 1])
        wt2 = rt("wt2", [P, TILES, 1])
        E1 = rt("E1", [P, TILES, NE])
        E2 = rt("E2", [P, TILES, NE])
        Em = rt("Em", [P, TILES, NE], BF16)
        rkm = rt("rkm", [P, TILES, NE])
        rpos = rt("rpos", [P, TILES, NE])
        rtmp = rt("rtmp", [P, TILES, NE])
        posf = rt("posf", [P, 2, TILES])
        rsel = rt("rsel", [P, 2, TILES])
        bsel = rt("bsel", [P, 2, TILES])
        wsel = rt("wsel", [P, 2, TILES])
        inr = rt("inr", [P, 2, TILES])
        in2 = rt("in2", [P, 2, TILES])
        pos = rt("pos", [P, 2, TILES], I32)
        cnt = rt("cnt", [P, NE])
        cmax = rt("cmax", [P, 1])
        cge = rt("cge", [P, 4])
        cr = rt("cr", [P, 1])
        crf = rt("crf", [P, 2])
        sidx = rt("sidx", [P, NE], I32)
        stok = rt("stok", [P, NE])

        ss, sd, rstd = small[:, 0:5], small[:, 5:10], small[:, 10:15]
        g_ss, g_ln, g_rs = small[:, 15:20], small[:, 20:25], small[:, 25:30]
        a_mx, a_rd = small[:, 30:35], small[:, 35:40]
        a_nm, a_rs, a_es = ([small[:, 40 + 10 * i + 5 * j:45 + 10 * i + 5 * j] for j in range(2)] for i in range(3))

        ps = ctx.enter_context(nc.psum_tensor("ps", [P, 8, 512], F32))
        psf = ps[:, :, :].rearrange("p b c -> p (b c)")

        def pair(i, n=TOK, m=P):
            return psf[0:m, 1024 * i:1024 * i + n]

        def two(i, m=P):
            return ps[0:m, 2 * i:2 * i + 2, 0:HT]

        def in_two(ap):
            return ap.rearrange("p (a n) -> p a n", a=2)

        mod_d = nc.dram_tensor("mod_scratch", (ADA_BLOCKS, 2, D), F32, kind="Internal").ap()
        x_d = nc.dram_tensor("x_scratch", (TOK, D), F32, kind="Internal").ap()
        h2_d = nc.dram_tensor("h2_scratch", (TOK, D), F32, kind="Internal").ap()
        ye_d = nc.dram_tensor("expert_scratch", (NE * SLOTS, D), F32, kind="Internal").ap()

        s_held = {e.engine: sem(f"held_{i}") for i, e in enumerate((nc.sync, nc.gpsimd, nc.scalar, nc.vector, nc.tensor))}
        s_x0, s_c0 = sem("x_loaded_first"), sem("cond_loaded")
        s_out_tile = sem("projected_tile")
        s_const, s_init, s_cond = sem("consts_loaded"), sem("init_done"), sem("cond_ready")
        s_raw = [sem(f"raw_loaded{i}") for i in range(RAW)]
        s_rawx = [sem(f"raw_expert_loaded{i}") for i in range(EXU)]
        s_lay, s_lay2, s_lay3 = sem("layer_rows_loaded"), sem("layer_consts_loaded"), sem("gla_consts_loaded")
        s_ada, s_mrow = sem("ada_unit_used"), sem("mod_row_ready")
        s_mst = [sem(f"mod_row_stored{i}") for i in range(2)]
        s_modl, s_xsav, s_xload, s_gtl = sem("mod_loaded"), sem("x_saved"), sem("x_loaded"), sem("gate_loaded")
        s_split, s_used = sem("unit_split"), sem("unit_used")
        s_sd, s_h, s_hps, s_hhi, s_hT = sem("norm_root"), sem("h_ready"), sem("h_transposed"), sem("hT_hi_ready"), sem("hT_ready")
        s_v, s_r, s_tv, s_lr = sem("v_ready"), sem("r_silu_ready"), sem("tv_ready"), sem("lr_ready")
        s_gqk, s_gz, s_gzb, s_gsp, s_gcb, s_gE, s_gin = (sem(n) for n in (
            "gla_q_k_copied", "gla_gate_logits", "gla_gate_biased", "gla_softplus", "gla_decay_sums", "gla_exps", "gla_qk_decayed"))
        s_gkT, s_gke, s_gatt, s_gam, s_gds, s_gst, s_go, s_gsq, s_gss, s_grs, s_gy, s_gyT = (sem(n) for n in (
            "gla_kend_transposed", "gla_kend_copied", "gla_scores", "gla_scores_masked", "gla_state_steps", "gla_states",
            "gla_out", "gla_squares", "gla_square_sums", "gla_rstd", "gla_y", "gla_y_transposed"))
        s_st0 = [sem(f"state_loaded{i}") for i in range(2)]
        s_y = sem("y_ready")
        s_kraw, s_rot, s_rope, s_kt, s_kc, s_qc = (sem(n) for n in (
            "attn_raw_copied", "attn_rotated", "attn_roped", "attn_keys_turned", "attn_keys_copied", "attn_prompt_copied"))
        s_sc, s_sce, s_nm, s_ex, s_p, s_pt, s_pte, s_ao = (sem(n) for n in (
            "attn_scores", "attn_scores_taken", "attn_max", "attn_exp", "attn_probs", "attn_probs_turned", "attn_pT_copied", "attn_out"))
        s_cc, s_cu, s_cy = sem("conv_c_copied"), sem("conv_u_ready"), sem("conv_y_taken")
        s_sig, s_zm, s_z = sem("merge_gate_ready"), sem("merge_branch_taken"), sem("z_ready")
        s_h2s = [sem(f"h2_stored{i}") for i in range(2)]
        s_x1, s_h2T, s_rl, s_rlog = sem("x_mixed"), sem("h2T_copied"), sem("router_logits"), sem("router_taken")
        s_gx, s_gxe, s_rM, s_rk, s_info = sem("router_shifted"), sem("router_exps"), sem("routes_ready"), sem("ranks_ready"), sem("rounds_known")
        r_oh, r_idx, r_slots = sem("onehot_ready"), sem("slot_step_done"), sem("slots_ready")
        r_xg = [gather_sem(f"slot_rows_loaded{i}") for i in range(2)]
        r_hi, r_lo, r_used = sem("expert_unit_hi"), sem("expert_unit_lo"), sem("expert_unit_used")
        r_T, r_Thi, r_Tlo = sem("rows_transposed"), sem("xT_hi_ready"), sem("xT_ready")
        r_hg, r_hid, r_HT, r_hT = sem("expert_silu"), sem("expert_hidden"), sem("hidden_transposed"), sem("hidT_ready")
        r_yo = sem("expert_rows_copied")
        r_ys = [sem(f"expert_rows_stored{i}") for i in range(2)]
        s_yg = [gather_sem(f"token_rows_loaded{i}") for i in range(2)]
        r_added, s_done = sem("round_added"), sem("layer_done")
        s_fsd, s_fy = sem("final_root"), sem("final_ready")
        s_fg, s_out, s_sto = sem("final_gain_loaded"), sem("outputs_stored"), sem("states_stored")

        block = ctx.enter_context(nc.Block())

        w_in_u = a["w_in"].rearrange("l (k p) n -> p (l k) n", p=P)
        w_br_u = a["w_branch"].rearrange("l b (k p) n -> p (l b k) n", p=P)
        w_out_u = a["w_out"].rearrange("l (k p) n -> p (l k) n", p=P)
        w_ada_u = a["w_ada"].rearrange("l d n -> (l d) n")
        w_eg_u = a["w_exp_gate"].rearrange("l e (k p) f -> p (l e k) f", p=P)
        w_eu_u = a["w_exp_up"].rearrange("l e (k p) f -> p (l e k) f", p=P)
        w_ed_u = a["w_exp_down"].rearrange("l e (k p) n -> (l e k p) n", p=P)

        def u_cols(u):
            if u == U_LR:
                return KC * 2 * RANK
            if U_M <= u < U_OUT and (u - U_M) % 2 == 1:
                return 4 * P
            return 1024

        def set_semaphores(eng, i):
            for s in sems[i::5]:
                eng.sem_inc(s, SET)
            eng.drain()
            eng.sem_inc(s_start, 1)
            eng.wait_ge(s_start, 5)
            hold(eng)

        def raw_slot(j):
            return raw[:, j, :] if j < RAW else raw_more[:, j - RAW, :]

        def hold(eng):
            eng.sem_inc(s_held[eng.engine])

        def rounds_before(eng, l):
            hold(eng)
            return eng.value_load(info[0:1, ds(l * 2, 1)], min_val=0, max_val=5 * DEPTH)

        def rounds_now(eng, l):
            return eng.value_load(info[0:1, ds(l * 2 + 1, 1)], min_val=1, max_val=5)

        def span(b):
            if b == PT:
                return P, 2 * P
            return (P if b == 0 else 0), (3 * P if b == PT - 1 else 4 * P)

        def tiles_of(t):
            return (TILES + 1) // 2 if t % 2 == 0 else TILES // 2

        def h_tiles(b):
            return {3: (0, 1), 4: (2, 3), 5: (4,)}.get(b, ())

        def ktiles(b):
            lo_, hi_ = span(b)
            return (hi_ - lo_) // P

        @block.sync
        def _(sp):
            set_semaphores(sp, 0)
            sp.dma_start(con[:, :], a["table"][:, 0:CONST_RES]).then_inc(s_const, 16)
            tri_at = CONST["tri"][0]
            sp.dma_start(tri_in[:, :], a["table"][:, tri_at:tri_at + 2 * P]).then_inc(s_const, 16)
            sp.wait_ge(s_init, SET + 1)

            def feature_unit(l, u, col, width=P):
                slot = u % RAW
                dst = raw[:, slot, 0:KC * width].rearrange("p (k n) -> p k n", k=KC)
                return sp.dma_start(dst, w_in_u[:, ds(l * KC, KC), col:col + width])

            def token_unit(l, u, j, src, col):
                dst = raw[:, u % RAW, :].rearrange("p (k n) -> p k n", k=2)
                return sp.dma_start(dst, src[:, ds(l * KC + 2 * j, 2), col:col + 512])

            def free_slot(l, u):
                if u < RAW:
                    sp.wait_ge(s_ada, SET + l * ADA + ADA - RAW + u + 1)
                else:
                    sp.wait_ge(s_split, SET + l * UNITS + u - RAW + 1)

            with sp.Fori(0, DEPTH) as l:
                done = rounds_before(sp, l)
                sp.wait_ge(s_done, SET + l)
                for g in range(2):
                    sp.dma_start(ada_b[g:g + 1, :, :], a["b_ada"][ds(l, 1), :].rearrange("l (b d) -> l b d", d=D)).then_inc(s_lay, 16)
                    for i, n in enumerate(("norm1_g", "norm2_g")):
                        sp.dma_start(ada_g[g:g + 1, i, :], a[n][ds(l, 1), :]).then_inc(s_lay, 16)
                for u in range(ADA):
                    b, k = u // KC, u % KC
                    if u < RAW:
                        sp.wait_ge(r_lo, SET + done * ROUND_UNITS + u + 1)
                    else:
                        sp.wait_ge(s_ada, SET + l * ADA + u - RAW + 1)
                    sp.dma_start(raw[:, u % RAW, :], w_ada_u[ds(l * D + k * P, P), b * D:(b + 1) * D]).then_inc(s_raw[u % RAW], 16)
                    if u == 5:
                        sp.dma_start(g_norm[:, :], a["gla_norm_g"][ds(l, 1), :].broadcast_to([P, HEADS * DV])).then_inc(s_lay2, 16)
                        sp.dma_start(cossin[:, :, :], a["table"][:, CONST["cos"][0]:CONST["cos"][0] + 2 * SAMPLE]).then_inc(s_lay2, 16)
                        sp.dma_start(cv[:, :], a["cache_v"].rearrange("b l p k d -> p (b l) (k d)")[:, ds(l, 1), :]).then_inc(s_lay2, 16)
                        for kv in range(KVH):
                            for r in range(2):
                                sp.dma_start(ckd[:, kv, r, :], a["cache_k"].rearrange("b l p k d -> p (b l) (k d)")[
                                    :, ds(l, 1), kv * HD:(kv + 1) * HD]).then_inc(s_lay2, 16)
                        for d in range(2):
                            for o in range(2):
                                if o == d:
                                    sp.dma_start(w_gate[RANK * o:RANK * (o + 1), d, :], a["gla_w_gate"].rearrange(
                                        "l d r n -> (l d r) n")[ds(l * 2 * RANK + d * RANK, RANK), :]).then_inc(s_lay2, 16)
                                else:
                                    sp.dma_start(w_gate[RANK * o:RANK * (o + 1), d, :], a["zeros"][0:RANK, :]).then_inc(s_lay2, 16)
                            sp.dma_start(b_gate[:, d, :], a["gla_b_gate"].rearrange("l d (c p) -> p (l d) c", p=P)[
                                :, ds(l * 2 + d, 1), :]).then_inc(s_lay2, 16)
                        for j in range(CONV_K):
                            sp.dma_start(conv_w[:, :, j], a["conv_w"].rearrange("l j (c p) -> p (l j) c", p=P)[
                                :, ds(l * CONV_K + j, 1), :]).then_inc(s_lay2, 16)
                        sp.dma_start(sink[:, :], a["attn_sink"][ds(l, 1), :].broadcast_to([P, AH])).then_inc(s_lay2, 16)
                        sp.dma_start(w_rt[:, :, 0:NG], a["w_route_group"].rearrange("l (k p) n -> p (l k) n", p=P)[
                            :, ds(l * KC, KC), :]).then_inc(s_lay2, 16)
                        sp.dma_start(w_rt[:, :, NG:], a["w_route_expert"].rearrange("l (k p) n -> p (l k) n", p=P)[
                            :, ds(l * KC, KC), :]).then_inc(s_lay2, 16)
                        sp.dma_start(b_rt[:, 0:NG], a["b_route_group"][ds(l, 1), :].broadcast_to([P, NG])).then_inc(s_lay2, 16)
                        sp.dma_start(b_rt[:, NG:], a["b_route_expert"][ds(l, 1), :].broadcast_to([P, NE])).then_inc(s_lay2, 16)
                for u in range(U_M):
                    free_slot(l, u)
                    if u == U_CONV + 2:
                        hold(sp)
                    if u < U_TV:
                        ins = token_unit(l, u, u % 4, w_in_u, C_GV if u < U_R else C_GR)
                    elif u == U_TV:
                        ins = feature_unit(l, u, C_TV)
                    elif u == U_LR:
                        ins = feature_unit(l, u, C_LF, 2 * RANK)
                    elif u < U_K:
                        h, i = divmod(u - U_GLA, 2)
                        ins = feature_unit(l, u, (C_GQ, C_GK)[i] + h * P)
                    elif u < U_Q:
                        kv = u - U_K
                        dst = raw[:, u % RAW, :].rearrange("p (k r n) -> p k r n", k=KC, r=2)
                        for r in range(2):
                            ins = sp.dma_start(dst[:, :, r, :], w_in_u[:, ds(l * KC, KC), C_TK + kv * HD:C_TK + (kv + 1) * HD])
                            if r == 0:
                                ins.then_inc(s_raw[u % RAW], 16)
                    elif u < U_CONV:
                        ins = feature_unit(l, u, C_TQ + (u - U_Q) * P)
                    else:
                        f, i = divmod(u - U_CONV, 3)
                        ins = feature_unit(l, u, (C_AC, C_AH, C_AB)[i] + f * P)
                    ins.then_inc(s_raw[u % RAW], 16)
                hold(sp)
                with sp.Fori(0, KC) as n:
                    for i in range(3):
                        for j in range(2):
                            slot = 2 * i + j
                            sp.wait_ge(s_split, SET + l * UNITS + U_M - RAW + n * 6 + slot + 1)
                            if j == 0:
                                dst = raw[:, slot, :].rearrange("p (k n) -> p k n", k=KC)
                                sp.dma_start(dst, w_in_u[:, ds(l * KC, KC), ds(n * P + (C_MA, C_MB, C_MC)[i], P)]).then_inc(s_raw[slot], 16)
                            else:
                                dst = raw[:, slot, 0:512].rearrange("p (k n) -> p k n", k=4)
                                sp.dma_start(dst, w_br_u[:, ds(l * 12 + 4 * i, 4), ds(n * P, P)]).then_inc(s_raw[slot], 16)
                for u in range(U_OUT, UNITS):
                    free_slot(l, u)
                    token_unit(l, u, (u - U_OUT) % 4, w_out_u, 512 * ((u - U_OUT) // 4)).then_inc(s_raw[u % RAW], 16)
                sp.wait_ge(s_info, SET + l + 1)
                done = rounds_before(sp, l)
                now = rounds_now(sp, l)
                sp.wait_ge(s_split, SET + (l + 1) * UNITS)
                for i in range(2):
                    sp.wait_ge(s_h2s[i], SET + 16 * tiles_of(i) * (l + 1))
                sp.wait_ge(s_hps, SET + (l + 1) * 2 * TILES)
                hold(sp)
                with sp.Fori(0, now) as r:
                    hold(sp)
                    with sp.Fori(0, NE // 2) as ep:
                        for j in range(EXU):
                            g = (done + r) * ROUND_UNITS + ep * EXU
                            sp.wait_ge(r_lo, SET + g + j + 1)
                            i, q = divmod(j, EXU // 2)
                            if q < 4:
                                e = (l * NE + ep * 2 + i) * KC + 2 * q
                                dst = raw_slot(j).rearrange("p (k i f) -> p k i f", k=2, i=2)
                                sp.dma_start(dst[:, :, 0, :], w_eg_u[:, ds(e, 2), :]).then_inc(s_rawx[j], 16)
                                sp.dma_start(dst[:, :, 1, :], w_eu_u[:, ds(e, 2), :]).then_inc(s_rawx[j], 16)
                            else:
                                e = (l * NE + ep * 2 + i) * 2 + q - 4
                                sp.dma_start(raw_slot(j), w_ed_u[ds(e * P, P), :]).then_inc(s_rawx[j], 16)
            sp.wait_ge(s_done, SET + DEPTH)
            sp.dma_start(gt[:, 0, :], a["final_norm_g"].rearrange("(o d) -> o d", o=1).broadcast_to([P, D])).then_inc(s_fg, 16)
            for t in range(TILES):
                sp.wait_ge(s_fy, SET + t + 1)
                dst = out_ys[0, t * P:(t + 1) * P, :] if t < PT else out_yp[0]
                sp.dma_start(dst, x[:, t, :]).then_inc(s_out, 16)
            sp.wait_ge(s_out, SET + 16 * (TILES + 2 * DEPTH))
            sp.wait_ge(s_sto, SET + 16 * 2 * HEADS * DEPTH)

        def raw_value(l, u):
            slot = u % RAW
            fills = ADA // RAW
            per_layer = fills + sum(1 + (U_K <= v < U_Q) for v in range(UNITS) if v % RAW == slot)
            here = fills + sum(1 + (U_K <= v < U_Q) for v in range(u + 1) if v % RAW == slot)
            return l * (16 * per_layer) + 16 * here

        @block.gpsimd
        def _(pool):
            set_semaphores(pool, 1)
            nc.gpsimd.memset(info[:, :], 0).then_inc(s_init, 1)

            def split(l, u, value=None, cols=None):
                slot, ring = u % RAW, u % SPL
                n = u_cols(u) if cols is None else cols
                pool.wait_ge(s_raw[slot], SET + (raw_value(l, u) if value is None else value[0]))
                if value is None:
                    if u >= SPL:
                        pool.wait_ge(s_used, SET + l * UNITS + u - SPL + 1)
                else:
                    pool.wait_ge(s_used, SET + value[1])
                hold(pool)
                nc.gpsimd.tensor_copy(w_hi[:, ring, 0:n], raw[:, slot, 0:n])
                pool.drain()
                nc.gpsimd.tensor_tensor(w_lo[:, ring, 0:n], raw[:, slot, 0:n], w_hi[:, ring, 0:n].bitcast(F32),
                                        ALU.subtract).then_inc(s_split, 1)

            with pool.Fori(0, DEPTH) as l:
                done = None
                pool.wait_ge(s_done, SET + l)
                for u in range(U_M):
                    split(l, u)
                hold(pool)
                with pool.Fori(0, KC) as n:
                    for j in range(6):
                        split(l, U_M + j, (raw_value(l, U_M + j) + n * 16, l * UNITS + U_M + n * 6 + j - SPL + 1),
                              u_cols(U_M + j))
                for u in range(U_OUT, UNITS):
                    split(l, u)
                pool.wait_ge(s_info, SET + l + 1)
                done = rounds_before(pool, l)
                now = rounds_now(pool, l)
                for i in range(2):
                    pool.wait_ge(s_h2s[i], SET + 16 * tiles_of(i) * (l + 1))
                hold(pool)
                with pool.Fori(0, now) as r:
                    g = done + r
                    pool.wait_ge(r_slots, SET + 2 * g + 2)
                    for e in range(NE):
                        if e >= 2:
                            pool.wait_ge(r_T, SET + g * NE + e - 1)
                        else:
                            pool.wait_ge(r_T, SET + g * NE)
                        hold(pool)
                        nc.gpsimd.indirect_dma_start(
                            out=xg[:, e % 2, :], out_offset=None, in_=h2_d,
                            in_offset=bass.IndirectOffsetOnAxis(ap=sidx[:, e:e + 1].bitcast(U32), axis=0)).then_inc(r_xg[e % 2], 16)
                    for i in range(2):
                        pool.wait_ge(r_ys[i], SET + (g + 1) * (16 * NE // 2))
                    for t in range(TILES):
                        if t >= 2:
                            pool.wait_ge(r_added, SET + g * TILES + t - 1)
                        for k in range(2):
                            hold(pool)
                            nc.gpsimd.indirect_dma_start(
                                out=yg[:, t % 2, k, :], out_offset=None, in_=ye_d,
                                in_offset=bass.IndirectOffsetOnAxis(ap=pos[:, k, t:t + 1].bitcast(U32), axis=0)).then_inc(s_yg[t % 2], 16)

        @block.scalar
        def _(act):
            set_semaphores(act, 2)
            A = nc.scalar.activation
            for g, c in ((0, a["c"][0, :]), (1, a["c_ctx"])):
                for k in range(KC):
                    act.dma_start(condT[:, k, g:g + 1], c[k * P:(k + 1) * P].rearrange("(p o) -> p o", o=1)).then_inc(s_c0, 16)
            xs = a["x_sample"].rearrange("b (t p) d -> p (b t) d", p=P)
            act.dma_start(x[:, 0:PT, :], xs).then_inc(s_x0, 16)
            act.dma_start(x[:, PT, :], a["x_prompt"][0]).then_inc(s_x0, 16)
            act.wait_ge(s_const, SET + 32)
            act.wait_ge(s_c0, SET + 16 * 2 * KC)
            A(condT[:, :, :], condT[:, :, :], ACT.Silu).then_inc(s_cond, 1)

            def roots(l, which):
                for t in range(TILES):
                    act.drain()
                    if which == 1:
                        act.wait_ge(s_x1, SET + l * 2 * TILES + TILES + t + 1)
                    A(junk[:, :], x[:, t, :], ACT.Square, accum_out=ss[:, t:t + 1])
                act.drain()
                A(sd, ss, ACT.Sqrt, bias=eps, scale=1.0 / D).then_inc(s_sd, 1)

            act.wait_ge(s_x0, SET + 32)
            act.drain()
            with act.Fori(0, DEPTH) as l:
                act.wait_ge(s_done, SET + l)
                act.dma_start(x_d.rearrange("(t p) d -> p t d", p=P), x[:, :, :]).then_inc(s_xsav, 16)
                roots(l, 0)
                for b in range(ADA_BLOCKS):
                    act.wait_ge(s_mrow, SET + l * ADA_BLOCKS + b + 1)
                    act.dma_start(mod_d[b], mrow[:, b % 2, :]).then_inc(s_mst[b % 2], 16)
                    if b == 1:
                        act.wait_ge(s_mst[0], SET + 16 * (l * 3 + 1))
                        act.wait_ge(s_mst[1], SET + 16 * (l * 3 + 1))
                        for g in range(2):
                            act.dma_start(modB[:, g, :], mod_d[0, g:g + 1, :].broadcast_to([P, D])).then_inc(s_modl, 16)
                            act.dma_start(modA[:, g, :], mod_d[1, g:g + 1, :].broadcast_to([P, D])).then_inc(s_modl, 16)
                    for t in h_tiles(b):
                        act.wait_ge(s_hps, SET + l * 2 * TILES + t + 1)
                        nc.scalar.copy(hT_hi[:, :, t * P:(t + 1) * P], pair(2 + t % 2, 1024).rearrange("p (k n) -> p k n", k=KC)).then_inc(s_hhi, 1)
                for i in range(2):
                    act.wait_ge(s_mst[i], SET + 16 * 3 * (l + 1))
                act.wait_ge(s_used, SET + l * UNITS + U_V + 4)
                for t in range(TILES):
                    nc.scalar.copy(v_sb[:, t, :], ps[:, t, :]).then_inc(s_v, 1)
                act.wait_ge(s_used, SET + l * UNITS + U_R + 4)
                for t in range(TILES):
                    A(rg[:, t, :], ps[:, (5 + t) % 8, :], ACT.Silu).then_inc(s_r, 1)
                act.wait_ge(s_used, SET + l * UNITS + U_TV + 1)
                nc.scalar.copy(tv[:, :, :], pair(1).rearrange("p (t n) -> p t n", n=P)).then_inc(s_tv, 1)
                act.wait_ge(s_used, SET + l * UNITS + U_LR + 1)
                nc.scalar.copy(in_two(lrT[:, :]), two(2, 2 * RANK)).then_inc(s_lr, 1)
                act.wait_ge(s_tv, SET + l + 1)
                act.dma_start(out_cv[0, ds(l, 1)].rearrange("l p k d -> p (l k d)"), tv[:, PT, :]).then_inc(s_out, 16)
                act.wait_ge(s_hT, SET + (l + 1) * TILES)
                act.wait_ge(s_xsav, SET + 16 * (l + 1))
                act.dma_start(scanm[:, :], a["table"][:, CONST["scan"][0]:CONST["scan"][0] + TOK]).then_inc(s_lay3, 16)

                def q_k(h):
                    act.wait_ge(s_used, SET + l * UNITS + U_GLA + 2 * h + 1)
                    act.wait_ge(s_gin, SET + 2 * (l * HEADS + max(h - 1, 0)))
                    A(in_two(qs[h % 2][:, :]), two(3), ACT.Copy, scale=float(DK) ** -0.5).then_inc(s_gqk, 1)
                    act.wait_ge(s_used, SET + l * UNITS + U_GLA + 2 * h + 2)
                    nc.scalar.copy(in_two(ks[h % 2][:, :]), two(2)).then_inc(s_gqk, 1)

                for h in range(HEADS):
                    for d in range(2):
                        act.wait_ge(s_go, SET + l * HEADS + h)
                        act.wait_ge(s_sto, SET + 16 * (l * 2 * HEADS + 2 * h))
                        act.dma_start(st[d][:, 0, :], a["state_gla"].rearrange("b l d h k v -> k (b l d h) v")[
                            :, ds(l * 2 * HEADS + d * HEADS + h, 1), :]).then_inc(s_st0[d], 16)
                    hh = l * HEADS + h
                    for d in range(2):
                        act.wait_ge(s_gzb, SET + hh * 2 + d + 1)
                        A(sp_[:, d, :], zb[:, d, :], ACT.Abs)
                        act.drain()
                        A(sp_[:, d, :], sp_[:, d, :], ACT.Exp, scale=-1.0)
                        act.drain()
                        A(sp_[:, d, :], sp_[:, d, :], ACT.Ln, bias=one).then_inc(s_gsp, 1)
                    for d in range(2):
                        act.wait_ge(s_gcb, SET + hh * 2 + d + 1)
                        A(E_[:, d, :], cb[:, d, :], ACT.Exp, scale=1.0 / TAU)
                        A(En[:, d, :], cb[:, d, :], ACT.Exp, scale=-1.0 / TAU).then_inc(s_gE, 1)
                    q_k(h)
                    for d in range(2):
                        act.wait_ge(s_gkT, SET + hh * 2 + d + 1)
                        nc.scalar.copy(zb[:, d, :], pair(2 + d)).then_inc(s_gke, 1)
                    for d in range(2):
                        act.wait_ge(s_gst, SET + hh * 2 + d + 1)
                        act.dma_start(out_st[0, ds(l, 1), d, h].rearrange("l k v -> k (l v)"), st[d][:, SCH + 3, :]).then_inc(s_sto, 16)
                    act.wait_ge(s_go, SET + hh + 1)
                    A(osq[:, :, :], pair(3).rearrange("p (t n) -> p t n", n=DV), ACT.Square).then_inc(s_gsq, 1)
                    act.wait_ge(s_gss, SET + hh + 1)
                    A(g_ln, g_ss, ACT.Ln, bias=eps, scale=1.0 / DV)
                    act.drain()
                    A(g_rs, g_ln, ACT.Exp, scale=-0.5).then_inc(s_grs, 1)
                for kv in range(KVH):
                    j = l * (KVH + 4) + kv
                    act.drain()
                    act.wait_ge(s_y, SET + l * 12 + HEADS)
                    act.wait_ge(s_used, SET + l * UNITS + U_K + kv + 1)
                    act.wait_ge(s_rope, SET + j)
                    act.wait_ge(s_kt, SET + l * KVH + kv)
                    nc.scalar.copy(in_two(qraw[:, :]), two(0)).then_inc(s_kraw, 1)
                    act.drain()
                    nc.scalar.copy(kT[:, kv, P + SAMPLE:], qraw[:, SAMPLE:])
                    act.wait_ge(s_kt, SET + l * KVH + kv + 1)
                    nc.scalar.copy(kT[:, kv, 0:P], ps[:, 5, 0:P])
                    nc.scalar.copy(kout[:, kv, :], ps[:, 5, P:P + HD]).then_inc(s_kc, 1)
                act.wait_ge(s_kc, SET + (l + 1) * KVH)
                act.dma_start(out_ck[0, ds(l, 1)].rearrange("l p k d -> p (l k d)"), kout[:, :, :]).then_inc(s_out, 16)

                def q_chunk(c):
                    j = l * (KVH + 4) + KVH + c
                    act.drain()
                    act.wait_ge(s_used, SET + l * UNITS + U_Q + c + 1)
                    act.wait_ge(s_rope, SET + j)
                    nc.scalar.copy(in_two(qraw[:, :]), two(0)).then_inc(s_kraw, 1)
                    act.drain()
                    if c >= 2:
                        act.wait_ge(s_sc, SET + (l * AH + 2 * (c - 1)) * TILES)
                    nc.scalar.copy(qT[:, c % 2, SAMPLE:], qraw[:, SAMPLE:]).then_inc(s_qc, 1)

                def exps(hd):
                    i, b_ = hd % 2, l * AH + hd
                    act.wait_ge(s_nm, SET + b_ + 1)
                    for b in range(TILES):
                        lo_, hi_ = span(b)
                        A(s_sb[:, i, b, lo_:hi_], s_sb[:, i, b, lo_:hi_], ACT.Exp, bias=a_nm[i][:, b:b + 1], accum_out=a_rs[i][:, b:b + 1])
                    A(a_es[i], a_nm[i], ACT.Exp, bias=sink[:, hd:hd + 1]).then_inc(s_ex, 1)

                def probs_copy(hd):
                    b_ = l * AH + hd
                    for b in range(TILES):
                        n = ktiles(b) * P
                        act.drain()
                        act.wait_ge(s_pt, SET + b_ * TILES + b + 1)
                        nc.scalar.copy(pT[:, b % 2, 0:n], ps[:, 2 + b % 2, 0:n]).then_inc(s_pte, 1)

                q_chunk(0)
                exps(0)
                for hd in range(AH):
                    if hd % 2 == 0 and hd < AH - 2:
                        q_chunk(hd // 2 + 1)
                    probs_copy(hd)
                    if hd + 1 < AH:
                        exps(hd + 1)
                for f in range(4):
                    act.drain()
                    act.wait_ge(s_y, SET + l * 12 + HEADS + 4)
                    act.wait_ge(s_used, SET + l * UNITS + U_CONV + 3 * f + 1)
                    act.wait_ge(s_cu, SET + l * 4 + f)
                    nc.scalar.copy(in_two(csb[:, :]), two((3 * f) % 4)).then_inc(s_cc, 1)
                hold(act)
                with act.Fori(0, KC) as n:
                    for i in range(3):
                        act.drain()
                        act.wait_ge(s_used, SET + l * UNITS + U_M + n * 6 + 2 * i + 1)
                        if i == 0:
                            act.wait_ge(s_y, SET + (l + 1) * 12)
                        act.wait_ge(s_zm, SET + (l * KC + n) * 3)
                        A(in_two(sg[:, i, :]), two((2 * i) % 4), ACT.Sigmoid).then_inc(s_sig, 1)
                act.wait_ge(s_used, SET + l * UNITS + U_OUT)
                act.dma_start(x[:, :, :], x_d.rearrange("(t p) d -> p t d", p=P)).then_inc(s_xload, 16)
                for g in range(2):
                    act.dma_start(gt[:, g, :], mod_d[2, g:g + 1, :].broadcast_to([P, D])).then_inc(s_gtl, 16)
                    act.dma_start(modB[:, g, :], mod_d[3, g:g + 1, :].broadcast_to([P, D])).then_inc(s_modl, 16)
                    act.dma_start(modA[:, g, :], mod_d[4, g:g + 1, :].broadcast_to([P, D])).then_inc(s_modl, 16)
                roots(l, 1)
                for g in range(2):
                    act.dma_start(gt[:, g, :], mod_d[5, g:g + 1, :].broadcast_to([P, D])).then_inc(s_gtl, 16)
                for t in range(TILES):
                    act.wait_ge(s_h, SET + (l * 2 + 1) * TILES + t + 1)
                    act.dma_start(h2_d[t * P:(t + 1) * P, :], hbuf[:, t % 2, :]).then_inc(s_h2s[t % 2], 16)
                    act.drain()
                    act.wait_ge(s_hps, SET + (l * 2 + 1) * TILES + t + 1)
                    if t >= 2:
                        act.wait_ge(s_rl, SET + l * TILES + t - 1)
                    nc.scalar.copy(h2T[:, t % 2, :, :], pair(t % 2, 1024).rearrange("p (k n) -> p k n", k=KC)).then_inc(s_h2T, 1)
                act.wait_ge(s_gx, SET + l + 1)
                A(gex[:, :, :], gex[:, :, :], ACT.Exp)
                A(e21[:, :, :], e21[:, :, :], ACT.Exp).then_inc(s_gxe, 1)
                act.wait_ge(s_info, SET + l + 1)
                done = rounds_before(act, l)
                now = rounds_now(act, l)
                hold(act)
                with act.Fori(0, now) as r:
                    act.wait_ge(r_added, SET + (done + r) * TILES)

                    def expert_pair(ep, first, last):
                        g = (done + r) * (NE // 2) + ep

                        def half(j):
                            fill = 32 if j % 6 < 4 else 16
                            act.wait_ge(s_rawx[j], SET + g * fill + fill)
                            act.wait_ge(r_used, SET + g * EXU + j + 1)
                            nc.scalar.copy(w_hi[:, j % SPL, :], raw_slot(j)).then_inc(r_hi, 1)

                        def turned_rows(i):
                            act.wait_ge(r_T, SET + g * 2 + i + 1)
                            nc.scalar.copy(xT_hi[:, i % 2, :, :], pair(0, 1024).rearrange("p (k n) -> p k n", k=KC)).then_inc(r_Thi, 1)

                        def result(i):
                            act.wait_ge(r_used, SET + SPL + g * EXU + 6 * (i + 1))
                            act.wait_ge(r_ys[i % 2], SET + (g + i // 2) * 16)
                            nc.scalar.copy(yo[:, i % 2, :], pair(1, 1024)).then_inc(r_yo, 1)
                            act.wait_ge(r_yo, SET + g * 2 + i + 1)
                            act.dma_start(ye_d[ds((ep * 2 + i) * SLOTS, SLOTS), :], yo[:, i % 2, :]).then_inc(r_ys[i % 2], 16)

                        for i in range(2):
                            if first and i == 0:
                                turned_rows(0)
                            for q in range(3):
                                half(6 * i + q)
                            if not (first and i == 0):
                                result(i - 1)
                            for q in range(3, 6):
                                half(6 * i + q)
                            act.wait_ge(r_used, SET + SPL + g * EXU + 6 * i + 4)
                            A(hg[:, i, :], ps[:, 4 + i, 0:FE], ACT.Silu).then_inc(r_hg, 1)
                            if not (last and i == 1):
                                turned_rows(i + 1)
                        if last:
                            result(1)

                    expert_pair(0, True, False)
                    hold(act)
                    with act.Fori(1, NE // 2 - 1) as ep:
                        expert_pair(ep, False, False)
                    expert_pair(NE // 2 - 1, False, True)
            for t in range(TILES):
                act.drain()
                act.wait_ge(s_done, SET + DEPTH)
                A(junk[:, :], x[:, t, :], ACT.Square, accum_out=ss[:, t:t + 1])
            act.drain()
            A(sd, ss, ACT.Sqrt, bias=eps, scale=1.0 / D).then_inc(s_fsd, 1)

        @block.vector
        def _(dve):
            dve.sem_inc(r_lo, EXU)
            set_semaphores(dve, 3)
            V = nc.vector
            gl = lambda t: 0 if t < PT else 1

            def norm_tile(l, which, t, k):
                if t >= 2:
                    dve.wait_ge(s_hps, SET + (l * 2 + which) * TILES + t - 1)
                    if which:
                        dve.wait_ge(s_h2s[t % 2], SET + 16 * (l * tiles_of(t) + t // 2))
                V.scalar_tensor_tensor(hbuf[:, t % 2, :], x[:, t, :], rstd[:, t:t + 1], modA[:, gl(t), :], ALU.mult, ALU.mult)
                dve.drain()
                V.tensor_tensor(hbuf[:, t % 2, :], hbuf[:, t % 2, :], modB[:, gl(t), :], ALU.add).then_inc(s_h, 1)

            dve.wait_ge(s_const, SET + 32)
            dve.wait_ge(s_x0, SET + 32)
            V.tensor_copy(tri_b[:, :], tri_in[:, :])
            V.tensor_copy(tok_b[:, :, :], C("tokid").rearrange("p (t i) -> p t i", i=2))
            with dve.Fori(0, DEPTH) as l:

                def hT_low(t):
                    dve.wait_ge(s_hhi, SET + l * TILES + t + 1)
                    V.tensor_tensor(hT_lo[:, :, t * P:(t + 1) * P], pair(2 + t % 2, 1024).rearrange("p (k n) -> p k n", k=KC),
                                    hT_hi[:, :, t * P:(t + 1) * P].bitcast(F32), ALU.subtract).then_inc(s_hT, 1)

                for b in range(ADA_BLOCKS):
                    dve.drain()
                    dve.wait_ge(s_lay, SET + (l + 1) * 16 * 6)
                    dve.wait_ge(s_ada, SET + l * ADA + KC * (b + 1))
                    dve.wait_ge(s_mst[b % 2], SET + 16 * (l * 3 + b // 2))
                    ins = V.tensor_tensor(mrow[:, b % 2, :], pair(b % 2, 1024, 2), ada_b[:, b, :], ALU.add)
                    if b % 3 == 1:
                        dve.drain()
                        ins = V.scalar_tensor_tensor(mrow[:, b % 2, :], mrow[:, b % 2, :], 1.0, ada_g[:, b // 3, :], ALU.add, ALU.mult)
                    ins.then_inc(s_mrow, 1)
                    if b == 2:
                        dve.wait_ge(s_sd, SET + l * 2 + 1)
                        V.reciprocal(rstd, sd)
                        dve.drain()
                        dve.wait_ge(s_modl, SET + 16 * 8 * l + 64)
                        norm_tile(l, 0, 0, 0)
                        norm_tile(l, 0, 1, 0)
                    for t in h_tiles(b):
                        hT_low(t)
                        if t + 2 < TILES:
                            norm_tile(l, 0, t + 2, 0)
                dve.wait_ge(s_lay2, SET + (l + 1) * 16 * 21)
                for t in range(TILES):
                    dve.wait_ge(s_r, SET + l * TILES + t + 1)
                    V.tensor_tensor(rg[:, t, :], rg[:, t, :], g_norm[:, :], ALU.mult)
                dve.drain()
                dve.wait_ge(s_lay3, SET + (l + 1) * 16)
                dve.wait_ge(s_xsav, SET + 16 * (l + 1))
                for d in range(2):
                    V.memset(st[d][:, SCH + 1, :], 0.0)
                    V.memset(attm[:, d, :, :], 0.0)

                def biased(h, d):
                    dve.drain()
                    dve.wait_ge(s_gz, SET + (l * HEADS + h) * 2 + d + 1)
                    V.tensor_scalar(in_two(zb[:, d, :]), two(d), b_gate[:, d, h:h + 1], None, ALU.add).then_inc(s_gzb, 1)

                biased(0, 0)
                biased(0, 1)
                for h in range(HEADS):
                    hh = l * HEADS + h
                    for d in range(2):
                        dve.wait_ge(s_gsp, SET + hh * 2 + d + 1)
                        V.scalar_tensor_tensor(zb[:, d, :], zb[:, d, :], 0.0, sp_[:, d, :], ALU.min, ALU.subtract)
                        dve.drain()
                        if d == 0:
                            V.tensor_tensor_scan(cb[:, d, :], scanm[:, :], zb[:, d, :], 0.0, ALU.mult, ALU.add).then_inc(s_gcb, 1)
                        else:
                            V.tensor_tensor_scan(cb[:, d, ::-1], scanm[:, :], zb[:, d, ::-1], 0.0, ALU.mult, ALU.add).then_inc(s_gcb, 1)
                    for d in range(2):
                        dve.wait_ge(s_gqk, SET + hh * 2 + 2)
                        dve.wait_ge(s_gE, SET + hh * 2 + d + 1)
                        V.tensor_tensor(cb[:, d, :], qs[h % 2][:, :], E_[:, d, :], ALU.mult)
                        V.tensor_tensor(En[:, d, :], ks[h % 2][:, :], En[:, d, :], ALU.mult)
                        dve.drain()
                        last = CHUNK - 1 if d == 0 else 0
                        ev = E_[:, d, :].rearrange("p (n c) -> p n c", c=CHUNK)[:, :, last:last + 1].broadcast_to([P, NCH, CHUNK])
                        V.tensor_tensor(sp_[:, d, :].rearrange("p (n c) -> p n c", c=CHUNK), En[:, d, :].rearrange("p (n c) -> p n c", c=CHUNK),
                                        ev, ALU.mult).then_inc(s_gin, 1)
                    for d in range(2):
                        dve.wait_ge(s_gatt, SET + hh * 2 + d + 1)
                        hold(dve)
                        for o in (0, CHUNK):
                            c = slice(o, o + CHUNK)
                            m = C(("fwd", "bwd")[d])[c, :].bitcast(I32).rearrange("p (o c) -> p o c", o=1).broadcast_to([CHUNK, TILES, CHUNK])
                            ins = V.copy_predicated(attm[c, d, :, c], m, pair(d)[c, :].rearrange("p (t c) -> p t c", c=P)[:, :, c])
                        ins.then_inc(s_gam, 1)
                    for d in range(2):
                        dve.drain()
                        dve.wait_ge(s_gds, SET + hh * 4 + 2 * d + 2)
                        dve.wait_ge(s_st0[d], SET + 16 * (hh + 1))
                        dst_ = psf[:, 1536 * d:1536 * d + NCH * DV].rearrange("p (n v) -> p n v", v=DV)
                        steps = [(i, i if d == 0 else SCH - 1 - i) for i in range(SCH - 1)]
                        steps += [(SCH + 1 + i, SCH + i if d == 0 else NCH - 1 - i) for i in range(2)]
                        for q, (i, n) in enumerate(sorted(steps, key=lambda s: s[0] % (SCH + 1))):
                            if q:
                                dve.drain()
                            e_col = n * CHUNK + (CHUNK - 1 if d == 0 else 0)
                            ins = V.scalar_tensor_tensor(st[d][:, i + 1, :], st[d][:, i, :], E_[:, d, e_col:e_col + 1], dst_[:, n, :], ALU.mult, ALU.add)
                        ins.then_inc(s_gst, 1)
                    dve.wait_ge(s_gsq, SET + hh + 1)
                    V.tensor_reduce(g_ss, osq[:, :, :], AX.X, ALU.add).then_inc(s_gss, 1)
                    if h + 1 < HEADS:
                        biased(h + 1, 0)
                    dve.wait_ge(s_grs, SET + hh + 1)
                    for t in range(TILES):
                        ins = V.scalar_tensor_tensor(yb[:, t, :], pair(3)[:, t * DV:(t + 1) * DV], g_rs[:, t:t + 1], rg[:, t, h * DV:(h + 1) * DV],
                                                     ALU.mult, ALU.mult)
                    ins.then_inc(s_gy, 1)
                    if h + 1 < HEADS:
                        biased(h + 1, 1)
                    dve.wait_ge(s_gyT, SET + hh + 1)
                    V.tensor_copy(yT_hi[:, 4 + h, :], pair(2))
                    dve.drain()
                    V.tensor_tensor(yT_lo[:, 4 + h, :], pair(2), yT_hi[:, 4 + h, :].bitcast(F32), ALU.subtract).then_inc(s_y, 1)

                dve.drain()
                for i in range(2):
                    V.memset(s_sb[:, i, 0, 0:P], -BIG)
                    V.memset(s_sb[:, i, PT - 1, 3 * P:], -BIG)
                    V.memset(s_sb[:, i, PT, 0:P], -BIG)
                    V.memset(s_sb[:, i, PT, 2 * P:], -BIG)

                def rope(j, dst):
                    dve.drain()
                    dve.wait_ge(s_kraw, SET + l * (KVH + 4) + j + 1)
                    V.tensor_tensor(rt1[:, :], qraw[:, 0:SAMPLE], cossin[:, 0, :], ALU.mult)
                    dve.wait_ge(s_rot, SET + l * (KVH + 4) + j + 1)
                    V.tensor_tensor(rt2[:, :], ps[:, 4, :], cossin[:, 1, :], ALU.mult)
                    dve.drain()
                    V.tensor_tensor(dst, rt1[:, :], rt2[:, :], ALU.add).then_inc(s_rope, 1)

                rope(0, kT[:, 0, P:P + SAMPLE])
                rope(1, kT[:, 1, P:P + SAMPLE])
                rope(2, qT[:, 0, 0:SAMPLE])

                def scores(hd):
                    i, b_ = hd % 2, l * AH + hd
                    if hd >= 2:
                        dve.wait_ge(s_pt, SET + (b_ - 1) * TILES)
                    for b in range(TILES):
                        lo_, hi_ = span(b)
                        dve.wait_ge(s_sc, SET + b_ * TILES + b + 1)
                        V.scalar_tensor_tensor(s_sb[:, i, b, lo_:hi_], ps[:, 5 + b % 2, lo_:hi_], float(HD) ** -0.5, strip[:, lo_:hi_],
                                               ALU.mult, ALU.add).then_inc(s_sce, 1)

                def maxima(hd):
                    i = hd % 2
                    dve.drain()
                    V.tensor_reduce(a_mx, s_sb[:, i, :, :], AX.X, ALU.max)
                    dve.drain()
                    V.tensor_scalar(a_nm[i], a_mx, sink[:, hd:hd + 1], -1.0, ALU.max, ALU.mult).then_inc(s_nm, 1)

                def normalise(hd):
                    i = hd % 2
                    dve.wait_ge(s_ex, SET + l * AH + hd + 1)
                    V.tensor_tensor(a_rd, a_rs[i], a_es[i], ALU.add)
                    dve.drain()
                    V.reciprocal(a_rd, a_rd)
                    dve.drain()
                    for b in range(TILES):
                        lo_, hi_ = span(b)
                        ins = V.tensor_scalar(s_sb[:, i, b, lo_:hi_], s_sb[:, i, b, lo_:hi_], a_rd[:, b:b + 1], None, ALU.mult)
                    ins.then_inc(s_p, 1)

                def take_y(c):
                    dve.wait_ge(s_ao, SET + l * 4 + c + 1)
                    dve.wait_ge(s_sto, SET + 16 * 2 * HEADS * (l + 1))
                    V.tensor_copy(yT_hi[:, 8 + c, 0:SAMPLE], ps[:, 7, :])
                    V.tensor_copy(yT_hi[:, 8 + c, SAMPLE:], ps[:, 1, 384:512])
                    dve.drain()
                    V.tensor_tensor(yT_lo[:, 8 + c, 0:SAMPLE], ps[:, 7, :], yT_hi[:, 8 + c, 0:SAMPLE].bitcast(F32), ALU.subtract)
                    V.tensor_tensor(yT_lo[:, 8 + c, SAMPLE:], ps[:, 1, 384:512], yT_hi[:, 8 + c, SAMPLE:].bitcast(F32), ALU.subtract).then_inc(s_y, 1)

                scores(0)
                maxima(0)
                for hd in range(AH):
                    if hd + 1 < AH:
                        scores(hd + 1)
                    if hd % 2 == 0 and hd >= 2:
                        take_y(hd // 2 - 1)
                    normalise(hd)
                    if hd + 1 < AH:
                        maxima(hd + 1)
                    if hd % 2 == 0 and hd < AH - 2:
                        rope(3 + hd // 2, qT[:, (hd // 2 + 1) % 2, 0:SAMPLE])
                take_y(AH // 2 - 1)
                dve.drain()
                for z in (0, SAMPLE + 1, SAMPLE + 2, TOK + 3):
                    V.memset(upad[:, z:z + 1], 0.0)
                for f in range(4):
                    dve.drain()
                    dve.wait_ge(s_cc, SET + l * 4 + f + 1)
                    dve.wait_ge(s_used, SET + l * UNITS + U_CONV + 3 * f + 2)
                    hp = two((3 * f + 1) % 4)
                    V.tensor_tensor(upad[:, 1:HT + 1], hp[:, 0, :], csb[:, 0:HT], ALU.mult)
                    V.tensor_tensor(upad[:, HT + 1:SAMPLE + 1], hp[:, 1, 0:SAMPLE - HT], csb[:, HT:SAMPLE], ALU.mult)
                    V.tensor_tensor(upad[:, SAMPLE + 3:TOK + 3], hp[:, 1, SAMPLE - HT:], csb[:, SAMPLE:], ALU.mult).then_inc(s_cu, 1)
                    dve.drain()
                    for j in range(CONV_K):
                        for a0, u0, n in ((0, 0, SAMPLE), (SAMPLE, SAMPLE + 2, PROMPT)):
                            if j == 0:
                                V.tensor_scalar(yf[:, a0:a0 + n], upad[:, u0:u0 + n], conv_w[:, f, 0:1], None, ALU.mult)
                            else:
                                V.scalar_tensor_tensor(yf[:, a0:a0 + n], upad[:, u0 + j:u0 + j + n], conv_w[:, f, j:j + 1], yf[:, a0:a0 + n],
                                                       ALU.mult, ALU.add)
                        dve.drain()
                    dve.wait_ge(s_used, SET + l * UNITS + U_CONV + 3 * f + 3)
                    dve.wait_ge(s_out, SET + 32 * (l + 1))
                    V.tensor_tensor(in_two(yf[:, :]), in_two(yf[:, :]), two((3 * f + 2) % 4), ALU.mult).then_inc(s_cy, 1)
                    dve.drain()
                    V.tensor_copy(yT_hi[:, f, :], yf[:, :])
                    dve.drain()
                    V.tensor_tensor(yT_lo[:, f, :], yf[:, :], yT_hi[:, f, :].bitcast(F32), ALU.subtract).then_inc(s_y, 1)
                hold(dve)
                with dve.Fori(0, KC) as n:
                    for i in range(3):
                        g = (l * KC + n) * 3
                        dve.drain()
                        dve.wait_ge(s_sig, SET + g + i + 1)
                        dve.wait_ge(s_used, SET + l * UNITS + U_M + n * 6 + 2 * i + 2)
                        V.tensor_tensor(in_two((zacc if i == 0 else zt)[:, :]), in_two(sg[:, i, :]), two((2 * i + 1) % 4), ALU.mult).then_inc(s_zm, 1)
                        dve.drain()
                        if i:
                            V.tensor_tensor(zacc[:, :], zacc[:, :], zt[:, :], ALU.add)
                            dve.drain()
                    V.tensor_copy(zT_hi[:, ds(n, 1), :], zacc[:, :].rearrange("p (o c) -> p o c", o=1))
                    dve.drain()
                    V.tensor_tensor(zT_lo[:, ds(n, 1), :], zacc[:, :].rearrange("p (o c) -> p o c", o=1),
                                    zT_hi[:, ds(n, 1), :].bitcast(F32), ALU.subtract).then_inc(s_z, 1)
                for hf in range(2):
                    for t in range(TILES):
                        c0 = 512 * hf
                        dve.drain()
                        dve.wait_ge(s_xload, SET + 16 * (l + 1))
                        dve.wait_ge(s_gtl, SET + 64 * l + 32)
                        if t < PT:
                            dve.wait_ge(s_out_tile, SET + (l * 2 + hf) * PT + t + 1)
                        else:
                            dve.wait_ge(s_used, SET + l * UNITS + U_OUT + 4 * (hf + 1))
                        V.tensor_tensor(hbuf[:, t % 2, 0:512], ps[:, (5 * hf + t) % 8, :], gt[:, gl(t), c0:c0 + 512], ALU.mult)
                        dve.drain()
                        V.tensor_tensor(x[:, t, c0:c0 + 512], x[:, t, c0:c0 + 512], hbuf[:, t % 2, 0:512], ALU.add).then_inc(s_x1, 1)
                dve.wait_ge(s_sd, SET + l * 2 + 2)
                V.reciprocal(rstd, sd)
                dve.drain()
                dve.wait_ge(s_modl, SET + 16 * 8 * (l + 1))
                for t in range(TILES):
                    norm_tile(l, 1, t, 0)
                dve.wait_ge(s_rl, SET + (l + 1) * TILES)
                V.tensor_tensor(lgt[:, :, :], ps[:, 7, 0:TILES * 32].rearrange("p (t n) -> p t n", n=32)[:, :, 0:NG + NE],
                                b_rt[:, :].rearrange("p (o n) -> p o n", o=1).broadcast_to([P, TILES, NG + NE]), ALU.add).then_inc(s_rlog, 1)
                dve.drain()
                lg = lgt[:, :, 0:NG]

                def bc(ap, n):
                    return ap.broadcast_to([P, TILES, n])

                def tt(o, i0, i1, op):
                    V.tensor_tensor(o, i0, i1, op)
                    dve.drain()

                def first_best(oh, scores_, mx, eq, pk, top):
                    V.tensor_reduce(mx[:, :, 0], scores_, AX.X, ALU.max)
                    dve.drain()
                    tt(eq[:, :, :], scores_, bc(mx[:, :, :], NG), ALU.is_equal)
                    tt(pk[:, :, :], eq[:, :, :], C("prio").rearrange("p (o n) -> p o n", o=1).broadcast_to([P, TILES, NG]), ALU.mult)
                    V.tensor_reduce(top[:, :, 0], pk[:, :, :], AX.X, ALU.max)
                    dve.drain()
                    tt(oh[:, :, :], pk[:, :, :], bc(top[:, :, :], NG), ALU.is_equal)

                first_best(goh, lg, gmax, geq, gpk, gsum)
                tt(gex[:, :, :], lg, bc(gmax[:, :, :], NG), ALU.subtract)
                le = lgt[:, :, NG:].rearrange("p t (g j) -> p t j g", g=NG)
                for t in range(TILES):
                    V.tensor_tensor(lsel4[:, t, :, :], le[:, t, :, :], goh[:, t, :].rearrange("p (o g) -> p o g", o=1).broadcast_to([P, EPG, NG]), ALU.mult)
                dve.drain()
                V.tensor_reduce(lsel[:, :, :], lsel4[:, :, :, :], AX.X, ALU.add)
                dve.drain()
                first_best(oh1, lsel[:, :, :], m1, geq, gpk, gsum)
                V.scalar_tensor_tensor(lsel2[:, :, :], oh1[:, :, :], -BIG, lsel[:, :, :], ALU.mult, ALU.add)
                dve.drain()
                first_best(oh2, lsel2[:, :, :], m2, geq, gpk, gsum)
                V.tensor_tensor(e21[:, :, :], m2[:, :, :], m1[:, :, :], ALU.subtract).then_inc(s_gx, 1)
                dve.wait_ge(s_gxe, SET + l + 1)
                V.tensor_reduce(gsum[:, :, 0], gex[:, :, :], AX.X, ALU.add)
                V.tensor_scalar(wt1[:, :, :], e21[:, :, :], 1.0, None, ALU.add)
                dve.drain()
                V.reciprocal(pgrp[:, :, :], gsum[:, :, :])
                V.reciprocal(wt2[:, :, :], wt1[:, :, :])
                dve.drain()
                tt(wt1[:, :, :], pgrp[:, :, :], wt2[:, :, :], ALU.mult)
                tt(wt2[:, :, :], wt1[:, :, :], e21[:, :, :], ALU.mult)
                for t in range(TILES):
                    for oh, Ek in ((oh1, E1), (oh2, E2)):
                        V.tensor_tensor(Ek[:, t, :].rearrange("p (g j) -> p g j", g=NG), goh[:, t, :].rearrange("p (g o) -> p g o", o=1).broadcast_to([P, NG, EPG]),
                                        oh[:, t, :].rearrange("p (o j) -> p o j", o=1).broadcast_to([P, NG, EPG]), ALU.mult)
                dve.drain()
                V.tensor_tensor(Em[:, :, :], E1[:, :, :], E2[:, :, :], ALU.add).then_inc(s_rM, 1)
                dve.wait_ge(s_rk, SET + l + 1)
                rk = ps[:, 6, 0:TILES * NE].rearrange("p (t e) -> p t e", e=NE)
                V.scalar_tensor_tensor(rkm[:, :, :], rk, 1.0, Em[:, :, :], ALU.add, ALU.mult)
                V.tensor_reduce(cmax[:, :], ps[:, 6, TILES * NE:TILES * NE + NE], AX.X, ALU.max)
                dve.drain()
                V.tensor_scalar(rkm[:, :, :], rkm[:, :, :], -1.0, None, ALU.add)
                V.tensor_tensor(cge[:, :], cmax[:, :].broadcast_to([P, 4]), C("thr"), ALU.is_gt)
                for k, Ek in enumerate((E1, E2)):
                    tt(rtmp[:, :, :], rk, Ek[:, :, :], ALU.mult)
                    V.tensor_reduce(rsel[:, k, :], rtmp[:, :, :], AX.X, ALU.add)
                    tt(rpos[:, :, :], C("base").rearrange("p (o e) -> p o e", o=1).broadcast_to([P, TILES, NE]), Ek[:, :, :], ALU.mult)
                    V.tensor_reduce(bsel[:, k, :], rpos[:, :, :], AX.X, ALU.add)
                    dve.drain()
                V.tensor_reduce(cr[:, :], cge[:, :], AX.X, ALU.add)
                V.tensor_copy(crf[:, 0:1], info[:, ds(l * 2, 1)])
                dve.drain()
                V.tensor_scalar(cr[:, :], cr[:, :], 1.0, None, ALU.add)
                dve.drain()
                V.tensor_copy(info[:, ds(l * 2 + 1, 1)], cr[:, :])
                V.tensor_tensor(crf[:, 1:2], crf[:, 0:1], cr[:, :], ALU.add)
                dve.drain()
                V.tensor_copy(info[:, ds(l * 2 + 2, 1)], crf[:, 1:2]).then_inc(s_info, 1)
                dve.wait_ge(s_info, SET + l + 1)
                done = rounds_before(dve, l)
                now = rounds_now(dve, l)
                hold(dve)
                with dve.Fori(0, now) as r:
                    for e in range(NE):
                        if e >= ONEHOTS:
                            dve.wait_ge(r_idx, SET + (done + r) * NE + e - ONEHOTS + 1)
                        V.tensor_tensor(onehot[:, e % ONEHOTS, :, :], iota.rearrange("p (o s) -> p o s", o=1).broadcast_to([P, TILES, SLOTS]),
                                        rkm[:, :, e:e + 1].broadcast_to([P, TILES, SLOTS]), ALU.is_equal).then_inc(r_oh, 1)
                    dve.wait_ge(r_idx, SET + (done + r + 1) * NE)
                    V.tensor_reduce(stok[:, :], ps[:, 5, 0:2 * NE].rearrange("p (e i) -> p e i", i=2), AX.X, ALU.add)
                    dve.drain()
                    V.tensor_copy(sidx[:, :], stok[:, :]).then_inc(r_slots, 1)
                    V.tensor_scalar(rkm[:, :, :], rkm[:, :, :], -float(SLOTS), None, ALU.add)
                    V.tensor_scalar(posf[:, :, :], rsel[:, :, :], 0.0, float(SLOTS - 1), ALU.max, ALU.min)
                    V.tensor_scalar(inr[:, :, :], rsel[:, :, :], 0.0, None, ALU.is_ge)
                    V.tensor_scalar(in2[:, :, :], rsel[:, :, :], float(SLOTS), None, ALU.is_lt)
                    dve.drain()
                    V.tensor_tensor(posf[:, :, :], posf[:, :, :], bsel[:, :, :], ALU.add)
                    V.tensor_tensor(inr[:, :, :], inr[:, :, :], in2[:, :, :], ALU.mult)
                    V.tensor_scalar(rsel[:, :, :], rsel[:, :, :], -float(SLOTS), None, ALU.add)
                    dve.drain()
                    V.tensor_copy(pos[:, :, :], posf[:, :, :])
                    V.tensor_tensor(wsel[:, 0, :], inr[:, 0, :], wt1[:, :, 0], ALU.mult)
                    V.tensor_tensor(wsel[:, 1, :], inr[:, 1, :], wt2[:, :, 0], ALU.mult).then_inc(r_slots, 1)
                    dve.drain()

                    def expert_pair(ep, first, last):
                        g = (done + r) * (NE // 2) + ep

                        def low(j):
                            ring = j % SPL
                            dve.wait_ge(r_hi, SET + g * EXU + j + 1)
                            V.tensor_tensor(w_lo[:, ring, :], raw_slot(j), w_hi[:, ring, :].bitcast(F32), ALU.subtract).then_inc(r_lo, 1)

                        def turned_rows(i):
                            dve.drain()
                            dve.wait_ge(r_Thi, SET + g * 2 + i + 1)
                            V.tensor_tensor(xT_lo[:, i % 2, :, :], pair(0, 1024).rearrange("p (k n) -> p k n", k=KC),
                                            xT_hi[:, i % 2, :, :].bitcast(F32), ALU.subtract).then_inc(r_Tlo, 1)

                        if first:
                            turned_rows(0)
                        for i in range(2):
                            for q in range(6):
                                low(6 * i + q)
                            dve.drain()
                            dve.wait_ge(r_hg, SET + g * 2 + i + 1)
                            V.tensor_tensor(hid[:, i, :], hg[:, i, :], ps[:, 4 + i, FE:2 * FE], ALU.mult).then_inc(r_hid, 1)
                            src = ps[:, 6, 256 * i:256 * i + 256].rearrange("p (k n) -> p k n", k=2)
                            dve.drain()
                            dve.wait_ge(r_HT, SET + g * 2 + i + 1)
                            V.tensor_copy(hidT_hi[:, i, :, :], src)
                            dve.drain()
                            V.tensor_tensor(hidT_lo[:, i, :, :], src, hidT_hi[:, i, :, :].bitcast(F32), ALU.subtract).then_inc(r_hT, 1)
                            if not (last and i == 1):
                                turned_rows(i + 1)

                    expert_pair(0, True, False)
                    hold(dve)
                    with dve.Fori(1, NE // 2 - 1) as ep:
                        expert_pair(ep, False, False)
                    expert_pair(NE // 2 - 1, False, True)
                    dve.wait_ge(s_gtl, SET + 64 * (l + 1))
                    for t in range(TILES):
                        dve.wait_ge(s_yg[t % 2], 32 * ((done + r) * tiles_of(t) + t // 2 + 1))
                        V.tensor_scalar(yg[:, t % 2, 0, :], yg[:, t % 2, 0, :], wsel[:, 0, t:t + 1], None, ALU.mult)
                        dve.drain()
                        V.scalar_tensor_tensor(yg[:, t % 2, 0, :], yg[:, t % 2, 1, :], wsel[:, 1, t:t + 1], yg[:, t % 2, 0, :], ALU.mult, ALU.add)
                        dve.drain()
                        V.tensor_tensor(yg[:, t % 2, 0, :], yg[:, t % 2, 0, :], gt[:, gl(t), :], ALU.mult)
                        dve.drain()
                        V.tensor_tensor(x[:, t, :], x[:, t, :], yg[:, t % 2, 0, :], ALU.add).then_inc(r_added, 1)
                dve.drain()
                dve.sem_inc(s_done, 1)
            dve.wait_ge(s_fsd, SET + 1)
            V.reciprocal(rstd, sd)
            dve.drain()
            dve.wait_ge(s_fg, SET + 16)
            for t in range(TILES):
                V.scalar_tensor_tensor(x[:, t, :], x[:, t, :], rstd[:, t:t + 1], gt[:, 0, :], ALU.mult, ALU.mult).then_inc(s_fy, 1)

        @block.tensor
        def _(pe):
            pe.sem_inc(r_used, SPL)
            set_semaphores(pe, 4)
            mm = nc.tensor.matmul
            tr = nc.tensor.transpose

            def passes(ring):
                return ((w_hi[:, ring, :], 0), (w_hi[:, ring, :], 1), (w_lo[:, ring, :], 0))

            def feature(l, u, b, act_pair, value=None, k0=0, nk=KC, m=P, chunk0=0):
                ring = u % SPL
                pe.wait_ge(s_split, SET + (l * UNITS + u + 1 if value is None else value))
                for k in range(nk):
                    for i, (w, h) in enumerate(passes(ring)):
                        for c in range(2):
                            ins = mm(ps[0:m, 2 * b + c, 0:HT], w[:, k * m:(k + 1) * m], act_pair[h][:, chunk0 + k, HT * c:HT * (c + 1)],
                                     start=(k == 0 and i == 0), stop=(k == nk - 1 and i == 2))
                ins.then_inc(s_used, 1)

            def tokens(l, u, j, act_pair, bank, tile_done=None):
                ring = u % SPL
                pe.wait_ge(s_split, SET + l * UNITS + u + 1)
                for kk in range(2):
                    k = 2 * j + kk
                    cols = slice(512 * kk, 512 * kk + 512)
                    for t in range(TILES):
                        for i, (w, h) in enumerate(passes(ring)):
                            ins = mm(ps[:, bank(t), :], act_pair[h][:, k, t * P:(t + 1) * P], w[:, cols],
                                     start=(k == 0 and i == 0), stop=(k == KC - 1 and i == 2))
                        if tile_done is not None and k == KC - 1 and t < PT:
                            ins.then_inc(tile_done, 1)
                ins.then_inc(s_used, 1)

            hT, yT, zT = (hT_hi, hT_lo), (yT_hi, yT_lo), (zT_hi, zT_lo)
            pe.wait_ge(s_const, SET + 32)
            pe.wait_ge(s_cond, SET + 1)
            with pe.Fori(0, DEPTH) as l:
                pe.wait_ge(s_done, SET + l)
                for b in range(ADA_BLOCKS):
                    if b >= 2:
                        pe.wait_ge(s_mrow, SET + l * ADA_BLOCKS + b - 1)
                    for k in range(KC):
                        u = b * KC + k
                        slot = u % RAW
                        per_layer = raw_value(1, 0) - raw_value(0, 0) if slot == 0 else raw_value(1, slot) - raw_value(0, slot)
                        pe.wait_ge(s_raw[slot], SET + l * per_layer + 16 * (u // RAW + 1))
                        for c in range(2):
                            ins = mm(ps[0:2, 2 * (b % 2) + c, :], condT[:, k, :], raw[:, slot, 512 * c:512 * c + 512], start=(k == 0), stop=(k == KC - 1))
                        ins.then_inc(s_ada, 1)
                    for t in h_tiles(b):
                        pe.wait_ge(s_h, SET + l * 2 * TILES + t + 1)
                        if t >= 2:
                            pe.wait_ge(s_hT, SET + l * TILES + t - 1)
                        for k in range(KC):
                            ins = tr(psf[:, 1024 * (2 + t % 2) + k * P:1024 * (2 + t % 2) + (k + 1) * P], hbuf[:, t % 2, k * P:(k + 1) * P], ident)
                        ins.then_inc(s_hps, 1)
                pe.wait_ge(s_hT, SET + (l + 1) * TILES)
                pe.wait_ge(s_mrow, SET + (l + 1) * ADA_BLOCKS)
                for j in range(4):
                    tokens(l, U_V + j, j, hT, lambda t: t)
                pe.wait_ge(s_v, SET + (l + 1) * TILES)
                for j in range(4):
                    tokens(l, U_R + j, j, hT, lambda t: (5 + t) % 8)
                pe.wait_ge(s_split, SET + l * UNITS + U_TV + 1)
                for t in range(TILES):
                    for k in range(KC):
                        for i, (w, h) in enumerate(passes(U_TV % SPL)):
                            ins = mm(psf[:, 1024 + t * P:1024 + (t + 1) * P], hT[h][:, k, t * P:(t + 1) * P], w[:, k * P:(k + 1) * P],
                                     start=(k == 0 and i == 0), stop=(k == KC - 1 and i == 2))
                ins.then_inc(s_used, 1)
                pe.wait_ge(s_r, SET + (l + 1) * TILES)
                feature(l, U_LR, 2, hT, m=2 * RANK)
                feature(l, U_GLA, 3, hT)
                pe.wait_ge(s_tv, SET + l + 1)
                pe.wait_ge(s_lr, SET + l + 1)
                pe.wait_ge(s_lay2, SET + (l + 1) * 16 * 21)

                def gate_logits(h):
                    for d in range(2):
                        for c in range(2):
                            ins = mm(ps[:, 2 * d + c, 0:HT], w_gate[:, d, h * DK:(h + 1) * DK], lrT[:, HT * c:HT * (c + 1)], start=True, stop=True)
                        ins.then_inc(s_gz, 1)

                gate_logits(0)
                feature(l, U_GLA + 1, 2, hT)
                for h in range(HEADS):
                    hh = l * HEADS + h
                    pe.wait_ge(s_gqk, SET + hh * 2 + 2)
                    for d in range(2):
                        pe.wait_ge(s_gin, SET + hh * 2 + d + 1)
                        for t in range(TILES):
                            ins = tr(psf[:, 1024 * (2 + d) + t * P:1024 * (2 + d) + (t + 1) * P], sp_[:, d, t * P:(t + 1) * P], ident)
                        ins.then_inc(s_gkT, 1)
                        for t in range(TILES):
                            cs = slice(t * P, (t + 1) * P)
                            ins = mm(psf[:, 1024 * d + t * P:1024 * d + (t + 1) * P], En[:, d, cs], cb[:, d, cs], start=True, stop=True)
                        ins.then_inc(s_gatt, 1)
                    for d in range(2):
                        pe.wait_ge(s_gke, SET + hh * 2 + d + 1)
                        pe.wait_ge(s_gam, SET + hh * 2 + 2)
                        for q in range(2):
                            if q:
                                pe.wait_ge(s_gds, SET + hh * 4 + 2 * d + 1)
                                hold(pe)
                            o = CHUNK * q
                            for t in range(TILES):
                                n = 2 * t + q
                                ins = mm(psf[:, 1536 * d + n * DV:1536 * d + (n + 1) * DV], zb[o:o + CHUNK, d, t * P:(t + 1) * P],
                                         v_sb[o:o + CHUNK, t, h * DV:(h + 1) * DV], start=True, stop=True)
                            ins.then_inc(s_gds, 1)
                    pe.wait_ge(s_gst, SET + hh * 2 + 2)
                    hold(pe)
                    for t in range(TILES):
                        dst = ps[:, 6 + t // 4, (t % 4) * DV:(t % 4 + 1) * DV]
                        for d in range(2):
                            mm(dst, attm[:, d, t, :], v_sb[:, t, h * DV:(h + 1) * DV], start=(d == 0), stop=False, skip_group_check=True)
                        for d in range(2):
                            for n in (2 * t, 2 * t + 1):
                                o = CHUNK * (n % 2)
                                if n < SCH:
                                    i = n if d == 0 else SCH - 1 - n
                                else:
                                    i = SCH + 1 + (n - SCH if d == 0 else NCH - 1 - n)
                                ins = mm(dst[o:o + CHUNK, :], cb[:, d, n * CHUNK:(n + 1) * CHUNK], st[d][:, i, :], start=False, stop=(d == 1),
                                         skip_group_check=True)
                    ins.then_inc(s_go, 1)
                    if h + 1 < HEADS:
                        gate_logits(h + 1)
                    pe.wait_ge(s_gy, SET + hh + 1)
                    for t in range(TILES):
                        ins = tr(psf[:, 2048 + t * P:2048 + (t + 1) * P], yb[:, t, :], ident)
                    ins.then_inc(s_gyT, 1)
                    if h + 1 < HEADS:
                        feature(l, U_GLA + 2 * h + 2, 3, hT)
                        pe.wait_ge(s_y, SET + l * 12 + h + 1)
                        feature(l, U_GLA + 2 * h + 3, 2, hT)
                for kv in range(KVH):
                    j = l * (KVH + 4) + kv
                    pe.wait_ge(s_kraw, SET + j)
                    feature(l, U_K + kv, 0, hT)
                    if kv == 0:
                        pe.wait_ge(s_y, SET + l * 12 + HEADS)
                    pe.wait_ge(s_kraw, SET + j + 1)
                    pe.wait_ge(s_rope, SET + j)
                    mm(ps[:, 4, :], rot, qraw[:, 0:SAMPLE], start=True, stop=True).then_inc(s_rot, 1)
                    pe.wait_ge(s_kc, SET + l * KVH + kv)
                    tr(ps[:, 5, 0:P], ckd[:, kv, :, :], ident)
                    tr(ps[:, 5, P:2 * P], qraw[:, SAMPLE:], ident).then_inc(s_kt, 1)

                def q_chunk(c):
                    j = l * (KVH + 4) + KVH + c
                    pe.wait_ge(s_kraw, SET + j)
                    feature(l, U_Q + c, 0, hT)
                    pe.wait_ge(s_kraw, SET + j + 1)
                    pe.wait_ge(s_rope, SET + j)
                    mm(ps[:, 4, :], rot, qraw[:, 0:SAMPLE], start=True, stop=True).then_inc(s_rot, 1)

                def scores(hd):
                    c, o, kv, b_ = hd // 2, HD * (hd % 2), hd // 4, l * AH + hd
                    if hd == 0:
                        pe.wait_ge(s_kc, SET + (l + 1) * KVH)
                    if hd % 2 == 0:
                        pe.wait_ge(s_rope, SET + l * (KVH + 4) + KVH + c + 1)
                        pe.wait_ge(s_qc, SET + l * 4 + c + 1)
                    rows = slice(o, o + HD)
                    for b in range(TILES):
                        n = b_ * TILES + b
                        if b >= 2:
                            pe.wait_ge(s_sce, SET + n - 1)
                        else:
                            pe.wait_ge(s_sce, SET + b_ * TILES)
                        q = qT[rows, c % 2, b * P:(b + 1) * P]
                        dst = ps[:, 5 + b % 2, :]
                        own_ = P + b * P
                        if b == PT:
                            ins = mm(dst[:, P:2 * P], q, kT[rows, kv, own_:own_ + P], start=True, stop=True)
                        else:
                            if b == 0:
                                mm(dst[:, P:2 * P], q, kT[rows, kv, own_:own_ + P], start=True, stop=True)
                            else:
                                mm(dst[:, 0:2 * P], q, kT[rows, kv, own_ - P:own_ + P], start=True, stop=True)
                            ins = mm(dst[:, 2 * P:3 * P], q, kT[rows, kv, 0:P], start=True, stop=True)
                            if b < PT - 1:
                                ins = mm(dst[:, 3 * P:4 * P], q, kT[rows, kv, own_ + P:own_ + 2 * P], start=True, stop=True)
                        ins.then_inc(s_sc, 1)

                def values(hd):
                    c, o, kv, b_ = hd // 2, HD * (hd % 2), hd // 4, l * AH + hd
                    pe.wait_ge(s_p, SET + b_ + 1)

                    def turn(b):
                        n = b_ * TILES + b
                        lo_, hi_ = span(b)
                        pe.wait_ge(s_pte, SET + (n - 1 if b >= 2 else b_ * TILES))
                        for i in range(ktiles(b)):
                            ins = tr(ps[:, 2 + b % 2, i * P:(i + 1) * P], s_sb[:, hd % 2, b, lo_ + i * P:lo_ + (i + 1) * P], ident)
                        ins.then_inc(s_pt, 1)

                    def weigh(b):
                        pe.wait_ge(s_pte, SET + b_ * TILES + b + 1)
                        vals = [tv[:, PT, :]] if b == PT else (
                            ([tv[:, b - 1, :]] if b > 0 else []) + [tv[:, b, :], cv[:, :]] + ([tv[:, b + 1, :]] if b < PT - 1 else []))
                        dst = ps[o:o + HD, 1, 384:512] if b == PT else ps[o:o + HD, 7, b * P:(b + 1) * P]
                        for i, v in enumerate(vals):
                            ins = mm(dst, v[:, kv * HD:(kv + 1) * HD], pT[:, b % 2, i * P:(i + 1) * P], start=(i == 0), stop=(i == len(vals) - 1))
                        return ins

                    for b in range(TILES + 1):
                        if b < TILES:
                            turn(b)
                        if b >= 1:
                            ins = weigh(b - 1)
                    if hd % 2:
                        ins.then_inc(s_ao, 1)

                q_chunk(0)
                scores(0)
                for hd in range(AH):
                    if hd + 1 < AH:
                        scores(hd + 1)
                    if hd % 2 == 0:
                        pe.wait_ge(s_y, SET + l * 12 + HEADS + hd // 2)
                    if hd % 2 == 0 and hd < AH - 2:
                        q_chunk(hd // 2 + 1)
                    values(hd)
                pe.wait_ge(s_y, SET + l * 12 + HEADS + 4)
                for f in range(4):
                    for i in range(3):
                        n = 3 * f + i
                        if n >= 4:
                            fo, io = divmod(n - 4, 3)
                            pe.wait_ge((s_cc, s_cu, s_cy)[io], SET + l * 4 + fo + 1)
                        feature(l, U_CONV + n, n % 4, hT)
                pe.wait_ge(s_cy, SET + (l + 1) * 4)
                pe.wait_ge(s_y, SET + (l + 1) * 12)
                hold(pe)
                with pe.Fori(0, KC) as n:
                    for i in range(3):
                        v = l * UNITS + U_M + n * 6 + 2 * i + 1
                        g = (l * KC + n) * 3
                        if i == 2:
                            pe.wait_ge(s_sig, SET + g + 1)
                        else:
                            pe.wait_ge(s_sig, SET + g)
                        feature(l, U_M + 2 * i, (2 * i) % 4, hT, v)
                        if i == 2:
                            pe.wait_ge(s_zm, SET + g + 1)
                        else:
                            pe.wait_ge(s_zm, SET + g)
                        feature(l, U_M + 2 * i + 1, (2 * i + 1) % 4, yT, v + 1, nk=4, chunk0=4 * i)
                pe.wait_ge(s_z, SET + (l + 1) * KC)
                for hf in range(2):
                    if hf == 1:
                        pe.wait_ge(s_x1, SET + l * 2 * TILES + 2)
                    for j in range(4):
                        tokens(l, U_OUT + 4 * hf + j, j, zT, lambda t: (5 * hf + t) % 8, s_out_tile)
                pe.wait_ge(s_x1, SET + (l + 1) * 2 * TILES)
                for t in range(TILES + 1):
                    if t < TILES:
                        pe.wait_ge(s_h, SET + (l * 2 + 1) * TILES + t + 1)
                        if t >= 2:
                            pe.wait_ge(s_h2T, SET + l * TILES + t - 1)
                        for k in range(KC):
                            ins = tr(psf[:, 1024 * (t % 2) + k * P:1024 * (t % 2) + (k + 1) * P], hbuf[:, t % 2, k * P:(k + 1) * P], ident)
                        ins.then_inc(s_hps, 1)
                    if t >= 1:
                        pe.wait_ge(s_h2T, SET + l * TILES + t)
                        for k in range(KC):
                            ins = mm(ps[:, 7, (t - 1) * 32:(t - 1) * 32 + NG + NE], h2T[:, (t - 1) % 2, k, :], w_rt[:, k, :], start=(k == 0), stop=(k == KC - 1))
                        ins.then_inc(s_rl, 1)
                pe.wait_ge(s_rM, SET + l + 1)
                for t in range(TILES + 1):
                    for i in range(min(t + 1, TILES)):
                        ins = mm(ps[:, 6, t * NE:(t + 1) * NE], tri_b[:, 0:P] if i == t else tri_b[:, P:], Em[:, i, :], start=(i == 0), stop=(i == min(t, TILES - 1)))
                ins.then_inc(s_rk, 1)
                pe.wait_ge(s_info, SET + l + 1)
                done = rounds_before(pe, l)
                now = rounds_now(pe, l)
                hold(pe)
                with pe.Fori(0, now) as r:
                    pe.wait_ge(r_hid, SET + (done + r) * NE)
                    for e in range(NE):
                        pe.wait_ge(r_oh, SET + (done + r) * NE + e + 1)
                        for t in range(TILES):
                            ins = mm(ps[:, 5, 2 * e:2 * e + 2], onehot[:, e % ONEHOTS, t, :], tok_b[:, t, :], start=(t == 0), stop=(t == TILES - 1))
                        ins.then_inc(r_idx, 1)
                    pe.wait_ge(r_slots, SET + (done + r) * 2 + 1)

                    def expert_pair(ep, first, last):
                        g = (done + r) * (NE // 2) + ep

                        def unit(j):
                            pe.wait_ge(r_lo, SET + EXU + g * EXU + j + 1)
                            return passes(j % SPL)

                        def turn_rows(i):
                            pe.wait_ge(r_xg[i % 2], (g + i // 2 + 1) * 16)
                            pe.wait_ge(r_Tlo, SET + g * 2 + i)
                            for k in range(KC):
                                ins = tr(psf[:, k * P:(k + 1) * P], xg[:, i % 2, k * P:(k + 1) * P], ident)
                            ins.then_inc(r_T, 1)

                        if first:
                            turn_rows(0)
                        for i in range(2):
                            pe.wait_ge(r_Tlo, SET + g * 2 + i + 1)
                            for j in range(4):
                                for kk, ws in enumerate((unit(6 * i + j), passes((6 * i + j) % SPL))):
                                    k = 2 * j + kk
                                    for q, (w, h) in enumerate(ws):
                                        ins = mm(ps[:, 4 + i, :], (xT_hi, xT_lo)[h][:, i, k, :], w[:, 512 * kk:512 * kk + 512],
                                                 start=(k == 0 and q == 0), stop=(k == KC - 1 and q == 2))
                                ins.then_inc(r_used, 1)
                            if not (last and i == 1):
                                turn_rows(i + 1)
                            pe.wait_ge(r_hid, SET + g * 2 + i + 1)
                            for k in range(2):
                                ins = tr(ps[:, 6, 256 * i + k * P:256 * i + (k + 1) * P], hid[:, i, k * P:(k + 1) * P], ident)
                            ins.then_inc(r_HT, 1)
                            pe.wait_ge(r_hT, SET + g * 2 + i + 1)
                            pe.wait_ge(r_yo, SET + g * 2 + i)
                            for k in range(2):
                                for q, (w, h) in enumerate(unit(6 * i + 4 + k)):
                                    for c in range(2):
                                        ins = mm(ps[:, 2 + c, :], (hidT_hi, hidT_lo)[h][:, i, k, :], w[:, 512 * c:512 * c + 512],
                                                 start=(k == 0 and q == 0), stop=(k == 1 and q == 2))
                                ins.then_inc(r_used, 1)

                    expert_pair(0, True, False)
                    hold(pe)
                    with pe.Fori(1, NE // 2 - 1) as ep:
                        expert_pair(ep, False, False)
                    expert_pair(NE // 2 - 1, False, True)


_INS = ["x_prompt", "x_sample", "state_gla", "cache_k", "cache_v", "c", "c_ctx", "w_ada", "b_ada", "norm1_g", "norm2_g",
        "w_in", "conv_w", "gla_w_gate", "gla_b_gate", "gla_norm_g", "attn_sink", "w_branch", "w_out", "w_route_group",
        "b_route_group", "w_route_expert", "b_route_expert", "w_exp_gate", "w_exp_up", "w_exp_down", "final_norm_g"]
_OUTS = [("y_prompt", (1, PROMPT, D)), ("y_sample", (1, SAMPLE, D)), ("new_state_gla", (1, DEPTH, 2, HEADS, DK, DV)),
         ("new_cache_k", (1, DEPTH, PROMPT, KVH, HD)), ("new_cache_v", (1, DEPTH, PROMPT, KVH, HD))]


def kernel(**inputs):
    import concourse.bacc as bacc
    from concourse.bass_utils import run_bass_kernel_spmd

    nc = bacc.Bacc("TRN2", target_bir_lowering=False, num_devices=1)
    arrays = {n: np.ascontiguousarray(inputs[n]) for n in _INS}
    arrays["table"] = shape_constants()
    arrays["zeros"] = np.zeros((RANK, HEADS * DK), np.float32)
    ins = {n: nc.dram_tensor(f"in_{n}", v.shape, F32, kind="ExternalInput").ap() for n, v in arrays.items()}
    outs = [nc.dram_tensor(f"out_{n}", s, F32, kind="ExternalOutput").ap() for n, s in _OUTS]
    build(nc, ins, *outs)
    r = run_bass_kernel_spmd(nc, [{f"in_{n}": v for n, v in arrays.items()}], core_ids=[0])
    return tuple(r.results[0][f"out_{n}"] for n, _ in _OUTS)
```

```python
from contextlib import ExitStack

import numpy as np

import concourse.bass as bass
import concourse.mybir as mybir

F32 = mybir.dt.float32
F32R = mybir.dt.float32r
I32 = mybir.dt.int32
BF16 = mybir.dt.bfloat16
U32 = mybir.dt.uint32
ALU = mybir.AluOpType
ACT = mybir.ActivationFunctionType
AX = mybir.AxisListType
P = 128

DEPTH, D = 2, 1024
KC = D // P
SAMPLE, PROMPT = 512, 128
TOK = SAMPLE + PROMPT
TILES = TOK // P
PT = TILES - 1
GRID_W = 64
EPS = 1e-6
CONV_W, CONV_K = 512, 3
HEADS, DK, DV, CHUNK = 4, 128, 128, 64
NCH = TOK // CHUNK
HT = TOK // 2
SCH = SAMPLE // CHUNK
RANK, TAU = 16, 16.0
AH, KVH, HD = 8, 2, 64
NG, EPG = 4, 4
NE = NG * EPG
FE = 256
SLOTS = P
BIG = 1e30
SET = 1

SPLITS = (CONV_W, CONV_W, CONV_W, HEADS * DK, HEADS * DK, HEADS * DV, HEADS * DV, RANK, RANK, AH * HD, KVH * HD, KVH * HD, D, D, D)
(C_AB, C_AC, C_AH, C_GQ, C_GK, C_GV, C_GR, C_LF, C_LB, C_TQ, C_TK, C_TV, C_MA, C_MB, C_MC) = [
    sum(SPLITS[:i]) for i in range(len(SPLITS))]

ADA_BLOCKS = 6
ADA = ADA_BLOCKS * KC
U_V, U_R, U_TV, U_LR, U_GLA = 0, 4, 8, 9, 10
U_K = U_GLA + 2 * HEADS
U_Q = U_K + KVH
U_CONV = U_Q + AH // 2
U_M = U_CONV + 3 * CONV_W // P
U_OUT = U_M + 6 * KC
UNITS = U_OUT + 8
RAW, SPL = 6, 3
EXU = 12
ONEHOTS = 8
ROUND_UNITS = NE // 2 * EXU

CONST = {}
_at = 0
for _name, _n in (("ident", P), ("rot", P), ("iota", P), ("strip", 4 * P), ("fwd", CHUNK),
                  ("bwd", CHUNK), ("prio", NG), ("base", NE), ("tokid", 2 * TILES), ("cst", 2), ("thr", 4)):
    CONST[_name] = (_at, _n)
    _at += _n
CONST_RES = _at
for _name, _n in (("cos", SAMPLE), ("sin", SAMPLE), ("scan", TOK), ("tri", P), ("ones", P)):
    CONST[_name] = (_at, _n)
    _at += _n
CONST_COLS = _at


def shape_constants():
    t = np.zeros((P, CONST_COLS), np.float32)

    def put(name, v):
        a, n = CONST[name]
        t[:, a:a + n] = v

    r = np.arange(P)
    put("ident", np.eye(P))
    rot = np.zeros((P, P))
    half = HD // 4
    for m in range(P):
        rot[(m + half) if m % (2 * half) < half else (m - half), m] = -1.0 if m % (2 * half) < half else 1.0
    put("rot", rot)
    put("tri", (r[:, None] < r[None, :]).astype(np.float32))
    put("ones", 1.0)
    put("iota", r[None, :])
    strip = np.zeros((P, 4 * P))
    strip[:, 0:P] = np.where(r[None, :] >= r[:, None], 0.0, -BIG)
    strip[:, 3 * P:] = np.where(r[None, :] <= r[:, None], 0.0, -BIG)
    put("strip", strip)
    s, c = (r % CHUNK)[:, None], np.arange(CHUNK)[None, :]
    put("fwd", s <= c)
    put("bwd", s >= c)
    put("prio", np.arange(NG, 0, -1)[None, :])
    put("base", (np.arange(NE) * SLOTS)[None, :])
    put("tokid", np.stack([np.broadcast_to(r[:, None], (P, TILES)), np.broadcast_to(P * np.arange(TILES), (P, TILES))], -1).reshape(P, 2 * TILES))
    put("cst", np.array([[EPS, 1.0]]))
    put("thr", (P * np.arange(1, 5))[None, :])
    inv = (10000.0 ** (-np.arange(half, dtype=np.float32) / half)).astype(np.float32)
    pos = np.arange(SAMPLE)
    d = r % HD
    where = np.where((d // (2 * half))[:, None] == 0, (pos // GRID_W)[None, :], (pos % GRID_W)[None, :]).astype(np.float32)
    ang = (where * inv[d % half][:, None]).astype(np.float32)
    put("cos", np.cos(ang.astype(np.float64)))
    put("sin", np.sin(ang.astype(np.float64)))
    put("scan", (np.arange(TOK) % CHUNK != 0)[None, :])
    return t


def ds(a, n):
    return bass.ds(a, n)


def build(nc, a, out_yp, out_ys, out_st, out_ck, out_cv):
    with ExitStack() as ctx:
        ctx.enter_context(nc.allow_non_contiguous_dma(reason="small vectors, one element per partition"))

        sems = []

        def sem(name):
            sems.append(ctx.enter_context(nc.semaphore(name)))
            return sems[-1]

        def gather_sem(name):
            return ctx.enter_context(nc.semaphore(name))

        s_start = ctx.enter_context(nc.semaphore("semaphores_set"))

        base = [(nc.sbuf_base + 63) // 64 * 64]

        def at(name, shape, dt, offset):
            return nc.alloc_sbuf_tensor_at(name, shape, dt, offset=offset)

        def room(nbytes):
            o = base[0]
            base[0] += (nbytes + 31) // 32 * 32
            return o

        def own(name, shape, dt=F32):
            return at(name, shape, dt, room((2 if dt == BF16 else 4) * int(np.prod(shape[1:]))))

        ROW = 4 * TOK
        o_ht = room(2 * KC * ROW)
        o_yhi = room(12 * ROW)
        o_ylo = room(12 * ROW)
        o_w = room(2 * KC * ROW)
        o_m = room(5 * ROW)
        raw = own("raw", [P, RAW, 1024])
        w_hi = own("w_hi", [P, SPL, 1024], F32R)
        w_lo = own("w_lo", [P, SPL, 1024], F32R)
        con = own("con", [P, CONST_RES])
        condT = own("condT", [P, KC, 2])
        conv_w = own("conv_w", [P, CONV_W // P, CONV_K])
        b_gate = own("b_gate", [P, 2, HEADS])
        sink = own("sink", [P, AH])
        w_rt = own("w_rt", [P, KC, NG + NE])
        b_rt = own("b_rt", [P, NG + NE])
        small = own("small", [P, 80])
        tri_b = own("tri_b", [P, 2 * P], BF16)
        tok_b = own("tok_b", [P, TILES, 2], BF16)
        info = own("info", [P, 2 * DEPTH + 2], I32)
        assert base[0] <= nc.sbuf_usable_end, (base[0], nc.sbuf_usable_end)

        def C(name):
            c, n = CONST[name]
            return con[:, c:c + n]

        ident, rot, iota, strip = (C(n) for n in ("ident", "rot", "iota", "strip"))
        tri_in = at("tri_in", [P, 2 * P], F32, o_ht)
        eps = C("cst")[:, 0:1]
        one = C("cst")[:, 1:2]
        hT_hi = at("hT_hi", [P, KC, TOK], F32R, o_ht)
        hT_lo = at("hT_lo", [P, KC, TOK], F32R, o_ht + KC * ROW)
        yT_hi = at("yT_hi", [P, 12, TOK], F32R, o_yhi)
        yT_lo = at("yT_lo", [P, 12, TOK], F32R, o_ylo)
        zT_hi = at("zT_hi", [P, KC, TOK], F32R, o_w)
        zT_lo = at("zT_lo", [P, KC, TOK], F32R, o_w + KC * ROW)
        x = at("x", [P, TILES, D], F32, o_yhi)
        gt = at("gt", [P, 2, D], F32, o_yhi + 8 * ROW)
        raw_more = at("raw_more", [P, EXU - RAW, 1024], F32, o_ylo)
        modA = at("modA", [P, 2, D], F32, o_ylo)
        modB = at("modB", [P, 2, D], F32, o_ylo + 8192)
        hbuf = at("hbuf", [P, 2, D], F32, o_ylo + 16384)
        junk = at("junk", [P, D], F32, o_ylo + 24576)
        ada_b = at("ada_b", [2, ADA_BLOCKS, D], F32, o_w)
        ada_g = at("ada_g", [2, 2, D], F32, o_w + 24576)
        mrow = at("mrow", [2, 2, D], F32, o_w + 32768)
        v_sb = at("v_sb", [P, TILES, HEADS * DV], F32, o_w)
        rg = at("rg", [P, TILES, HEADS * DV], F32, o_w + 4 * ROW)
        tv = at("tv", [P, TILES, P], F32, o_w + 8 * ROW)
        lrT = at("lrT", [2 * RANK, TOK], F32, o_w + 9 * ROW)
        qs = [at("qs0", [P, TOK], F32, o_w + 10 * ROW), at("qs1", [P, TOK], F32, o_yhi + 7 * ROW)]
        ks = [at("ks0", [P, TOK], F32, o_w + 11 * ROW), at("ks1", [P, TOK], F32, o_ylo + 7 * ROW)]
        zb = at("zb", [P, 2, TOK], F32, o_w + 12 * ROW)
        sp_ = at("sp_", [P, 2, TOK], F32, o_w + 14 * ROW)
        cb = at("cb", [P, 2, TOK], F32, o_yhi)
        E_ = at("E_", [P, 2, TOK], F32, o_yhi + 2 * ROW)
        En = at("En", [P, 2, TOK], F32, o_yhi + 8 * ROW)
        attm = at("attm", [P, 2, TILES, P], F32, o_yhi + 10 * ROW)
        NST = 12
        st = [at("st0", [P, NST, DV], F32, o_ylo), at("st1", [P, NST, DV], F32, o_ylo + 8 * ROW)]
        scanm = at("scanm", [P, TOK], F32, o_ylo + NST * DV * 4)
        yb = at("yb", [P, TILES, DV], F32, o_ylo + 8 * ROW + NST * DV * 4)
        osq = at("osq", [P, TILES, DV], F32, o_w + 15 * ROW)
        w_gate = at("w_gate", [2 * RANK, 2, HEADS * DK], F32, o_m)
        g_norm = at("g_norm", [P, HEADS * DV], F32, o_m + 4096)
        cossin = at("cossin", [P, 2, SAMPLE], F32, o_m + 6144)
        cv = at("cv", [P, KVH * HD], F32, o_m + 10240)
        ckd = at("ckd", [P, KVH, 2, HD], F32, o_m + 10752)
        s_sb = at("s_sb", [P, 2, TILES, 4 * P], F32, o_w)
        tv_end = o_w + 9 * ROW
        KCOLS = P + TOK
        kT = at("kT", [P, KVH, KCOLS], F32, tv_end)
        pT = at("pT", [P, 2, 4 * P], F32, tv_end + KVH * KCOLS * 4)
        qT = at("qT", [P, 2, TOK], F32, tv_end + KVH * KCOLS * 4 + 4096)
        qraw = at("qraw", [P, TOK], F32, tv_end + KVH * KCOLS * 4 + 4096 + 2 * ROW)
        assert tv_end + KVH * KCOLS * 4 + 4096 + 3 * ROW <= o_w + 16 * ROW
        rt1 = at("rt1", [P, SAMPLE], F32, o_yhi)
        rt2 = at("rt2", [P, SAMPLE], F32, o_yhi + 2048)
        kout = at("kout", [P, KVH, HD], F32, o_yhi + 4096)
        csb = at("csb", [P, TOK], F32, o_w)
        upad = at("upad", [P, TOK + 4], F32, o_w + ROW)
        yf = at("yf", [P, TOK], F32, o_w + 3 * ROW)
        sg = at("sg", [P, 3, TOK], F32, o_m)
        zacc = at("zacc", [P, TOK], F32, o_m + 3 * ROW)
        zt = at("zt", [P, TOK], F32, o_m + 4 * ROW)
        h2T = at("h2T", [P, 2, KC, P], F32, o_ht)
        xg = at("xg", [P, 2, D], F32, o_ht + 8192)
        yg = at("yg", [P, 2, 2, D], F32, o_ht + 16384)
        onehot = at("onehot", [P, ONEHOTS, TILES, SLOTS], BF16, o_ht + 16384)
        xT_hi = at("xT_hi", [P, 2, KC, SLOTS], F32R, o_w)
        xT_lo = at("xT_lo", [P, 2, KC, SLOTS], F32R, o_w + 8192)
        hidT_hi = at("hidT_hi", [P, 2, 2, SLOTS], F32R, o_w + 16384)
        hidT_lo = at("hidT_lo", [P, 2, 2, SLOTS], F32R, o_w + 18432)
        hid = at("hid", [P, 2, FE], F32, o_w + 20480)
        hg = at("hg", [P, 2, FE], F32, o_w + 22528)
        yo = at("yo", [P, 2, D], F32, o_w + 24576)
        _rt = [o_m]

        def rt(name, shape, dt=F32):
            o = _rt[0]
            _rt[0] += (4 * int(np.prod(shape[1:])) + 31) // 32 * 32
            assert _rt[0] <= o_m + 5 * ROW
            return at(name, shape, dt, o)

        lgt = rt("lgt", [P, TILES, NG + NE])
        gmax = rt("gmax", [P, TILES, 1])
        geq = rt("geq", [P, TILES, NG])
        gpk = rt("gpk", [P, TILES, NG])
        goh = rt("goh", [P, TILES, NG])
        gex = rt("gex", [P, TILES, NG])
        gsum = rt("gsum", [P, TILES, 1])
        pgrp = rt("pgrp", [P, TILES, 1])
        lsel4 = rt("lsel4", [P, TILES, EPG, NG])
        lsel = rt("lsel", [P, TILES, EPG])
        lsel2 = rt("lsel2", [P, TILES, EPG])
        m1 = rt("m1", [P, TILES, 1])
        m2 = rt("m2", [P, TILES, 1])
        oh1 = rt("oh1", [P, TILES, EPG])
        oh2 = rt("oh2", [P, TILES, EPG])
        e21 = rt("e21", [P, TILES, 1])
        wt1 = rt("wt1", [P, TILES, 1])
        wt2 = rt("wt2", [P, TILES, 1])
        E1 = rt("E1", [P, TILES, NE])
        E2 = rt("E2", [P, TILES, NE])
        Em = rt("Em", [P, TILES, NE], BF16)
        rkm = rt("rkm", [P, TILES, NE])
        rpos = rt("rpos", [P, TILES, NE])
        rtmp = rt("rtmp", [P, TILES, NE])
        posf = rt("posf", [P, 2, TILES])
        rsel = rt("rsel", [P, 2, TILES])
        bsel = rt("bsel", [P, 2, TILES])
        wsel = rt("wsel", [P, 2, TILES])
        inr = rt("inr", [P, 2, TILES])
        in2 = rt("in2", [P, 2, TILES])
        pos = rt("pos", [P, 2, TILES], I32)
        cmax = rt("cmax", [P, 1])
        cge = rt("cge", [P, 4])
        cr = rt("cr", [P, 1])
        crf = rt("crf", [P, 2])
        sidx = rt("sidx", [P, NE], I32)
        stok = rt("stok", [P, NE])

        ss, sd, rstd = small[:, 0:5], small[:, 5:10], small[:, 10:15]
        g_ss, g_ln, g_rs = small[:, 15:20], small[:, 20:25], small[:, 25:30]
        a_mx, a_rd = small[:, 30:35], small[:, 35:40]
        a_nm, a_rs, a_es = ([small[:, 40 + 10 * i + 5 * j:45 + 10 * i + 5 * j] for j in range(2)] for i in range(3))

        ps = ctx.enter_context(nc.psum_tensor("ps", [P, 8, 512], F32))
        psf = ps[:, :, :].rearrange("p b c -> p (b c)")

        def pair(i, n=TOK, m=P):
            return psf[0:m, 1024 * i:1024 * i + n]

        def two(i, m=P):
            return ps[0:m, 2 * i:2 * i + 2, 0:HT]

        def in_two(ap):
            return ap.rearrange("p (a n) -> p a n", a=2)

        mod_d = nc.dram_tensor("mod_scratch", (ADA_BLOCKS, 2, D), F32, kind="Internal").ap()
        x_d = nc.dram_tensor("x_scratch", (TOK, D), F32, kind="Internal").ap()
        h2_d = nc.dram_tensor("h2_scratch", (TOK, D), F32, kind="Internal").ap()
        ye_d = nc.dram_tensor("expert_scratch", (NE * SLOTS, D), F32, kind="Internal").ap()

        s_held = {e.engine: sem(f"held_{i}") for i, e in enumerate((nc.sync, nc.gpsimd, nc.scalar, nc.vector, nc.tensor))}
        s_x0, s_c0 = sem("x_loaded_first"), sem("cond_loaded")
        s_out_tile = sem("projected_tile")
        s_const, s_init, s_cond = sem("consts_loaded"), sem("init_done"), sem("cond_ready")
        s_raw = [sem(f"raw_loaded{i}") for i in range(RAW)]
        s_rawx = [sem(f"raw_expert_loaded{i}") for i in range(EXU)]
        s_lay, s_lay2, s_lay3 = sem("layer_rows_loaded"), sem("layer_consts_loaded"), sem("gla_consts_loaded")
        s_ada, s_mrow = sem("ada_unit_used"), sem("mod_row_ready")
        s_mst = [sem(f"mod_row_stored{i}") for i in range(2)]
        s_modl, s_xsav, s_xload, s_gtl = sem("mod_loaded"), sem("x_saved"), sem("x_loaded"), sem("gate_loaded")
        s_split, s_used = sem("unit_split"), sem("unit_used")
        s_sd, s_h, s_hps, s_hhi, s_hT = sem("norm_root"), sem("h_ready"), sem("h_transposed"), sem("hT_hi_ready"), sem("hT_ready")
        s_v, s_r, s_tv, s_lr = sem("v_ready"), sem("r_silu_ready"), sem("tv_ready"), sem("lr_ready")
        s_gqk, s_gz, s_gzb, s_gsp, s_gcb, s_gE, s_gin = (sem(n) for n in (
            "gla_q_k_copied", "gla_gate_logits", "gla_gate_biased", "gla_softplus", "gla_decay_sums", "gla_exps", "gla_qk_decayed"))
        s_gkT, s_gke, s_gatt, s_gam, s_gds, s_gst, s_go, s_gsq, s_gss, s_grs, s_gy, s_gyT = (sem(n) for n in (
            "gla_kend_transposed", "gla_kend_copied", "gla_scores", "gla_scores_masked", "gla_state_steps", "gla_states",
            "gla_out", "gla_squares", "gla_square_sums", "gla_rstd", "gla_y", "gla_y_transposed"))
        s_st0 = [sem(f"state_loaded{i}") for i in range(2)]
        s_y = sem("y_ready")
        s_kraw, s_rot, s_rope, s_kt, s_kc, s_qc = (sem(n) for n in (
            "attn_raw_copied", "attn_rotated", "attn_roped", "attn_keys_turned", "attn_keys_copied", "attn_prompt_copied"))
        s_sc, s_sce, s_nm, s_ex, s_p, s_pt, s_pte, s_ao = (sem(n) for n in (
            "attn_scores", "attn_scores_taken", "attn_max", "attn_exp", "attn_probs", "attn_probs_turned", "attn_pT_copied", "attn_out"))
        s_cc, s_cu, s_cy = sem("conv_c_copied"), sem("conv_u_ready"), sem("conv_y_taken")
        s_sig, s_zm, s_z = sem("merge_gate_ready"), sem("merge_branch_taken"), sem("z_ready")
        s_h2s = [sem(f"h2_stored{i}") for i in range(2)]
        s_x1, s_h2T, s_rl = sem("x_mixed"), sem("h2T_copied"), sem("router_logits")
        s_gx, s_gxe, s_rM, s_rk, s_info = sem("router_shifted"), sem("router_exps"), sem("routes_ready"), sem("ranks_ready"), sem("rounds_known")
        r_oh, r_idx, r_slots = sem("onehot_ready"), sem("slot_step_done"), sem("slots_ready")
        r_xg = [gather_sem(f"slot_rows_loaded{i}") for i in range(2)]
        r_hi, r_lo, r_used = sem("expert_unit_hi"), sem("expert_unit_lo"), sem("expert_unit_used")
        r_T, r_Thi, r_Tlo = sem("rows_transposed"), sem("xT_hi_ready"), sem("xT_ready")
        r_hg, r_hid, r_HT, r_hT = sem("expert_silu"), sem("expert_hidden"), sem("hidden_transposed"), sem("hidT_ready")
        r_yo = sem("expert_rows_copied")
        r_ys = [sem(f"expert_rows_stored{i}") for i in range(2)]
        s_yg = [gather_sem(f"token_rows_loaded{i}") for i in range(2)]
        r_first, r_added, s_done = sem("first_row_weighed"), sem("round_added"), sem("layer_done")
        s_fsd, s_fy = sem("final_root"), sem("final_ready")
        s_fg, s_out, s_sto = sem("final_gain_loaded"), sem("outputs_stored"), sem("states_stored")

        block = ctx.enter_context(nc.Block())

        w_in_u = a["w_in"].rearrange("l (k p) n -> p (l k) n", p=P)
        w_br_u = a["w_branch"].rearrange("l b (k p) n -> p (l b k) n", p=P)
        w_out_u = a["w_out"].rearrange("l (k p) n -> p (l k) n", p=P)
        w_ada_u = a["w_ada"].rearrange("l d n -> (l d) n")
        w_eg_u = a["w_exp_gate"].rearrange("l e (k p) f -> p (l e k) f", p=P)
        w_eu_u = a["w_exp_up"].rearrange("l e (k p) f -> p (l e k) f", p=P)
        w_ed_u = a["w_exp_down"].rearrange("l e (k p) n -> (l e k p) n", p=P)

        def u_cols(u):
            if u == U_LR:
                return KC * 2 * RANK
            if U_M <= u < U_OUT and (u - U_M) % 2 == 1:
                return 4 * P
            return 1024

        def set_semaphores(eng, i):
            for s in sems[i::5]:
                eng.sem_inc(s, SET)
            eng.drain()
            eng.sem_inc(s_start, 1)
            eng.wait_ge(s_start, 5)
            hold(eng)

        def raw_slot(j):
            return raw[:, j, :] if j < RAW else raw_more[:, j - RAW, :]

        def in_order(step):
            first = 4 if step % 2 else 10
            return [(first + q, q) for q in range(EXU // 2)]

        def expert_steps(eng, prologue, step, epilogue):
            prologue()
            step(0, 1, first=True)
            step(0, 2)
            hold(eng)
            with eng.Fori(1, NE // 2 - 1) as turn:
                step(turn, 1)
                step(turn, 2)
            step(NE // 2 - 1, 1, last=True)
            epilogue()

        def hold(eng):
            eng.sem_inc(s_held[eng.engine])

        def rounds_before(eng, l):
            hold(eng)
            return eng.value_load(info[0:1, ds(l * 2, 1)], min_val=0, max_val=5 * DEPTH)

        def rounds_now(eng, l):
            return eng.value_load(info[0:1, ds(l * 2 + 1, 1)], min_val=1, max_val=5)

        def span(b):
            if b == PT:
                return P, 2 * P
            return (P if b == 0 else 0), (3 * P if b == PT - 1 else 4 * P)

        def tiles_of(t):
            return (TILES + 1) // 2 if t % 2 == 0 else TILES // 2

        def h_tiles(b):
            return {3: (0, 1), 4: (2, 3), 5: (4,)}.get(b, ())

        def ktiles(b):
            lo_, hi_ = span(b)
            return (hi_ - lo_) // P

        @block.sync
        def _(sp):
            set_semaphores(sp, 0)
            sp.dma_start(con[:, :], a["table"][:, 0:CONST_RES]).then_inc(s_const, 16)
            tri_at = CONST["tri"][0]
            sp.dma_start(tri_in[:, :], a["table"][:, tri_at:tri_at + 2 * P]).then_inc(s_const, 16)
            sp.wait_ge(s_init, SET + 1)

            def feature_unit(l, u, col, width=P):
                slot = u % RAW
                dst = raw[:, slot, 0:KC * width].rearrange("p (k n) -> p k n", k=KC)
                return sp.dma_start(dst, w_in_u[:, ds(l * KC, KC), col:col + width])

            def token_unit(l, u, j, src, col):
                dst = raw[:, u % RAW, :].rearrange("p (k n) -> p k n", k=2)
                return sp.dma_start(dst, src[:, ds(l * KC + 2 * j, 2), col:col + 512])

            def free_slot(l, u):
                if u < RAW:
                    sp.wait_ge(s_ada, SET + l * ADA + ADA - RAW + u + 1)
                else:
                    sp.wait_ge(s_split, SET + l * UNITS + u - RAW + 1)

            with sp.Fori(0, DEPTH) as l:
                done = rounds_before(sp, l)
                for u in range(ADA):
                    b, k = u // KC, u % KC
                    if u < RAW:
                        sp.wait_ge(r_lo, SET + done * ROUND_UNITS + u + 1)
                    else:
                        sp.wait_ge(s_ada, SET + l * ADA + u - RAW + 1)
                    sp.dma_start(raw[:, u % RAW, :], w_ada_u[ds(l * D + k * P, P), b * D:(b + 1) * D]).then_inc(s_raw[u % RAW], 16)
                    if u == 2 * KC - 1:
                        sp.wait_ge(s_done, SET + l)
                        for g in range(2):
                            sp.dma_start(ada_b[g:g + 1, :, :], a["b_ada"][ds(l, 1), :].rearrange("l (b d) -> l b d", d=D)).then_inc(s_lay, 16)
                            for i, n in enumerate(("norm1_g", "norm2_g")):
                                sp.dma_start(ada_g[g:g + 1, i, :], a[n][ds(l, 1), :]).then_inc(s_lay, 16)
                for u in range(U_M):
                    free_slot(l, u)
                    if u == U_CONV + 2:
                        hold(sp)
                    if u < U_TV:
                        ins = token_unit(l, u, u % 4, w_in_u, C_GV if u < U_R else C_GR)
                    elif u == U_TV:
                        ins = feature_unit(l, u, C_TV)
                    elif u == U_LR:
                        ins = feature_unit(l, u, C_LF, 2 * RANK)
                    elif u < U_K:
                        h, i = divmod(u - U_GLA, 2)
                        ins = feature_unit(l, u, (C_GQ, C_GK)[i] + h * P)
                    elif u < U_Q:
                        kv = u - U_K
                        dst = raw[:, u % RAW, :].rearrange("p (k r n) -> p k r n", k=KC, r=2)
                        for r in range(2):
                            ins = sp.dma_start(dst[:, :, r, :], w_in_u[:, ds(l * KC, KC), C_TK + kv * HD:C_TK + (kv + 1) * HD])
                            if r == 0:
                                ins.then_inc(s_raw[u % RAW], 16)
                    elif u < U_CONV:
                        ins = feature_unit(l, u, C_TQ + (u - U_Q) * P)
                    else:
                        f, i = divmod(u - U_CONV, 3)
                        ins = feature_unit(l, u, (C_AC, C_AH, C_AB)[i] + f * P)
                    ins.then_inc(s_raw[u % RAW], 16)
                hold(sp)
                with sp.Fori(0, KC) as n:
                    for i in range(3):
                        for j in range(2):
                            slot = 2 * i + j
                            sp.wait_ge(s_split, SET + l * UNITS + U_M - RAW + n * 6 + slot + 1)
                            if j == 0:
                                dst = raw[:, slot, :].rearrange("p (k n) -> p k n", k=KC)
                                sp.dma_start(dst, w_in_u[:, ds(l * KC, KC), ds(n * P + (C_MA, C_MB, C_MC)[i], P)]).then_inc(s_raw[slot], 16)
                            else:
                                dst = raw[:, slot, 0:512].rearrange("p (k n) -> p k n", k=4)
                                sp.dma_start(dst, w_br_u[:, ds(l * 12 + 4 * i, 4), ds(n * P, P)]).then_inc(s_raw[slot], 16)
                for u in range(U_OUT, UNITS):
                    free_slot(l, u)
                    token_unit(l, u, (u - U_OUT) % 4, w_out_u, 512 * ((u - U_OUT) // 4)).then_inc(s_raw[u % RAW], 16)
                sp.wait_ge(s_info, SET + l + 1)
                done = rounds_before(sp, l)
                now = rounds_now(sp, l)
                sp.wait_ge(s_split, SET + (l + 1) * UNITS)
                for i in range(2):
                    sp.wait_ge(s_h2s[i], SET + 16 * tiles_of(i) * (l + 1))
                sp.wait_ge(s_hps, SET + (l + 1) * 2 * TILES)
                hold(sp)
                with sp.Fori(0, now) as r:
                    g = (done + r) * ROUND_UNITS

                    def load(turn, j, e, q):
                        sp.wait_ge(r_lo, SET + g + turn * EXU + j + 1)
                        dst = raw_slot(j % EXU)
                        if q < 4:
                            c = (l * NE + e) * KC + 2 * q
                            dst = dst.rearrange("p (k i f) -> p k i f", k=2, i=2)
                            sp.dma_start(dst[:, :, 0, :], w_eg_u[:, ds(c, 2), :]).then_inc(s_rawx[j % EXU], 16)
                            sp.dma_start(dst[:, :, 1, :], w_eu_u[:, ds(c, 2), :]).then_inc(s_rawx[j % EXU], 16)
                        else:
                            c = (l * NE + e) * 2 + q - 4
                            sp.dma_start(dst[:, 0:512], w_ed_u[ds(c * P, P), 0:512]).then_inc(s_rawx[j % EXU], 16)
                            sp.dma_start(dst[:, 512:], w_ed_u[ds(c * P, P), 512:D]).then_inc(s_rawx[j % EXU], 16)

                    def prologue():
                        for q in range(4):
                            load(0, q, 0, q)

                    def step(turn, i, first=False, last=False):
                        e = turn * 2 + i
                        for j, q in in_order(i):
                            load(turn, j, e if q < 4 else e - 1, q)

                    def epilogue():
                        for q in (4, 5):
                            load(NE // 2 - 1, 6 + q, NE - 1, q)

                    expert_steps(sp, prologue, step, epilogue)
            sp.wait_ge(s_done, SET + DEPTH)
            sp.dma_start(gt[:, 0, :], a["final_norm_g"].rearrange("(o d) -> o d", o=1).broadcast_to([P, D])).then_inc(s_fg, 16)
            for t in range(TILES):
                sp.wait_ge(s_fy, SET + t + 1)
                dst = out_ys[0, t * P:(t + 1) * P, :] if t < PT else out_yp[0]
                sp.dma_start(dst, x[:, t, :]).then_inc(s_out, 16)
            sp.wait_ge(s_out, SET + 16 * (TILES + 2 * DEPTH))
            sp.wait_ge(s_sto, SET + 16 * 2 * HEADS * DEPTH)

        def raw_value(l, u):
            slot = u % RAW
            fills = ADA // RAW
            per_layer = fills + sum(1 + (U_K <= v < U_Q) for v in range(UNITS) if v % RAW == slot)
            here = fills + sum(1 + (U_K <= v < U_Q) for v in range(u + 1) if v % RAW == slot)
            return l * (16 * per_layer) + 16 * here

        @block.gpsimd
        def _(pool):
            set_semaphores(pool, 1)
            nc.gpsimd.memset(info[:, :], 0).then_inc(s_init, 1)

            def split(l, u, value=None, cols=None):
                slot, ring = u % RAW, u % SPL
                n = u_cols(u) if cols is None else cols
                pool.wait_ge(s_raw[slot], SET + (raw_value(l, u) if value is None else value[0]))
                if value is None:
                    if u >= SPL:
                        pool.wait_ge(s_used, SET + l * UNITS + u - SPL + 1)
                else:
                    pool.wait_ge(s_used, SET + value[1])
                hold(pool)
                nc.gpsimd.tensor_copy(w_hi[:, ring, 0:n], raw[:, slot, 0:n])
                pool.drain()
                nc.gpsimd.tensor_tensor(w_lo[:, ring, 0:n], raw[:, slot, 0:n], w_hi[:, ring, 0:n].bitcast(F32),
                                        ALU.subtract).then_inc(s_split, 1)

            with pool.Fori(0, DEPTH) as l:
                pool.wait_ge(s_done, SET + l)
                for u in range(U_M):
                    split(l, u)
                hold(pool)
                with pool.Fori(0, KC) as n:
                    for j in range(6):
                        split(l, U_M + j, (raw_value(l, U_M + j) + n * 16, l * UNITS + U_M + n * 6 + j - SPL + 1),
                              u_cols(U_M + j))
                for u in range(U_OUT, UNITS):
                    split(l, u)
                pool.wait_ge(s_info, SET + l + 1)
                done = rounds_before(pool, l)
                now = rounds_now(pool, l)
                for i in range(2):
                    pool.wait_ge(s_h2s[i], SET + 16 * tiles_of(i) * (l + 1))
                hold(pool)
                with pool.Fori(0, now) as r:
                    g = done + r
                    pool.wait_ge(r_slots, SET + 2 * g + 2)
                    for e in range(NE):
                        if e >= 2:
                            pool.wait_ge(r_T, SET + g * NE + e - 1)
                        else:
                            pool.wait_ge(r_T, SET + g * NE)
                        hold(pool)
                        nc.gpsimd.indirect_dma_start(
                            out=xg[:, e % 2, :], out_offset=None, in_=h2_d,
                            in_offset=bass.IndirectOffsetOnAxis(ap=sidx[:, e:e + 1].bitcast(U32), axis=0)).then_inc(r_xg[e % 2], 16)
                    for i in range(2):
                        pool.wait_ge(r_ys[i], SET + (g + 1) * (16 * NE // 2))
                    for t in range(TILES):
                        if t >= 2:
                            pool.wait_ge(r_added, SET + g * TILES + t - 1)
                        for k in range(2):
                            hold(pool)
                            nc.gpsimd.indirect_dma_start(
                                out=yg[:, t % 2, k, :], out_offset=None, in_=ye_d,
                                in_offset=bass.IndirectOffsetOnAxis(ap=pos[:, k, t:t + 1].bitcast(U32), axis=0)).then_inc(s_yg[t % 2], 16)

        @block.scalar
        def _(act):
            set_semaphores(act, 2)
            A = nc.scalar.activation
            for g, c in ((0, a["c"][0, :]), (1, a["c_ctx"])):
                for k in range(KC):
                    act.dma_start(condT[:, k, g:g + 1], c[k * P:(k + 1) * P].rearrange("(p o) -> p o", o=1)).then_inc(s_c0, 16)
            xs = a["x_sample"].rearrange("b (t p) d -> p (b t) d", p=P)
            act.dma_start(x[:, 0:PT, :], xs).then_inc(s_x0, 16)
            act.dma_start(x[:, PT, :], a["x_prompt"][0]).then_inc(s_x0, 16)
            act.wait_ge(s_const, SET + 32)
            act.wait_ge(s_c0, SET + 16 * 2 * KC)
            A(condT[:, :, :], condT[:, :, :], ACT.Silu).then_inc(s_cond, 1)

            def roots(l, which):
                for t in range(TILES):
                    act.drain()
                    if which == 1:
                        act.wait_ge(s_x1, SET + l * 2 * TILES + TILES + t + 1)
                    A(junk[:, :], x[:, t, :], ACT.Square, accum_out=ss[:, t:t + 1])
                act.drain()
                A(sd, ss, ACT.Sqrt, bias=eps, scale=1.0 / D).then_inc(s_sd, 1)

            act.wait_ge(s_x0, SET + 32)
            act.drain()
            with act.Fori(0, DEPTH) as l:
                act.wait_ge(s_done, SET + l)
                hold(act)
                roots(l, 0)
                for b in range(ADA_BLOCKS):
                    act.wait_ge(s_mrow, SET + l * ADA_BLOCKS + b + 1)
                    act.dma_start(mod_d[b], mrow[:, b % 2, :]).then_inc(s_mst[b % 2], 16)
                    if b == 1:
                        act.wait_ge(s_mst[0], SET + 16 * (l * 3 + 1))
                        act.wait_ge(s_mst[1], SET + 16 * (l * 3 + 1))
                        for g in range(2):
                            act.dma_start(modB[:, g, :], mod_d[0, g:g + 1, :].broadcast_to([P, D])).then_inc(s_modl, 16)
                            act.dma_start(modA[:, g, :], mod_d[1, g:g + 1, :].broadcast_to([P, D])).then_inc(s_modl, 16)
                    for t in h_tiles(b):
                        act.wait_ge(s_hps, SET + l * 2 * TILES + t + 1)
                        nc.scalar.copy(hT_hi[:, :, t * P:(t + 1) * P], pair(2 + t % 2, 1024).rearrange("p (k n) -> p k n", k=KC)).then_inc(s_hhi, 1)
                act.dma_start(x_d.rearrange("(t p) d -> p t d", p=P), x[:, :, :]).then_inc(s_xsav, 16)
                act.dma_start(g_norm[:, :], a["gla_norm_g"][ds(l, 1), :].broadcast_to([P, HEADS * DV])).then_inc(s_lay2, 16)
                act.dma_start(cossin[:, :, :], a["table"][:, CONST["cos"][0]:CONST["cos"][0] + 2 * SAMPLE]).then_inc(s_lay2, 16)
                act.dma_start(cv[:, :], a["cache_v"].rearrange("b l p k d -> p (b l) (k d)")[:, ds(l, 1), :]).then_inc(s_lay2, 16)
                for kv in range(KVH):
                    for r in range(2):
                        act.dma_start(ckd[:, kv, r, :], a["cache_k"].rearrange("b l p k d -> p (b l) (k d)")[
                            :, ds(l, 1), kv * HD:(kv + 1) * HD]).then_inc(s_lay2, 16)
                for d in range(2):
                    for o in range(2):
                        if o == d:
                            act.dma_start(w_gate[RANK * o:RANK * (o + 1), d, :], a["gla_w_gate"].rearrange(
                                "l d r n -> (l d r) n")[ds(l * 2 * RANK + d * RANK, RANK), :]).then_inc(s_lay2, 16)
                        else:
                            act.dma_start(w_gate[RANK * o:RANK * (o + 1), d, :], a["zeros"][0:RANK, :]).then_inc(s_lay2, 16)
                    act.dma_start(b_gate[:, d, :], a["gla_b_gate"].rearrange("l d (c p) -> p (l d) c", p=P)[
                        :, ds(l * 2 + d, 1), :]).then_inc(s_lay2, 16)
                for j in range(CONV_K):
                    act.dma_start(conv_w[:, :, j], a["conv_w"].rearrange("l j (c p) -> p (l j) c", p=P)[
                        :, ds(l * CONV_K + j, 1), :]).then_inc(s_lay2, 16)
                act.dma_start(sink[:, :], a["attn_sink"][ds(l, 1), :].broadcast_to([P, AH])).then_inc(s_lay2, 16)
                act.dma_start(w_rt[:, :, 0:NG], a["w_route_group"].rearrange("l (k p) n -> p (l k) n", p=P)[
                    :, ds(l * KC, KC), :]).then_inc(s_lay2, 16)
                act.dma_start(w_rt[:, :, NG:], a["w_route_expert"].rearrange("l (k p) n -> p (l k) n", p=P)[
                    :, ds(l * KC, KC), :]).then_inc(s_lay2, 16)
                act.dma_start(b_rt[:, 0:NG], a["b_route_group"][ds(l, 1), :].broadcast_to([P, NG])).then_inc(s_lay2, 16)
                act.dma_start(b_rt[:, NG:], a["b_route_expert"][ds(l, 1), :].broadcast_to([P, NE])).then_inc(s_lay2, 16)
                for i in range(2):
                    act.wait_ge(s_mst[i], SET + 16 * 3 * (l + 1))
                act.wait_ge(s_used, SET + l * UNITS + U_V + 4)
                for t in range(TILES):
                    nc.scalar.copy(v_sb[:, t, :], ps[:, t, :]).then_inc(s_v, 1)
                act.wait_ge(s_used, SET + l * UNITS + U_R + 4)
                for t in range(TILES):
                    A(rg[:, t, :], ps[:, (5 + t) % 8, :], ACT.Silu).then_inc(s_r, 1)
                act.wait_ge(s_used, SET + l * UNITS + U_TV + 1)
                nc.scalar.copy(tv[:, :, :], pair(1).rearrange("p (t n) -> p t n", n=P)).then_inc(s_tv, 1)
                act.wait_ge(s_used, SET + l * UNITS + U_LR + 1)
                nc.scalar.copy(in_two(lrT[:, :]), two(2, 2 * RANK)).then_inc(s_lr, 1)
                act.wait_ge(s_tv, SET + l + 1)
                act.dma_start(out_cv[0, ds(l, 1)].rearrange("l p k d -> p (l k d)"), tv[:, PT, :]).then_inc(s_out, 16)
                act.wait_ge(s_hT, SET + (l + 1) * TILES)
                act.wait_ge(s_xsav, SET + 16 * (l + 1))
                act.dma_start(scanm[:, :], a["table"][:, CONST["scan"][0]:CONST["scan"][0] + TOK]).then_inc(s_lay3, 16)

                def q_k(h):
                    act.wait_ge(s_used, SET + l * UNITS + U_GLA + 2 * h + 1)
                    act.wait_ge(s_gin, SET + 2 * (l * HEADS + max(h - 1, 0)))
                    A(in_two(qs[h % 2][:, :]), two(3), ACT.Copy, scale=float(DK) ** -0.5).then_inc(s_gqk, 1)
                    act.wait_ge(s_used, SET + l * UNITS + U_GLA + 2 * h + 2)
                    nc.scalar.copy(in_two(ks[h % 2][:, :]), two(2)).then_inc(s_gqk, 1)

                for h in range(HEADS):
                    for d in range(2):
                        act.wait_ge(s_go, SET + l * HEADS + h)
                        act.wait_ge(s_sto, SET + 16 * (l * 2 * HEADS + 2 * h))
                        act.dma_start(st[d][:, 0, :], a["state_gla"].rearrange("b l d h k v -> k (b l d h) v")[
                            :, ds(l * 2 * HEADS + d * HEADS + h, 1), :]).then_inc(s_st0[d], 16)
                    hh = l * HEADS + h
                    for d in range(2):
                        act.wait_ge(s_gzb, SET + hh * 2 + d + 1)
                        A(sp_[:, d, :], zb[:, d, :], ACT.Abs)
                        act.drain()
                        A(sp_[:, d, :], sp_[:, d, :], ACT.Exp, scale=-1.0)
                        act.drain()
                        A(sp_[:, d, :], sp_[:, d, :], ACT.Ln, bias=one).then_inc(s_gsp, 1)
                    for d in range(2):
                        act.wait_ge(s_gcb, SET + hh * 2 + d + 1)
                        A(E_[:, d, :], cb[:, d, :], ACT.Exp, scale=1.0 / TAU)
                        A(En[:, d, :], cb[:, d, :], ACT.Exp, scale=-1.0 / TAU).then_inc(s_gE, 1)
                    q_k(h)
                    for d in range(2):
                        act.wait_ge(s_gkT, SET + hh * 2 + d + 1)
                        nc.scalar.copy(zb[:, d, :], pair(2 + d)).then_inc(s_gke, 1)
                    for d in range(2):
                        act.wait_ge(s_gst, SET + hh * 2 + d + 1)
                        act.dma_start(out_st[0, ds(l, 1), d, h].rearrange("l k v -> k (l v)"), st[d][:, SCH + 3, :]).then_inc(s_sto, 16)
                    act.wait_ge(s_go, SET + hh + 1)
                    A(osq[:, :, :], pair(3).rearrange("p (t n) -> p t n", n=DV), ACT.Square).then_inc(s_gsq, 1)
                    act.wait_ge(s_gss, SET + hh + 1)
                    A(g_ln, g_ss, ACT.Ln, bias=eps, scale=1.0 / DV)
                    act.drain()
                    A(g_rs, g_ln, ACT.Exp, scale=-0.5).then_inc(s_grs, 1)
                for kv in range(KVH):
                    j = l * (KVH + 4) + kv
                    act.drain()
                    act.wait_ge(s_y, SET + l * 12 + HEADS)
                    act.wait_ge(s_used, SET + l * UNITS + U_K + kv + 1)
                    act.wait_ge(s_rope, SET + j)
                    act.wait_ge(s_kt, SET + l * KVH + kv)
                    nc.scalar.copy(in_two(qraw[:, :]), two(0)).then_inc(s_kraw, 1)
                    act.drain()
                    nc.scalar.copy(kT[:, kv, P + SAMPLE:], qraw[:, SAMPLE:])
                    act.wait_ge(s_kt, SET + l * KVH + kv + 1)
                    nc.scalar.copy(kT[:, kv, 0:P], ps[:, 5, 0:P])
                    nc.scalar.copy(kout[:, kv, :], ps[:, 5, P:P + HD]).then_inc(s_kc, 1)
                act.wait_ge(s_kc, SET + (l + 1) * KVH)
                act.dma_start(out_ck[0, ds(l, 1)].rearrange("l p k d -> p (l k d)"), kout[:, :, :]).then_inc(s_out, 16)

                def q_chunk(c):
                    j = l * (KVH + 4) + KVH + c
                    act.drain()
                    act.wait_ge(s_used, SET + l * UNITS + U_Q + c + 1)
                    act.wait_ge(s_rope, SET + j)
                    nc.scalar.copy(in_two(qraw[:, :]), two(0)).then_inc(s_kraw, 1)
                    act.drain()
                    if c >= 2:
                        act.wait_ge(s_sc, SET + (l * AH + 2 * (c - 1)) * TILES)
                    nc.scalar.copy(qT[:, c % 2, SAMPLE:], qraw[:, SAMPLE:]).then_inc(s_qc, 1)

                def exps(hd):
                    i, b_ = hd % 2, l * AH + hd
                    act.wait_ge(s_nm, SET + b_ + 1)
                    for b in range(TILES):
                        lo_, hi_ = span(b)
                        A(s_sb[:, i, b, lo_:hi_], s_sb[:, i, b, lo_:hi_], ACT.Exp, bias=a_nm[i][:, b:b + 1], accum_out=a_rs[i][:, b:b + 1])
                    A(a_es[i], a_nm[i], ACT.Exp, bias=sink[:, hd:hd + 1]).then_inc(s_ex, 1)

                def probs_copy(hd):
                    b_ = l * AH + hd
                    for b in range(TILES):
                        n = ktiles(b) * P
                        act.drain()
                        act.wait_ge(s_pt, SET + b_ * TILES + b + 1)
                        nc.scalar.copy(pT[:, b % 2, 0:n], ps[:, 2 + b % 2, 0:n]).then_inc(s_pte, 1)

                q_chunk(0)
                exps(0)
                for hd in range(0, AH, 2):
                    exps(hd + 1)
                    if hd < AH - 2:
                        q_chunk(hd // 2 + 1)
                    probs_copy(hd)
                    probs_copy(hd + 1)
                    if hd < AH - 2:
                        exps(hd + 2)
                for f in range(4):
                    act.drain()
                    act.wait_ge(s_y, SET + l * 12 + HEADS + 4)
                    act.wait_ge(s_used, SET + l * UNITS + U_CONV + 3 * f + 1)
                    act.wait_ge(s_cu, SET + l * 4 + f)
                    nc.scalar.copy(in_two(csb[:, :]), two((3 * f) % 4)).then_inc(s_cc, 1)
                hold(act)
                with act.Fori(0, KC) as n:
                    for i in range(3):
                        act.drain()
                        act.wait_ge(s_used, SET + l * UNITS + U_M + n * 6 + 2 * i + 1)
                        if i == 0:
                            act.wait_ge(s_y, SET + (l + 1) * 12)
                        act.wait_ge(s_zm, SET + (l * KC + n) * 3)
                        A(in_two(sg[:, i, :]), two((2 * i) % 4), ACT.Sigmoid).then_inc(s_sig, 1)
                act.wait_ge(s_used, SET + l * UNITS + U_OUT)
                act.dma_start(x[:, :, :], x_d.rearrange("(t p) d -> p t d", p=P)).then_inc(s_xload, 16)
                for g in range(2):
                    act.dma_start(gt[:, g, :], mod_d[2, g:g + 1, :].broadcast_to([P, D])).then_inc(s_gtl, 16)
                    act.dma_start(modB[:, g, :], mod_d[3, g:g + 1, :].broadcast_to([P, D])).then_inc(s_modl, 16)
                    act.dma_start(modA[:, g, :], mod_d[4, g:g + 1, :].broadcast_to([P, D])).then_inc(s_modl, 16)
                roots(l, 1)
                for g in range(2):
                    act.dma_start(gt[:, g, :], mod_d[5, g:g + 1, :].broadcast_to([P, D])).then_inc(s_gtl, 16)
                for t in range(TILES):
                    act.wait_ge(s_h, SET + (l * 2 + 1) * TILES + t + 1)
                    act.dma_start(h2_d[t * P:(t + 1) * P, :], hbuf[:, t % 2, :]).then_inc(s_h2s[t % 2], 16)
                    act.drain()
                    act.wait_ge(s_hps, SET + (l * 2 + 1) * TILES + t + 1)
                    if t >= 2:
                        act.wait_ge(s_rl, SET + l * TILES + t - 1)
                    nc.scalar.copy(h2T[:, t % 2, :, :], pair(t % 2, 1024).rearrange("p (k n) -> p k n", k=KC)).then_inc(s_h2T, 1)
                act.wait_ge(s_gx, SET + l + 1)
                A(gex[:, :, :], gex[:, :, :], ACT.Exp)
                A(e21[:, :, :], e21[:, :, :], ACT.Exp).then_inc(s_gxe, 1)
                act.wait_ge(s_info, SET + l + 1)
                done = rounds_before(act, l)
                now = rounds_now(act, l)
                hold(act)
                with act.Fori(0, now) as r:
                    act.wait_ge(r_added, SET + (done + r) * TILES)

                    g = done + r

                    def half(turn, j):
                        act.wait_ge(s_rawx[j % EXU], SET + (g * (NE // 2) + turn + j // EXU + 1) * 32)
                        act.wait_ge(r_used, SET + g * ROUND_UNITS + turn * EXU + j + 1)
                        nc.scalar.copy(w_hi[:, j % SPL, :], raw_slot(j % EXU)).then_inc(r_hi, 1)

                    def turned_rows(turn, e):
                        act.wait_ge(r_T, SET + g * NE + turn * 2 + e + 1)
                        nc.scalar.copy(xT_hi[:, e % 2, :, :], pair(0, 1024).rearrange("p (k n) -> p k n", k=KC)).then_inc(r_Thi, 1)

                    def silu(turn, e, used):
                        act.wait_ge(r_used, SET + SPL + g * ROUND_UNITS + turn * EXU + used)
                        A(hg[:, e % 2, :], ps[:, 4 + e % 2, 0:FE], ACT.Silu).then_inc(r_hg, 1)

                    def result(turn, e):
                        act.wait_ge(r_used, SET + SPL + g * ROUND_UNITS + turn * EXU + (10 + 6 * e if e < 1 else EXU))
                        act.wait_ge(r_ys[e % 2], SET + (g * (NE // 2) + turn + e // 2) * 16)
                        nc.scalar.copy(yo[:, e % 2, :], pair(1, 1024)).then_inc(r_yo, 1)
                        act.wait_ge(r_yo, SET + g * NE + turn * 2 + e + 1)
                        act.dma_start(ye_d[ds((turn * 2 + e) * SLOTS, SLOTS), :], yo[:, e % 2, :]).then_inc(r_ys[e % 2], 16)

                    def prologue():
                        turned_rows(0, 0)
                        for q in range(4):
                            half(0, q)
                        silu(0, 0, 4)
                        turned_rows(0, 1)

                    def step(turn, i, first=False, last=False):
                        units = in_order(i)
                        for j, q in units[:2]:
                            half(turn, j)
                        if not first:
                            result(turn, i - 2)
                        for j, q in units[2:]:
                            half(turn, j)
                        silu(turn, i, units[3][0] + 1)
                        if not last:
                            turned_rows(turn, i + 1)

                    def epilogue():
                        for j in (10, 11):
                            half(NE // 2 - 1, j)
                        result(NE // 2 - 1, 0)
                        result(NE // 2 - 1, 1)

                    expert_steps(act, prologue, step, epilogue)
                    for t in range(TILES):
                        act.drain()
                        act.wait_ge(s_yg[t % 2], 32 * (g * tiles_of(t) + t // 2 + 1))
                        A(yg[:, t % 2, 0, :], yg[:, t % 2, 0, :], ACT.Copy, scale=wsel[:, 0, t:t + 1]).then_inc(r_first, 1)
            for t in range(TILES):
                act.drain()
                act.wait_ge(s_done, SET + DEPTH)
                A(junk[:, :], x[:, t, :], ACT.Square, accum_out=ss[:, t:t + 1])
            act.drain()
            A(sd, ss, ACT.Sqrt, bias=eps, scale=1.0 / D).then_inc(s_fsd, 1)

        @block.vector
        def _(dve):
            dve.sem_inc(r_lo, EXU)
            set_semaphores(dve, 3)
            V = nc.vector
            gl = lambda t: 0 if t < PT else 1

            def norm_tile(l, which, t):
                if t >= 2:
                    dve.wait_ge(s_hps, SET + (l * 2 + which) * TILES + t - 1)
                    if which:
                        dve.wait_ge(s_h2s[t % 2], SET + 16 * (l * tiles_of(t) + t // 2))
                V.scalar_tensor_tensor(hbuf[:, t % 2, :], x[:, t, :], rstd[:, t:t + 1], modA[:, gl(t), :], ALU.mult, ALU.mult)
                dve.drain()
                V.tensor_tensor(hbuf[:, t % 2, :], hbuf[:, t % 2, :], modB[:, gl(t), :], ALU.add).then_inc(s_h, 1)

            dve.wait_ge(s_const, SET + 32)
            dve.wait_ge(s_x0, SET + 32)
            V.tensor_copy(tri_b[:, :], tri_in[:, :])
            V.tensor_copy(tok_b[:, :, :], C("tokid").rearrange("p (t i) -> p t i", i=2))
            with dve.Fori(0, DEPTH) as l:

                def hT_low(t):
                    dve.wait_ge(s_hhi, SET + l * TILES + t + 1)
                    V.tensor_tensor(hT_lo[:, :, t * P:(t + 1) * P], pair(2 + t % 2, 1024).rearrange("p (k n) -> p k n", k=KC),
                                    hT_hi[:, :, t * P:(t + 1) * P].bitcast(F32), ALU.subtract).then_inc(s_hT, 1)

                for b in range(ADA_BLOCKS):
                    dve.drain()
                    dve.wait_ge(s_lay, SET + (l + 1) * 16 * 6)
                    dve.wait_ge(s_ada, SET + l * ADA + KC * (b + 1))
                    dve.wait_ge(s_mst[b % 2], SET + 16 * (l * 3 + b // 2))
                    ins = V.tensor_tensor(mrow[:, b % 2, :], pair(b % 2, 1024, 2), ada_b[:, b, :], ALU.add)
                    if b % 3 == 1:
                        dve.drain()
                        ins = V.scalar_tensor_tensor(mrow[:, b % 2, :], mrow[:, b % 2, :], 1.0, ada_g[:, b // 3, :], ALU.add, ALU.mult)
                    ins.then_inc(s_mrow, 1)
                    if b == 2:
                        dve.wait_ge(s_sd, SET + l * 2 + 1)
                        V.reciprocal(rstd, sd)
                        dve.drain()
                        dve.wait_ge(s_modl, SET + 16 * 8 * l + 64)
                        norm_tile(l, 0, 0)
                        norm_tile(l, 0, 1)
                    for t in h_tiles(b):
                        hT_low(t)
                        if t + 2 < TILES:
                            norm_tile(l, 0, t + 2)
                dve.wait_ge(s_lay2, SET + (l + 1) * 16 * 21)
                for t in range(TILES):
                    dve.wait_ge(s_r, SET + l * TILES + t + 1)
                    V.tensor_tensor(rg[:, t, :], rg[:, t, :], g_norm[:, :], ALU.mult)
                dve.drain()
                dve.wait_ge(s_lay3, SET + (l + 1) * 16)
                dve.wait_ge(s_xsav, SET + 16 * (l + 1))
                for d in range(2):
                    V.memset(st[d][:, SCH + 1, :], 0.0)
                    V.memset(attm[:, d, :, :], 0.0)

                def biased(h, d):
                    dve.drain()
                    dve.wait_ge(s_gz, SET + (l * HEADS + h) * 2 + d + 1)
                    V.tensor_scalar(in_two(zb[:, d, :]), two(d), b_gate[:, d, h:h + 1], None, ALU.add).then_inc(s_gzb, 1)

                biased(0, 0)
                biased(0, 1)
                for h in range(HEADS):
                    hh = l * HEADS + h
                    for d in range(2):
                        dve.wait_ge(s_gsp, SET + hh * 2 + d + 1)
                        V.scalar_tensor_tensor(zb[:, d, :], zb[:, d, :], 0.0, sp_[:, d, :], ALU.min, ALU.subtract)
                        dve.drain()
                        if d == 0:
                            V.tensor_tensor_scan(cb[:, d, :], scanm[:, :], zb[:, d, :], 0.0, ALU.mult, ALU.add).then_inc(s_gcb, 1)
                        else:
                            V.tensor_tensor_scan(cb[:, d, ::-1], scanm[:, :], zb[:, d, ::-1], 0.0, ALU.mult, ALU.add).then_inc(s_gcb, 1)
                    for d in range(2):
                        dve.wait_ge(s_gqk, SET + hh * 2 + 2)
                        dve.wait_ge(s_gE, SET + hh * 2 + d + 1)
                        V.tensor_tensor(cb[:, d, :], qs[h % 2][:, :], E_[:, d, :], ALU.mult)
                        V.tensor_tensor(En[:, d, :], ks[h % 2][:, :], En[:, d, :], ALU.mult)
                        dve.drain()
                        last = CHUNK - 1 if d == 0 else 0
                        ev = E_[:, d, :].rearrange("p (n c) -> p n c", c=CHUNK)[:, :, last:last + 1].broadcast_to([P, NCH, CHUNK])
                        V.tensor_tensor(sp_[:, d, :].rearrange("p (n c) -> p n c", c=CHUNK), En[:, d, :].rearrange("p (n c) -> p n c", c=CHUNK),
                                        ev, ALU.mult).then_inc(s_gin, 1)
                    for d in range(2):
                        dve.wait_ge(s_gatt, SET + hh * 2 + d + 1)
                        hold(dve)
                        for o in (0, CHUNK):
                            c = slice(o, o + CHUNK)
                            m = C(("fwd", "bwd")[d])[c, :].bitcast(I32).rearrange("p (o c) -> p o c", o=1).broadcast_to([CHUNK, TILES, CHUNK])
                            ins = V.copy_predicated(attm[c, d, :, c], m, pair(d)[c, :].rearrange("p (t c) -> p t c", c=P)[:, :, c])
                        ins.then_inc(s_gam, 1)
                    for d in range(2):
                        dve.drain()
                        dve.wait_ge(s_gds, SET + hh * 4 + 2 * d + 2)
                        dve.wait_ge(s_st0[d], SET + 16 * (hh + 1))
                        dst_ = psf[:, 1536 * d:1536 * d + NCH * DV].rearrange("p (n v) -> p n v", v=DV)
                        steps = [(i, i if d == 0 else SCH - 1 - i) for i in range(SCH - 1)]
                        steps += [(SCH + 1 + i, SCH + i if d == 0 else NCH - 1 - i) for i in range(2)]
                        for q, (i, n) in enumerate(sorted(steps, key=lambda s: s[0] % (SCH + 1))):
                            if q:
                                dve.drain()
                            e_col = n * CHUNK + (CHUNK - 1 if d == 0 else 0)
                            ins = V.scalar_tensor_tensor(st[d][:, i + 1, :], st[d][:, i, :], E_[:, d, e_col:e_col + 1], dst_[:, n, :], ALU.mult, ALU.add)
                        ins.then_inc(s_gst, 1)
                    dve.wait_ge(s_gsq, SET + hh + 1)
                    V.tensor_reduce(g_ss, osq[:, :, :], AX.X, ALU.add).then_inc(s_gss, 1)
                    if h + 1 < HEADS:
                        biased(h + 1, 0)
                    dve.wait_ge(s_grs, SET + hh + 1)
                    for t in range(TILES):
                        ins = V.scalar_tensor_tensor(yb[:, t, :], pair(3)[:, t * DV:(t + 1) * DV], g_rs[:, t:t + 1], rg[:, t, h * DV:(h + 1) * DV],
                                                     ALU.mult, ALU.mult)
                    ins.then_inc(s_gy, 1)
                    if h + 1 < HEADS:
                        biased(h + 1, 1)
                    dve.wait_ge(s_gyT, SET + hh + 1)
                    V.tensor_copy(yT_hi[:, 4 + h, :], pair(2))
                    dve.drain()
                    V.tensor_tensor(yT_lo[:, 4 + h, :], pair(2), yT_hi[:, 4 + h, :].bitcast(F32), ALU.subtract).then_inc(s_y, 1)

                dve.drain()
                for i in range(2):
                    V.memset(s_sb[:, i, 0, 0:P], -BIG)
                    V.memset(s_sb[:, i, PT - 1, 3 * P:], -BIG)
                    V.memset(s_sb[:, i, PT, 0:P], -BIG)
                    V.memset(s_sb[:, i, PT, 2 * P:], -BIG)

                def rope(j, dst):
                    dve.drain()
                    dve.wait_ge(s_kraw, SET + l * (KVH + 4) + j + 1)
                    V.tensor_tensor(rt1[:, :], qraw[:, 0:SAMPLE], cossin[:, 0, :], ALU.mult)
                    dve.wait_ge(s_rot, SET + l * (KVH + 4) + j + 1)
                    V.tensor_tensor(rt2[:, :], ps[:, 4, :], cossin[:, 1, :], ALU.mult)
                    dve.drain()
                    V.tensor_tensor(dst, rt1[:, :], rt2[:, :], ALU.add).then_inc(s_rope, 1)

                rope(0, kT[:, 0, P:P + SAMPLE])
                rope(1, kT[:, 1, P:P + SAMPLE])
                rope(2, qT[:, 0, 0:SAMPLE])

                def scores(hd):
                    i, b_ = hd % 2, l * AH + hd
                    if hd >= 2:
                        dve.wait_ge(s_pt, SET + (b_ - 1) * TILES)
                    for b in range(TILES):
                        lo_, hi_ = span(b)
                        dve.wait_ge(s_sc, SET + b_ * TILES + b + 1)
                        V.scalar_tensor_tensor(s_sb[:, i, b, lo_:hi_], ps[:, 5 + b % 2, lo_:hi_], float(HD) ** -0.5, strip[:, lo_:hi_],
                                               ALU.mult, ALU.add).then_inc(s_sce, 1)

                def maxima(hd):
                    i = hd % 2
                    dve.drain()
                    V.tensor_reduce(a_mx, s_sb[:, i, :, :], AX.X, ALU.max)
                    dve.drain()
                    V.tensor_scalar(a_nm[i], a_mx, sink[:, hd:hd + 1], -1.0, ALU.max, ALU.mult).then_inc(s_nm, 1)

                def normalise(hd):
                    i = hd % 2
                    dve.wait_ge(s_ex, SET + l * AH + hd + 1)
                    V.tensor_tensor(a_rd, a_rs[i], a_es[i], ALU.add)
                    dve.drain()
                    V.reciprocal(a_rd, a_rd)
                    dve.drain()
                    for b in range(TILES):
                        lo_, hi_ = span(b)
                        ins = V.tensor_scalar(s_sb[:, i, b, lo_:hi_], s_sb[:, i, b, lo_:hi_], a_rd[:, b:b + 1], None, ALU.mult)
                    ins.then_inc(s_p, 1)

                def take_y(c):
                    dve.wait_ge(s_ao, SET + l * 4 + c + 1)
                    dve.wait_ge(s_sto, SET + 16 * 2 * HEADS * (l + 1))
                    V.tensor_copy(yT_hi[:, 8 + c, 0:SAMPLE], ps[:, 7, :])
                    V.tensor_copy(yT_hi[:, 8 + c, SAMPLE:], ps[:, 1, 384:512])
                    dve.drain()
                    V.tensor_tensor(yT_lo[:, 8 + c, 0:SAMPLE], ps[:, 7, :], yT_hi[:, 8 + c, 0:SAMPLE].bitcast(F32), ALU.subtract)
                    V.tensor_tensor(yT_lo[:, 8 + c, SAMPLE:], ps[:, 1, 384:512], yT_hi[:, 8 + c, SAMPLE:].bitcast(F32), ALU.subtract).then_inc(s_y, 1)

                scores(0)
                maxima(0)
                for hd in range(0, AH, 2):
                    scores(hd + 1)
                    if hd >= 2:
                        take_y(hd // 2 - 1)
                    normalise(hd)
                    maxima(hd + 1)
                    if hd < AH - 2:
                        rope(3 + hd // 2, qT[:, (hd // 2 + 1) % 2, 0:SAMPLE])
                    normalise(hd + 1)
                    if hd < AH - 2:
                        scores(hd + 2)
                        maxima(hd + 2)
                take_y(AH // 2 - 1)
                dve.drain()
                for z in (0, SAMPLE + 1, SAMPLE + 2, TOK + 3):
                    V.memset(upad[:, z:z + 1], 0.0)
                for f in range(4):
                    dve.drain()
                    dve.wait_ge(s_cc, SET + l * 4 + f + 1)
                    dve.wait_ge(s_used, SET + l * UNITS + U_CONV + 3 * f + 2)
                    hp = two((3 * f + 1) % 4)
                    V.tensor_tensor(upad[:, 1:HT + 1], hp[:, 0, :], csb[:, 0:HT], ALU.mult)
                    V.tensor_tensor(upad[:, HT + 1:SAMPLE + 1], hp[:, 1, 0:SAMPLE - HT], csb[:, HT:SAMPLE], ALU.mult)
                    V.tensor_tensor(upad[:, SAMPLE + 3:TOK + 3], hp[:, 1, SAMPLE - HT:], csb[:, SAMPLE:], ALU.mult).then_inc(s_cu, 1)
                    dve.drain()
                    for j in range(CONV_K):
                        for a0, u0, n in ((0, 0, SAMPLE), (SAMPLE, SAMPLE + 2, PROMPT)):
                            if j == 0:
                                V.tensor_scalar(yf[:, a0:a0 + n], upad[:, u0:u0 + n], conv_w[:, f, 0:1], None, ALU.mult)
                            else:
                                V.scalar_tensor_tensor(yf[:, a0:a0 + n], upad[:, u0 + j:u0 + j + n], conv_w[:, f, j:j + 1], yf[:, a0:a0 + n],
                                                       ALU.mult, ALU.add)
                        dve.drain()
                    dve.wait_ge(s_used, SET + l * UNITS + U_CONV + 3 * f + 3)
                    dve.wait_ge(s_out, SET + 32 * (l + 1))
                    V.tensor_tensor(in_two(yf[:, :]), in_two(yf[:, :]), two((3 * f + 2) % 4), ALU.mult).then_inc(s_cy, 1)
                    dve.drain()
                    V.tensor_copy(yT_hi[:, f, :], yf[:, :])
                    dve.drain()
                    V.tensor_tensor(yT_lo[:, f, :], yf[:, :], yT_hi[:, f, :].bitcast(F32), ALU.subtract).then_inc(s_y, 1)
                hold(dve)
                with dve.Fori(0, KC) as n:
                    for i in range(3):
                        g = (l * KC + n) * 3
                        dve.drain()
                        dve.wait_ge(s_sig, SET + g + i + 1)
                        dve.wait_ge(s_used, SET + l * UNITS + U_M + n * 6 + 2 * i + 2)
                        V.tensor_tensor(in_two((zacc if i == 0 else zt)[:, :]), in_two(sg[:, i, :]), two((2 * i + 1) % 4), ALU.mult).then_inc(s_zm, 1)
                        dve.drain()
                        if i:
                            V.tensor_tensor(zacc[:, :], zacc[:, :], zt[:, :], ALU.add)
                            dve.drain()
                    V.tensor_copy(zT_hi[:, ds(n, 1), :], zacc[:, :].rearrange("p (o c) -> p o c", o=1))
                    dve.drain()
                    V.tensor_tensor(zT_lo[:, ds(n, 1), :], zacc[:, :].rearrange("p (o c) -> p o c", o=1),
                                    zT_hi[:, ds(n, 1), :].bitcast(F32), ALU.subtract).then_inc(s_z, 1)
                for hf in range(2):
                    for t in range(TILES):
                        c0 = 512 * hf
                        dve.drain()
                        dve.wait_ge(s_xload, SET + 16 * (l + 1))
                        dve.wait_ge(s_gtl, SET + 64 * l + 32)
                        if t < PT:
                            dve.wait_ge(s_out_tile, SET + (l * 2 + hf) * PT + t + 1)
                        else:
                            dve.wait_ge(s_used, SET + l * UNITS + U_OUT + 4 * (hf + 1))
                        V.tensor_tensor(hbuf[:, t % 2, 0:512], ps[:, (5 * hf + t) % 8, :], gt[:, gl(t), c0:c0 + 512], ALU.mult)
                        dve.drain()
                        V.tensor_tensor(x[:, t, c0:c0 + 512], x[:, t, c0:c0 + 512], hbuf[:, t % 2, 0:512], ALU.add).then_inc(s_x1, 1)
                dve.wait_ge(s_sd, SET + l * 2 + 2)
                V.reciprocal(rstd, sd)
                dve.drain()
                dve.wait_ge(s_modl, SET + 16 * 8 * (l + 1))
                for t in range(TILES):
                    norm_tile(l, 1, t)
                dve.wait_ge(s_rl, SET + (l + 1) * TILES)
                V.tensor_tensor(lgt[:, :, :], ps[:, 7, 0:TILES * 32].rearrange("p (t n) -> p t n", n=32)[:, :, 0:NG + NE],
                                b_rt[:, :].rearrange("p (o n) -> p o n", o=1).broadcast_to([P, TILES, NG + NE]), ALU.add)
                dve.drain()
                lg = lgt[:, :, 0:NG]

                def bc(ap, n):
                    return ap.broadcast_to([P, TILES, n])

                def tt(o, i0, i1, op):
                    V.tensor_tensor(o, i0, i1, op)
                    dve.drain()

                def first_best(oh, scores_, mx, eq, pk, top):
                    V.tensor_reduce(mx[:, :, 0], scores_, AX.X, ALU.max)
                    dve.drain()
                    tt(eq[:, :, :], scores_, bc(mx[:, :, :], NG), ALU.is_equal)
                    tt(pk[:, :, :], eq[:, :, :], C("prio").rearrange("p (o n) -> p o n", o=1).broadcast_to([P, TILES, NG]), ALU.mult)
                    V.tensor_reduce(top[:, :, 0], pk[:, :, :], AX.X, ALU.max)
                    dve.drain()
                    tt(oh[:, :, :], pk[:, :, :], bc(top[:, :, :], NG), ALU.is_equal)

                first_best(goh, lg, gmax, geq, gpk, gsum)
                tt(gex[:, :, :], lg, bc(gmax[:, :, :], NG), ALU.subtract)
                le = lgt[:, :, NG:].rearrange("p t (g j) -> p t j g", g=NG)
                for t in range(TILES):
                    V.tensor_tensor(lsel4[:, t, :, :], le[:, t, :, :], goh[:, t, :].rearrange("p (o g) -> p o g", o=1).broadcast_to([P, EPG, NG]), ALU.mult)
                dve.drain()
                V.tensor_reduce(lsel[:, :, :], lsel4[:, :, :, :], AX.X, ALU.add)
                dve.drain()
                first_best(oh1, lsel[:, :, :], m1, geq, gpk, gsum)
                V.scalar_tensor_tensor(lsel2[:, :, :], oh1[:, :, :], -BIG, lsel[:, :, :], ALU.mult, ALU.add)
                dve.drain()
                first_best(oh2, lsel2[:, :, :], m2, geq, gpk, gsum)
                V.tensor_tensor(e21[:, :, :], m2[:, :, :], m1[:, :, :], ALU.subtract).then_inc(s_gx, 1)
                dve.wait_ge(s_gxe, SET + l + 1)
                V.tensor_reduce(gsum[:, :, 0], gex[:, :, :], AX.X, ALU.add)
                V.tensor_scalar(wt1[:, :, :], e21[:, :, :], 1.0, None, ALU.add)
                dve.drain()
                V.reciprocal(pgrp[:, :, :], gsum[:, :, :])
                V.reciprocal(wt2[:, :, :], wt1[:, :, :])
                dve.drain()
                tt(wt1[:, :, :], pgrp[:, :, :], wt2[:, :, :], ALU.mult)
                tt(wt2[:, :, :], wt1[:, :, :], e21[:, :, :], ALU.mult)
                for t in range(TILES):
                    for oh, Ek in ((oh1, E1), (oh2, E2)):
                        V.tensor_tensor(Ek[:, t, :].rearrange("p (g j) -> p g j", g=NG), goh[:, t, :].rearrange("p (g o) -> p g o", o=1).broadcast_to([P, NG, EPG]),
                                        oh[:, t, :].rearrange("p (o j) -> p o j", o=1).broadcast_to([P, NG, EPG]), ALU.mult)
                dve.drain()
                V.tensor_tensor(Em[:, :, :], E1[:, :, :], E2[:, :, :], ALU.add).then_inc(s_rM, 1)
                dve.wait_ge(s_rk, SET + l + 1)
                rk = ps[:, 6, 0:TILES * NE].rearrange("p (t e) -> p t e", e=NE)
                V.scalar_tensor_tensor(rkm[:, :, :], rk, 1.0, Em[:, :, :], ALU.add, ALU.mult)
                V.tensor_reduce(cmax[:, :], ps[:, 6, TILES * NE:TILES * NE + NE], AX.X, ALU.max)
                dve.drain()
                V.tensor_scalar(rkm[:, :, :], rkm[:, :, :], -1.0, None, ALU.add)
                V.tensor_tensor(cge[:, :], cmax[:, :].broadcast_to([P, 4]), C("thr"), ALU.is_gt)
                for k, Ek in enumerate((E1, E2)):
                    tt(rtmp[:, :, :], rk, Ek[:, :, :], ALU.mult)
                    V.tensor_reduce(rsel[:, k, :], rtmp[:, :, :], AX.X, ALU.add)
                    tt(rpos[:, :, :], C("base").rearrange("p (o e) -> p o e", o=1).broadcast_to([P, TILES, NE]), Ek[:, :, :], ALU.mult)
                    V.tensor_reduce(bsel[:, k, :], rpos[:, :, :], AX.X, ALU.add)
                    dve.drain()
                V.tensor_reduce(cr[:, :], cge[:, :], AX.X, ALU.add)
                V.tensor_copy(crf[:, 0:1], info[:, ds(l * 2, 1)])
                dve.drain()
                V.tensor_scalar(cr[:, :], cr[:, :], 1.0, None, ALU.add)
                dve.drain()
                V.tensor_copy(info[:, ds(l * 2 + 1, 1)], cr[:, :])
                V.tensor_tensor(crf[:, 1:2], crf[:, 0:1], cr[:, :], ALU.add)
                dve.drain()
                V.tensor_copy(info[:, ds(l * 2 + 2, 1)], crf[:, 1:2]).then_inc(s_info, 1)
                dve.wait_ge(s_info, SET + l + 1)
                done = rounds_before(dve, l)
                now = rounds_now(dve, l)
                hold(dve)
                with dve.Fori(0, now) as r:
                    for e in range(NE):
                        if e >= ONEHOTS:
                            dve.wait_ge(r_idx, SET + (done + r) * NE + e - ONEHOTS + 1)
                        V.tensor_tensor(onehot[:, e % ONEHOTS, :, :], iota.rearrange("p (o s) -> p o s", o=1).broadcast_to([P, TILES, SLOTS]),
                                        rkm[:, :, e:e + 1].broadcast_to([P, TILES, SLOTS]), ALU.is_equal).then_inc(r_oh, 1)
                    dve.wait_ge(r_idx, SET + (done + r + 1) * NE)
                    V.tensor_reduce(stok[:, :], ps[:, 5, 0:2 * NE].rearrange("p (e i) -> p e i", i=2), AX.X, ALU.add)
                    dve.drain()
                    V.tensor_copy(sidx[:, :], stok[:, :]).then_inc(r_slots, 1)
                    V.tensor_scalar(rkm[:, :, :], rkm[:, :, :], -float(SLOTS), None, ALU.add)
                    V.tensor_scalar(posf[:, :, :], rsel[:, :, :], 0.0, float(SLOTS - 1), ALU.max, ALU.min)
                    V.tensor_scalar(inr[:, :, :], rsel[:, :, :], 0.0, None, ALU.is_ge)
                    V.tensor_scalar(in2[:, :, :], rsel[:, :, :], float(SLOTS), None, ALU.is_lt)
                    dve.drain()
                    V.tensor_tensor(posf[:, :, :], posf[:, :, :], bsel[:, :, :], ALU.add)
                    V.tensor_tensor(inr[:, :, :], inr[:, :, :], in2[:, :, :], ALU.mult)
                    V.tensor_scalar(rsel[:, :, :], rsel[:, :, :], -float(SLOTS), None, ALU.add)
                    dve.drain()
                    V.tensor_copy(pos[:, :, :], posf[:, :, :])
                    V.tensor_tensor(wsel[:, 0, :], inr[:, 0, :], wt1[:, :, 0], ALU.mult)
                    V.tensor_tensor(wsel[:, 1, :], inr[:, 1, :], wt2[:, :, 0], ALU.mult).then_inc(r_slots, 1)
                    dve.drain()

                    g = done + r

                    def low(turn, j):
                        dve.wait_ge(r_hi, SET + g * ROUND_UNITS + turn * EXU + j + 1)
                        V.tensor_tensor(w_lo[:, j % SPL, :], raw_slot(j % EXU), w_hi[:, j % SPL, :].bitcast(F32), ALU.subtract).then_inc(r_lo, 1)

                    def turned_rows(turn, e):
                        dve.drain()
                        dve.wait_ge(r_Thi, SET + g * NE + turn * 2 + e + 1)
                        V.tensor_tensor(xT_lo[:, e % 2, :, :], pair(0, 1024).rearrange("p (k n) -> p k n", k=KC),
                                        xT_hi[:, e % 2, :, :].bitcast(F32), ALU.subtract).then_inc(r_Tlo, 1)

                    def hidden(turn, e):
                        dve.drain()
                        dve.wait_ge(r_hg, SET + g * NE + turn * 2 + e + 1)
                        V.tensor_tensor(hid[:, e % 2, :], hg[:, e % 2, :], ps[:, 4 + e % 2, FE:2 * FE], ALU.mult).then_inc(r_hid, 1)

                    def turned_hidden(turn, e):
                        src = ps[:, 6, 256 * (e % 2):256 * (e % 2) + 256].rearrange("p (k n) -> p k n", k=2)
                        dve.drain()
                        dve.wait_ge(r_HT, SET + g * NE + turn * 2 + e + 1)
                        V.tensor_copy(hidT_hi[:, e % 2, :, :], src)
                        dve.drain()
                        V.tensor_tensor(hidT_lo[:, e % 2, :, :], src, hidT_hi[:, e % 2, :, :].bitcast(F32), ALU.subtract).then_inc(r_hT, 1)

                    def prologue():
                        turned_rows(0, 0)
                        for q in range(4):
                            low(0, q)
                        hidden(0, 0)
                        turned_rows(0, 1)

                    def step(turn, i, first=False, last=False):
                        units = in_order(i)
                        for j, q in units[:2]:
                            low(turn, j)
                        turned_hidden(turn, i - 1)
                        for j, q in units[2:]:
                            low(turn, j)
                        hidden(turn, i)
                        if not last:
                            turned_rows(turn, i + 1)

                    def epilogue():
                        turned_hidden(NE // 2 - 1, 1)
                        for j in (10, 11):
                            low(NE // 2 - 1, j)

                    expert_steps(dve, prologue, step, epilogue)
                    dve.wait_ge(s_gtl, SET + 64 * (l + 1))
                    for t in range(TILES):
                        dve.wait_ge(s_yg[t % 2], 32 * (g * tiles_of(t) + t // 2 + 1))
                        dve.wait_ge(r_first, SET + g * TILES + t + 1)
                        V.scalar_tensor_tensor(yg[:, t % 2, 0, :], yg[:, t % 2, 1, :], wsel[:, 1, t:t + 1], yg[:, t % 2, 0, :], ALU.mult, ALU.add)
                        dve.drain()
                        V.tensor_tensor(yg[:, t % 2, 0, :], yg[:, t % 2, 0, :], gt[:, gl(t), :], ALU.mult)
                        dve.drain()
                        V.tensor_tensor(x[:, t, :], x[:, t, :], yg[:, t % 2, 0, :], ALU.add).then_inc(r_added, 1)
                    dve.drain()
                dve.drain()
                dve.sem_inc(s_done, 1)
            dve.wait_ge(s_fsd, SET + 1)
            V.reciprocal(rstd, sd)
            dve.drain()
            dve.wait_ge(s_fg, SET + 16)
            for t in range(TILES):
                V.scalar_tensor_tensor(x[:, t, :], x[:, t, :], rstd[:, t:t + 1], gt[:, 0, :], ALU.mult, ALU.mult).then_inc(s_fy, 1)

        @block.tensor
        def _(pe):
            pe.sem_inc(r_used, SPL)
            set_semaphores(pe, 4)
            mm = nc.tensor.matmul
            tr = nc.tensor.transpose

            def passes(ring):
                return ((w_hi[:, ring, :], 0), (w_hi[:, ring, :], 1), (w_lo[:, ring, :], 0))

            def feature(l, u, b, act_pair, value=None, k0=0, nk=KC, m=P, chunk0=0):
                ring = u % SPL
                pe.wait_ge(s_split, SET + (l * UNITS + u + 1 if value is None else value))
                for k in range(nk):
                    for i, (w, h) in enumerate(passes(ring)):
                        for c in range(2):
                            ins = mm(ps[0:m, 2 * b + c, 0:HT], w[:, k * m:(k + 1) * m], act_pair[h][:, chunk0 + k, HT * c:HT * (c + 1)],
                                     start=(k == 0 and i == 0), stop=(k == nk - 1 and i == 2))
                ins.then_inc(s_used, 1)

            def tokens(l, u, j, act_pair, bank, tile_done=None):
                ring = u % SPL
                pe.wait_ge(s_split, SET + l * UNITS + u + 1)
                for kk in range(2):
                    k = 2 * j + kk
                    cols = slice(512 * kk, 512 * kk + 512)
                    for t in range(TILES):
                        for i, (w, h) in enumerate(passes(ring)):
                            ins = mm(ps[:, bank(t), :], act_pair[h][:, k, t * P:(t + 1) * P], w[:, cols],
                                     start=(k == 0 and i == 0), stop=(k == KC - 1 and i == 2))
                        if tile_done is not None and k == KC - 1 and t < PT:
                            ins.then_inc(tile_done, 1)
                ins.then_inc(s_used, 1)

            hT, yT, zT = (hT_hi, hT_lo), (yT_hi, yT_lo), (zT_hi, zT_lo)
            pe.wait_ge(s_const, SET + 32)
            pe.wait_ge(s_cond, SET + 1)
            pe.wait_ge(s_init, SET + 1)
            with pe.Fori(0, DEPTH) as l:
                pe.wait_ge(s_info, SET + l)
                before = rounds_before(pe, l)
                pe.wait_ge(r_yo, SET + before * NE)
                for b in range(ADA_BLOCKS):
                    if b >= 2:
                        pe.wait_ge(s_mrow, SET + l * ADA_BLOCKS + b - 1)
                    for k in range(KC):
                        u = b * KC + k
                        slot = u % RAW
                        per_layer = raw_value(1, 0) - raw_value(0, 0) if slot == 0 else raw_value(1, slot) - raw_value(0, slot)
                        pe.wait_ge(s_raw[slot], SET + l * per_layer + 16 * (u // RAW + 1))
                        for c in range(2):
                            ins = mm(ps[0:2, 2 * (b % 2) + c, :], condT[:, k, :], raw[:, slot, 512 * c:512 * c + 512], start=(k == 0), stop=(k == KC - 1))
                        ins.then_inc(s_ada, 1)
                    for t in h_tiles(b):
                        pe.wait_ge(s_h, SET + l * 2 * TILES + t + 1)
                        if t >= 2:
                            pe.wait_ge(s_hT, SET + l * TILES + t - 1)
                        for k in range(KC):
                            ins = tr(psf[:, 1024 * (2 + t % 2) + k * P:1024 * (2 + t % 2) + (k + 1) * P], hbuf[:, t % 2, k * P:(k + 1) * P], ident)
                        ins.then_inc(s_hps, 1)
                pe.wait_ge(s_hT, SET + (l + 1) * TILES)
                pe.wait_ge(s_mrow, SET + (l + 1) * ADA_BLOCKS)
                for j in range(4):
                    tokens(l, U_V + j, j, hT, lambda t: t)
                pe.wait_ge(s_v, SET + (l + 1) * TILES)
                for j in range(4):
                    tokens(l, U_R + j, j, hT, lambda t: (5 + t) % 8)
                pe.wait_ge(s_split, SET + l * UNITS + U_TV + 1)
                for t in range(TILES):
                    for k in range(KC):
                        for i, (w, h) in enumerate(passes(U_TV % SPL)):
                            ins = mm(psf[:, 1024 + t * P:1024 + (t + 1) * P], hT[h][:, k, t * P:(t + 1) * P], w[:, k * P:(k + 1) * P],
                                     start=(k == 0 and i == 0), stop=(k == KC - 1 and i == 2))
                ins.then_inc(s_used, 1)
                pe.wait_ge(s_r, SET + (l + 1) * TILES)
                feature(l, U_LR, 2, hT, m=2 * RANK)
                feature(l, U_GLA, 3, hT)
                pe.wait_ge(s_tv, SET + l + 1)
                pe.wait_ge(s_lr, SET + l + 1)
                pe.wait_ge(s_lay2, SET + (l + 1) * 16 * 21)

                def gate_logits(h):
                    for d in range(2):
                        for c in range(2):
                            ins = mm(ps[:, 2 * d + c, 0:HT], w_gate[:, d, h * DK:(h + 1) * DK], lrT[:, HT * c:HT * (c + 1)], start=True, stop=True)
                        ins.then_inc(s_gz, 1)

                gate_logits(0)
                feature(l, U_GLA + 1, 2, hT)
                for h in range(HEADS):
                    hh = l * HEADS + h
                    pe.wait_ge(s_gqk, SET + hh * 2 + 2)
                    for d in range(2):
                        pe.wait_ge(s_gin, SET + hh * 2 + d + 1)
                        for t in range(TILES):
                            ins = tr(psf[:, 1024 * (2 + d) + t * P:1024 * (2 + d) + (t + 1) * P], sp_[:, d, t * P:(t + 1) * P], ident)
                        ins.then_inc(s_gkT, 1)
                        for t in range(TILES):
                            cs = slice(t * P, (t + 1) * P)
                            ins = mm(psf[:, 1024 * d + t * P:1024 * d + (t + 1) * P], En[:, d, cs], cb[:, d, cs], start=True, stop=True)
                        ins.then_inc(s_gatt, 1)
                    for d in range(2):
                        pe.wait_ge(s_gke, SET + hh * 2 + d + 1)
                        pe.wait_ge(s_gam, SET + hh * 2 + 2)
                        for q in range(2):
                            if q:
                                pe.wait_ge(s_gds, SET + hh * 4 + 2 * d + 1)
                                hold(pe)
                            o = CHUNK * q
                            for t in range(TILES):
                                n = 2 * t + q
                                ins = mm(psf[:, 1536 * d + n * DV:1536 * d + (n + 1) * DV], zb[o:o + CHUNK, d, t * P:(t + 1) * P],
                                         v_sb[o:o + CHUNK, t, h * DV:(h + 1) * DV], start=True, stop=True)
                            ins.then_inc(s_gds, 1)
                    pe.wait_ge(s_gst, SET + hh * 2 + 2)
                    hold(pe)
                    for t in range(TILES):
                        dst = ps[:, 6 + t // 4, (t % 4) * DV:(t % 4 + 1) * DV]
                        for d in range(2):
                            mm(dst, attm[:, d, t, :], v_sb[:, t, h * DV:(h + 1) * DV], start=(d == 0), stop=False, skip_group_check=True)
                        for d in range(2):
                            for n in (2 * t, 2 * t + 1):
                                o = CHUNK * (n % 2)
                                if n < SCH:
                                    i = n if d == 0 else SCH - 1 - n
                                else:
                                    i = SCH + 1 + (n - SCH if d == 0 else NCH - 1 - n)
                                ins = mm(dst[o:o + CHUNK, :], cb[:, d, n * CHUNK:(n + 1) * CHUNK], st[d][:, i, :], start=False, stop=(d == 1),
                                         skip_group_check=True)
                    ins.then_inc(s_go, 1)
                    if h + 1 < HEADS:
                        gate_logits(h + 1)
                    pe.wait_ge(s_gy, SET + hh + 1)
                    for t in range(TILES):
                        ins = tr(psf[:, 2048 + t * P:2048 + (t + 1) * P], yb[:, t, :], ident)
                    ins.then_inc(s_gyT, 1)
                    if h + 1 < HEADS:
                        feature(l, U_GLA + 2 * h + 2, 3, hT)
                        pe.wait_ge(s_y, SET + l * 12 + h + 1)
                        feature(l, U_GLA + 2 * h + 3, 2, hT)
                for kv in range(KVH):
                    j = l * (KVH + 4) + kv
                    pe.wait_ge(s_kraw, SET + j)
                    feature(l, U_K + kv, 0, hT)
                    if kv == 0:
                        pe.wait_ge(s_y, SET + l * 12 + HEADS)
                    pe.wait_ge(s_kraw, SET + j + 1)
                    pe.wait_ge(s_rope, SET + j)
                    mm(ps[:, 4, :], rot, qraw[:, 0:SAMPLE], start=True, stop=True).then_inc(s_rot, 1)
                    pe.wait_ge(s_kc, SET + l * KVH + kv)
                    tr(ps[:, 5, 0:P], ckd[:, kv, :, :], ident)
                    tr(ps[:, 5, P:2 * P], qraw[:, SAMPLE:], ident).then_inc(s_kt, 1)

                def q_chunk(c):
                    j = l * (KVH + 4) + KVH + c
                    pe.wait_ge(s_kraw, SET + j)
                    feature(l, U_Q + c, 0, hT)
                    pe.wait_ge(s_kraw, SET + j + 1)
                    pe.wait_ge(s_rope, SET + j)
                    mm(ps[:, 4, :], rot, qraw[:, 0:SAMPLE], start=True, stop=True).then_inc(s_rot, 1)

                def scores(hd):
                    c, o, kv, b_ = hd // 2, HD * (hd % 2), hd // 4, l * AH + hd
                    if hd == 0:
                        pe.wait_ge(s_kc, SET + (l + 1) * KVH)
                    if hd % 2 == 0:
                        pe.wait_ge(s_rope, SET + l * (KVH + 4) + KVH + c + 1)
                        pe.wait_ge(s_qc, SET + l * 4 + c + 1)
                    rows = slice(o, o + HD)
                    for b in range(TILES):
                        n = b_ * TILES + b
                        if b >= 2:
                            pe.wait_ge(s_sce, SET + n - 1)
                        else:
                            pe.wait_ge(s_sce, SET + b_ * TILES)
                        q = qT[rows, c % 2, b * P:(b + 1) * P]
                        dst = ps[:, 5 + b % 2, :]
                        own_ = P + b * P
                        if b == PT:
                            ins = mm(dst[:, P:2 * P], q, kT[rows, kv, own_:own_ + P], start=True, stop=True)
                        else:
                            if b == 0:
                                mm(dst[:, P:2 * P], q, kT[rows, kv, own_:own_ + P], start=True, stop=True)
                            else:
                                mm(dst[:, 0:2 * P], q, kT[rows, kv, own_ - P:own_ + P], start=True, stop=True)
                            ins = mm(dst[:, 2 * P:3 * P], q, kT[rows, kv, 0:P], start=True, stop=True)
                            if b < PT - 1:
                                ins = mm(dst[:, 3 * P:4 * P], q, kT[rows, kv, own_ + P:own_ + 2 * P], start=True, stop=True)
                        ins.then_inc(s_sc, 1)

                def values(hd):
                    c, o, kv, b_ = hd // 2, HD * (hd % 2), hd // 4, l * AH + hd
                    pe.wait_ge(s_p, SET + b_ + 1)

                    def turn(b):
                        n = b_ * TILES + b
                        lo_, hi_ = span(b)
                        pe.wait_ge(s_pte, SET + (n - 1 if b >= 2 else b_ * TILES))
                        for i in range(ktiles(b)):
                            ins = tr(ps[:, 2 + b % 2, i * P:(i + 1) * P], s_sb[:, hd % 2, b, lo_ + i * P:lo_ + (i + 1) * P], ident)
                        ins.then_inc(s_pt, 1)

                    def weigh(b):
                        pe.wait_ge(s_pte, SET + b_ * TILES + b + 1)
                        vals = [tv[:, PT, :]] if b == PT else (
                            ([tv[:, b - 1, :]] if b > 0 else []) + [tv[:, b, :], cv[:, :]] + ([tv[:, b + 1, :]] if b < PT - 1 else []))
                        dst = ps[o:o + HD, 1, 384:512] if b == PT else ps[o:o + HD, 7, b * P:(b + 1) * P]
                        for i, v in enumerate(vals):
                            ins = mm(dst, v[:, kv * HD:(kv + 1) * HD], pT[:, b % 2, i * P:(i + 1) * P], start=(i == 0), stop=(i == len(vals) - 1))
                        return ins

                    for b in range(TILES + 1):
                        if b < TILES:
                            turn(b)
                        if b >= 1:
                            ins = weigh(b - 1)
                    if hd % 2:
                        ins.then_inc(s_ao, 1)

                q_chunk(0)
                scores(0)
                for hd in range(0, AH, 2):
                    scores(hd + 1)
                    pe.wait_ge(s_y, SET + l * 12 + HEADS + hd // 2)
                    if hd < AH - 2:
                        q_chunk(hd // 2 + 1)
                    values(hd)
                    values(hd + 1)
                    if hd < AH - 2:
                        scores(hd + 2)
                pe.wait_ge(s_y, SET + l * 12 + HEADS + 4)
                for f in range(4):
                    for i in range(3):
                        n = 3 * f + i
                        if n >= 4:
                            fo, io = divmod(n - 4, 3)
                            pe.wait_ge((s_cc, s_cu, s_cy)[io], SET + l * 4 + fo + 1)
                        feature(l, U_CONV + n, n % 4, hT)
                pe.wait_ge(s_cy, SET + (l + 1) * 4)
                pe.wait_ge(s_y, SET + (l + 1) * 12)
                hold(pe)
                with pe.Fori(0, KC) as n:
                    for i in range(3):
                        v = l * UNITS + U_M + n * 6 + 2 * i + 1
                        g = (l * KC + n) * 3
                        if i == 2:
                            pe.wait_ge(s_sig, SET + g + 1)
                        else:
                            pe.wait_ge(s_sig, SET + g)
                        feature(l, U_M + 2 * i, (2 * i) % 4, hT, v)
                        if i == 2:
                            pe.wait_ge(s_zm, SET + g + 1)
                        else:
                            pe.wait_ge(s_zm, SET + g)
                        feature(l, U_M + 2 * i + 1, (2 * i + 1) % 4, yT, v + 1, nk=4, chunk0=4 * i)
                pe.wait_ge(s_z, SET + (l + 1) * KC)
                for hf in range(2):
                    if hf == 1:
                        pe.wait_ge(s_x1, SET + l * 2 * TILES + 2)
                    for j in range(4):
                        tokens(l, U_OUT + 4 * hf + j, j, zT, lambda t: (5 * hf + t) % 8, s_out_tile)
                pe.wait_ge(s_x1, SET + (l + 1) * 2 * TILES)
                for t in range(TILES + 1):
                    if t < TILES:
                        pe.wait_ge(s_h, SET + (l * 2 + 1) * TILES + t + 1)
                        if t >= 2:
                            pe.wait_ge(s_h2T, SET + l * TILES + t - 1)
                        for k in range(KC):
                            ins = tr(psf[:, 1024 * (t % 2) + k * P:1024 * (t % 2) + (k + 1) * P], hbuf[:, t % 2, k * P:(k + 1) * P], ident)
                        ins.then_inc(s_hps, 1)
                    if t >= 1:
                        pe.wait_ge(s_h2T, SET + l * TILES + t)
                        for k in range(KC):
                            ins = mm(ps[:, 7, (t - 1) * 32:(t - 1) * 32 + NG + NE], h2T[:, (t - 1) % 2, k, :], w_rt[:, k, :], start=(k == 0), stop=(k == KC - 1))
                        ins.then_inc(s_rl, 1)
                pe.wait_ge(s_rM, SET + l + 1)
                for t in range(TILES + 1):
                    for i in range(min(t + 1, TILES)):
                        ins = mm(ps[:, 6, t * NE:(t + 1) * NE], tri_b[:, 0:P] if i == t else tri_b[:, P:], Em[:, i, :], start=(i == 0), stop=(i == min(t, TILES - 1)))
                ins.then_inc(s_rk, 1)
                pe.wait_ge(s_info, SET + l + 1)
                done = rounds_before(pe, l)
                now = rounds_now(pe, l)
                hold(pe)
                with pe.Fori(0, now) as r:
                    pe.wait_ge(r_hid, SET + (done + r) * NE)
                    for e in range(NE):
                        pe.wait_ge(r_oh, SET + (done + r) * NE + e + 1)
                        for t in range(TILES):
                            ins = mm(ps[:, 5, 2 * e:2 * e + 2], onehot[:, e % ONEHOTS, t, :], tok_b[:, t, :], start=(t == 0), stop=(t == TILES - 1))
                        ins.then_inc(r_idx, 1)
                    pe.wait_ge(r_slots, SET + (done + r) * 2 + 1)

                    g = done + r

                    def unit(turn, j):
                        pe.wait_ge(r_lo, SET + EXU + g * ROUND_UNITS + turn * EXU + j + 1)
                        return passes(j % SPL)

                    def turn_rows(turn, e):
                        pe.wait_ge(r_xg[e % 2], (g * (NE // 2) + turn + e // 2 + 1) * 16)
                        pe.wait_ge(r_Tlo, SET + g * NE + turn * 2 + e)
                        for k in range(KC):
                            ins = tr(psf[:, k * P:(k + 1) * P], xg[:, e % 2, k * P:(k + 1) * P], ident)
                        ins.then_inc(r_T, 1)

                    def gate_up(turn, e, first):
                        pe.wait_ge(r_Tlo, SET + g * NE + turn * 2 + e + 1)
                        for j in range(4):
                            for kk, ws in enumerate((unit(turn, first + j), passes((first + j) % SPL))):
                                k = 2 * j + kk
                                for q, (w, h) in enumerate(ws):
                                    ins = mm(ps[:, 4 + e % 2, :], (xT_hi, xT_lo)[h][:, e % 2, k, :], w[:, 512 * kk:512 * kk + 512],
                                             start=(k == 0 and q == 0), stop=(k == KC - 1 and q == 2))
                            ins.then_inc(r_used, 1)

                    def turn_hidden(turn, e):
                        pe.wait_ge(r_hid, SET + g * NE + turn * 2 + e + 1)
                        for k in range(2):
                            ins = tr(ps[:, 6, 256 * (e % 2) + k * P:256 * (e % 2) + (k + 1) * P], hid[:, e % 2, k * P:(k + 1) * P], ident)
                        ins.then_inc(r_HT, 1)

                    def down(turn, e, first):
                        pe.wait_ge(r_hT, SET + g * NE + turn * 2 + e + 1)
                        pe.wait_ge(r_yo, SET + g * NE + turn * 2 + e)
                        for k in range(2):
                            for q, (w, h) in enumerate(unit(turn, first + k)):
                                for c in range(2):
                                    ins = mm(ps[:, 2 + c, :], (hidT_hi, hidT_lo)[h][:, e % 2, k, :], w[:, 512 * c:512 * c + 512],
                                             start=(k == 0 and q == 0), stop=(k == 1 and q == 2))
                            ins.then_inc(r_used, 1)

                    def prologue():
                        turn_rows(0, 0)
                        gate_up(0, 0, 0)
                        turn_rows(0, 1)
                        turn_hidden(0, 0)

                    def step(turn, i, first=False, last=False):
                        u = in_order(i)[0][0]
                        gate_up(turn, i, u)
                        if not last:
                            turn_rows(turn, i + 1)
                        down(turn, i - 1, u + 4)
                        turn_hidden(turn, i)

                    def epilogue():
                        down(NE // 2 - 1, 1, 10)

                    expert_steps(pe, prologue, step, epilogue)


_INS = ["x_prompt", "x_sample", "state_gla", "cache_k", "cache_v", "c", "c_ctx", "w_ada", "b_ada", "norm1_g", "norm2_g",
        "w_in", "conv_w", "gla_w_gate", "gla_b_gate", "gla_norm_g", "attn_sink", "w_branch", "w_out", "w_route_group",
        "b_route_group", "w_route_expert", "b_route_expert", "w_exp_gate", "w_exp_up", "w_exp_down", "final_norm_g"]
_OUTS = [("y_prompt", (1, PROMPT, D)), ("y_sample", (1, SAMPLE, D)), ("new_state_gla", (1, DEPTH, 2, HEADS, DK, DV)),
         ("new_cache_k", (1, DEPTH, PROMPT, KVH, HD)), ("new_cache_v", (1, DEPTH, PROMPT, KVH, HD))]


def kernel(**inputs):
    import concourse.bacc as bacc
    from concourse.bass_utils import run_bass_kernel_spmd

    nc = bacc.Bacc("TRN2", target_bir_lowering=False, num_devices=1)
    arrays = {n: np.ascontiguousarray(inputs[n]) for n in _INS}
    arrays["table"] = shape_constants()
    arrays["zeros"] = np.zeros((RANK, HEADS * DK), np.float32)
    ins = {n: nc.dram_tensor(f"in_{n}", v.shape, F32, kind="ExternalInput").ap() for n, v in arrays.items()}
    outs = [nc.dram_tensor(f"out_{n}", s, F32, kind="ExternalOutput").ap() for n, s in _OUTS]
    build(nc, ins, *outs)
    r = run_bass_kernel_spmd(nc, [{f"in_{n}": v for n, v in arrays.items()}], core_ids=[0])
    return tuple(r.results[0][f"out_{n}"] for n, _ in _OUTS)
```
